# Optimizing a Trainium2 kernel written in Bass

```python
import jax, jax.numpy as jnp
from jax import lax
import numpy as np

D_MODEL = 1024
BATCH = 1
SEQ = 512
DEPTH = 2

ROPE_THETA = 500000.0
ROPE_DIM = 16
Q_BLOCK = 128
NORM_EPS = 1e-6

DSA_HEADS = 8
DSA_HEAD_DIM = 64
DSA_NOPE_DIM = DSA_HEAD_DIM - ROPE_DIM
DSA_KV_RANK = 128
DSA_V_DIM = 64
IDX_HEADS = 4
IDX_DIM = 64
INDEX_TOPK = 256

SB_HEADS = 8
SB_HEAD_DIM = 64

ML_HEADS = 4
ML_HEAD_DIM = 128
ML_CHUNK = 64
ML_CONV = 4

N_BRANCHES = 3
BRANCH_WIDTH = 512
DSA_Q_WIDTH = DSA_HEADS * DSA_HEAD_DIM
SB_WIDTH = SB_HEADS * SB_HEAD_DIM
ML_WIDTH = ML_HEADS * ML_HEAD_DIM

IN_WIDTHS = (
    DSA_Q_WIDTH,
    DSA_KV_RANK,
    ROPE_DIM,
    IDX_HEADS * IDX_DIM,
    IDX_DIM,
    IDX_HEADS,
    BRANCH_WIDTH,
    SB_WIDTH,
    SB_WIDTH,
    SB_WIDTH,
    BRANCH_WIDTH,
    2 * ML_WIDTH,
    ML_WIDTH,
    ML_HEADS,
    ML_HEADS,
    ML_WIDTH,
    BRANCH_WIDTH,
    N_BRANCHES * D_MODEL,
)
W_IN_COLS = sum(IN_WIDTHS)


def rms_norm(x, w):
    x32 = x.astype(jnp.float32)
    y = x32 * lax.rsqrt(jnp.mean(x32 * x32, axis=-1, keepdims=True) + NORM_EPS)
    return (y * w.astype(jnp.float32)).astype(x.dtype)

def rope_tables(seq):
    pos = jnp.arange(seq, dtype=jnp.float32)
    inv = ROPE_THETA ** (-jnp.arange(0, ROPE_DIM, 2, dtype=jnp.float32) / ROPE_DIM)
    ang = pos[:, None] * inv[None, :]
    return jnp.cos(ang), jnp.sin(ang)

def partial_rope(x, cos, sin):
    half = ROPE_DIM // 2
    x1 = x[..., :half]
    x2 = x[..., half:ROPE_DIM]
    out = jnp.concatenate([x1 * cos - x2 * sin, x2 * cos + x1 * sin, x[..., ROPE_DIM:]], axis=-1)
    return out.astype(x.dtype)

def to_blocks(a):
    b, s = a.shape[:2]
    a = a.reshape((b, s // Q_BLOCK, Q_BLOCK) + a.shape[2:])
    return jnp.moveaxis(a, 1, 0)

def from_blocks(a):
    a = jnp.moveaxis(a, 0, 1)
    return a.reshape((a.shape[0], a.shape[1] * a.shape[2]) + a.shape[3:])

def dsa_attention(q, c_kv, k_rope, iq, ik, iw, w_uk, w_uv, kv_norm_w, cos, sin):
    bsz, seq = q.shape[:2]
    topk = min(INDEX_TOPK, seq // 4)
    c_kv = rms_norm(c_kv, kv_norm_w)
    q_rope = partial_rope(q[..., :ROPE_DIM], cos[:, None], sin[:, None])
    q_nope = q[..., ROPE_DIM:]
    k_rope = partial_rope(k_rope, cos, sin)
    iq = partial_rope(iq, cos[:, None], sin[:, None]).astype(jnp.float32)
    ik = partial_rope(ik, cos, sin).astype(jnp.float32)
    q_abs = jnp.einsum('bshn,rhn->bshr', q_nope, w_uk)
    q_cat = jnp.concatenate([q_abs, q_rope], axis=-1).astype(jnp.float32) * DSA_HEAD_DIM ** -0.5
    kv_cat = jnp.concatenate([c_kv, k_rope], axis=-1).astype(jnp.float32)
    key_pos = jnp.arange(seq)
    starts = jnp.arange(0, seq, Q_BLOCK)

    def block(args):
        qb, iqb, iwb, start = args
        q_pos = start + jnp.arange(Q_BLOCK)
        causal = key_pos[None, :] <= q_pos[:, None]
        score = jnp.einsum('bth,bths->bts', iwb,
                           jax.nn.relu(jnp.einsum('bthd,bsd->bths', iqb, ik)))
        score = jnp.where(causal[None], score, -jnp.inf)
        _, sel = lax.top_k(score, topk)
        kv_sel = jax.vmap(lambda kv, ix: kv[ix])(kv_cat, sel)
        valid = sel <= q_pos[None, :, None]
        logits = jnp.einsum('bthf,btkf->bthk', qb, kv_sel)
        logits = jnp.where(valid[:, :, None, :], logits, -jnp.inf)
        p = jax.nn.softmax(logits, axis=-1)
        return jnp.einsum('bthk,btkr->bthr', p, kv_sel[..., :DSA_KV_RANK])

    o_lat = from_blocks(lax.map(block, (to_blocks(q_cat), to_blocks(iq),
                                        to_blocks(iw.astype(jnp.float32)), starts)))
    o = jnp.einsum('bshr,rhv->bshv', o_lat, w_uv)
    return o.reshape(bsz, seq, DSA_HEADS * DSA_V_DIM)

def stick_breaking_attention(q, k, v):
    bsz, seq = q.shape[:2]
    qs = q.astype(jnp.float32) * SB_HEAD_DIM ** -0.5
    k32 = k.astype(jnp.float32)
    v32 = v.astype(jnp.float32)
    key_pos = jnp.arange(seq)
    starts = jnp.arange(0, seq, Q_BLOCK)

    def block(args):
        qb, start = args
        q_pos = start + jnp.arange(Q_BLOCK)
        strict = key_pos[None, :] < q_pos[:, None]
        z = jnp.einsum('bthd,bshd->bhts', qb, k32)
        log_stay = jnp.where(strict, jax.nn.log_sigmoid(-z), 0.0)
        log_after = lax.cumsum(log_stay, axis=3, reverse=True) - log_stay
        a = jnp.where(strict, jnp.exp(jax.nn.log_sigmoid(z) + log_after), 0.0)
        return jnp.einsum('bhts,bshd->bthd', a, v32)

    o = from_blocks(lax.map(block, (to_blocks(qs), starts)))
    return o.reshape(bsz, seq, SB_HEADS * SB_HEAD_DIM)

def causal_depthwise_conv(u, w):
    return lax.conv_general_dilated(u, w[:, None, :].astype(u.dtype), window_strides=(1,),
                                    padding=[(ML_CONV - 1, 0)],
                                    dimension_numbers=('NWC', 'WIO', 'NWC'),
                                    feature_group_count=u.shape[-1])

def mlstm_chunkwise(q, k, v, i_pre, f_pre):
    bsz, seq = q.shape[:2]
    nc = seq // ML_CHUNK

    def chunked(a):
        a = jnp.moveaxis(a.astype(jnp.float32), 2, 1)
        a = a.reshape((bsz, ML_HEADS, nc, ML_CHUNK) + a.shape[3:])
        return jnp.moveaxis(a, 2, 0)

    qc = chunked(q)
    kc = chunked(k.astype(jnp.float32) * ML_HEAD_DIM ** -0.5)
    vc = chunked(v)
    ic = chunked(i_pre)
    lfc = chunked(jax.nn.log_sigmoid(f_pre.astype(jnp.float32)))
    tril = jnp.tril(jnp.ones((ML_CHUNK, ML_CHUNK), dtype=bool))

    def step(carry, inp):
        c_mem, n_mem, m_prev = carry
        qb, kb, vb, ib, lfb = inp
        b = jnp.cumsum(lfb, axis=-1)
        log_d = jnp.where(tril, b[..., :, None] - b[..., None, :] + ib[..., None, :], -jnp.inf)
        log_inter = b + m_prev[..., None]
        m_row = jnp.maximum(jnp.max(log_d, axis=-1), log_inter)
        w_intra = jnp.exp(log_d - m_row[..., None])
        w_inter = jnp.exp(log_inter - m_row)
        s = jnp.einsum('bhtd,bhsd->bhts', qb, kb) * w_intra
        num = (jnp.einsum('bhts,bhse->bhte', s, vb)
               + w_inter[..., None] * jnp.einsum('bhtd,bhde->bhte', qb, c_mem))
        den = jnp.sum(s, axis=-1) + w_inter * jnp.einsum('bhtd,bhd->bht', qb, n_mem)
        h = num / jnp.maximum(jnp.abs(den), jnp.exp(-m_row))[..., None]
        b_last = b[..., -1]
        log_w = b_last[..., None] - b + ib
        m_new = jnp.maximum(b_last + m_prev, jnp.max(log_w, axis=-1))
        w_upd = jnp.exp(log_w - m_new[..., None])
        decay = jnp.exp(b_last + m_prev - m_new)
        c_mem = decay[..., None, None] * c_mem + jnp.einsum('bhs,bhsd,bhse->bhde', w_upd, kb, vb)
        n_mem = decay[..., None] * n_mem + jnp.einsum('bhs,bhsd->bhd', w_upd, kb)
        return (c_mem, n_mem, m_new), h

    init = (jnp.zeros((bsz, ML_HEADS, ML_HEAD_DIM, ML_HEAD_DIM), jnp.float32),
            jnp.zeros((bsz, ML_HEADS, ML_HEAD_DIM), jnp.float32),
            jnp.zeros((bsz, ML_HEADS), jnp.float32))
    _, h = lax.scan(step, init, (qc, kc, vc, ic, lfc))
    h = jnp.moveaxis(h, 0, 2).reshape(bsz, ML_HEADS, seq, ML_HEAD_DIM)
    return jnp.moveaxis(h, 1, 2)

def head_layer_norm(h, w):
    h = h.astype(jnp.float32)
    mu = jnp.mean(h, axis=-1, keepdims=True)
    var = jnp.mean(jnp.square(h - mu), axis=-1, keepdims=True)
    y = (h - mu) * lax.rsqrt(var + NORM_EPS)
    return y.reshape(h.shape[0], h.shape[1], -1) * w.astype(jnp.float32)

def hybrid_layer(x, w_in, w_uk, w_uv, kv_norm_w, conv_w, i_bias, f_bias, ml_norm_w,
                 w_branch, w_out, norm_w, cos, sin):
    bsz, seq, _ = x.shape
    h = rms_norm(x, norm_w)
    p = h @ w_in
    splits = [int(c) for c in np.cumsum(IN_WIDTHS)[:-1]]
    (dsa_q, dsa_ckv, dsa_krope, idx_q, idx_k, idx_w, dsa_z,
     sb_q, sb_k, sb_v, sb_z,
     ml_qk, ml_v, ml_i, ml_f, ml_o, ml_z, merge) = jnp.split(p, splits, axis=-1)

    def heads(a, n):
        return a.reshape(bsz, seq, n, -1)

    y_a = dsa_attention(heads(dsa_q, DSA_HEADS), dsa_ckv, dsa_krope, heads(idx_q, IDX_HEADS),
                        idx_k, idx_w, w_uk, w_uv, kv_norm_w, cos, sin)
    y_b = stick_breaking_attention(heads(sb_q, SB_HEADS), heads(sb_k, SB_HEADS), heads(sb_v, SB_HEADS))
    ml_q, ml_k = jnp.split(jax.nn.silu(causal_depthwise_conv(ml_qk, conv_w)), 2, axis=-1)
    h_c = mlstm_chunkwise(heads(ml_q, ML_HEADS), heads(ml_k, ML_HEADS), heads(ml_v, ML_HEADS),
                          ml_i + i_bias, ml_f + f_bias)
    y_c = head_layer_norm(h_c, ml_norm_w) * jax.nn.sigmoid(ml_o.astype(jnp.float32))

    branches = jnp.stack([y_a * jax.nn.silu(dsa_z), y_b * jax.nn.silu(sb_z),
                          y_c * jax.nn.silu(ml_z)], axis=2)
    proj = jnp.einsum('bsgc,gcd->bsgd', branches, w_branch)
    gates = jax.nn.sigmoid(merge.reshape(bsz, seq, N_BRANCHES, D_MODEL).astype(jnp.float32))
    mixed = jnp.sum(gates * proj, axis=2)
    return x + (mixed @ w_out).astype(x.dtype)

def first_inputs(seed: int = 0) -> dict:
    key = jax.random.key(seed)
    ks = jax.random.split(key, 13)

    def nrm(k, shape, fan_in):
        return jax.random.normal(k, shape, jnp.float32) * fan_in ** -0.5

    x = jax.random.normal(ks[0], (BATCH, SEQ, D_MODEL), jnp.float32)
    w_in = nrm(ks[1], (DEPTH, D_MODEL, W_IN_COLS), D_MODEL)
    w_dsa_uk = nrm(ks[2], (DEPTH, DSA_KV_RANK, DSA_HEADS, DSA_NOPE_DIM), DSA_KV_RANK)
    w_dsa_uv = nrm(ks[3], (DEPTH, DSA_KV_RANK, DSA_HEADS, DSA_V_DIM), DSA_KV_RANK)
    dsa_kv_norm_w = 1.0 + 0.02 * jax.random.normal(ks[4], (DEPTH, DSA_KV_RANK), jnp.float32)
    ml_conv_w = nrm(ks[5], (DEPTH, ML_CONV, 2 * ML_WIDTH), ML_CONV)
    ml_i_bias = 0.1 * jax.random.normal(ks[6], (DEPTH, ML_HEADS), jnp.float32)
    ml_f_bias = (jnp.linspace(3.0, 6.0, ML_HEADS, dtype=jnp.float32)[None, :]
                 + 0.1 * jax.random.normal(ks[7], (DEPTH, ML_HEADS), jnp.float32))
    ml_norm_w = 1.0 + 0.02 * jax.random.normal(ks[8], (DEPTH, ML_WIDTH), jnp.float32)
    w_branch = nrm(ks[9], (DEPTH, N_BRANCHES, BRANCH_WIDTH, D_MODEL), BRANCH_WIDTH)
    w_out = nrm(ks[10], (DEPTH, D_MODEL, D_MODEL), D_MODEL)
    norm_w = 1.0 + 0.02 * jax.random.normal(ks[11], (DEPTH, D_MODEL), jnp.float32)
    final_norm_w = 1.0 + 0.02 * jax.random.normal(ks[12], (D_MODEL,), jnp.float32)
    return {'x': x, 'w_in': w_in, 'w_dsa_uk': w_dsa_uk, 'w_dsa_uv': w_dsa_uv,
            'dsa_kv_norm_w': dsa_kv_norm_w, 'ml_conv_w': ml_conv_w, 'ml_i_bias': ml_i_bias,
            'ml_f_bias': ml_f_bias, 'ml_norm_w': ml_norm_w, 'w_branch': w_branch,
            'w_out': w_out, 'norm_w': norm_w, 'final_norm_w': final_norm_w}

def first_block(x, w_in, w_dsa_uk, w_dsa_uv, dsa_kv_norm_w, ml_conv_w, ml_i_bias, ml_f_bias,
              ml_norm_w, w_branch, w_out, norm_w, final_norm_w):
    cos, sin = rope_tables(x.shape[1])
    for l in range(DEPTH):
        x = hybrid_layer(x, w_in[l], w_dsa_uk[l], w_dsa_uv[l], dsa_kv_norm_w[l], ml_conv_w[l],
                         ml_i_bias[l], ml_f_bias[l], ml_norm_w[l], w_branch[l], w_out[l],
                         norm_w[l], cos, sin)
    return rms_norm(x, final_norm_w)


DEPTH_2 = 1

HEAD_DIM = 64
ATTN_PATTERNS = ((128, 1), (512, 4), (2048, 16))
N_PATTERNS = 3
HEADS_PER_PATTERN = 4
N_ATTN_HEADS = N_PATTERNS * HEADS_PER_PATTERN
ATTN_WIDTH = N_ATTN_HEADS * HEAD_DIM
ATTN_OUT_WIDTH = HEADS_PER_PATTERN * HEAD_DIM
N_KEYS = ATTN_PATTERNS[0][0] // ATTN_PATTERNS[0][1] + 1
REL_BUCKETS = 32
REL_MAX_DIST = 2048
SSM_GROUP = 16
SSM_STATE = 64
SSM_WIDTH = 512
SSM_GROUPS = SSM_WIDTH // SSM_GROUP
DT_MIN = 1e-3
DT_MAX = 1e-1
MEM_LEN = 256
XATTN_HEADS = 4
XATTN_HEAD_DIM = 128
XATTN_WIDTH = XATTN_HEADS * XATTN_HEAD_DIM
IN_WIDTH = SSM_WIDTH + 3 * ATTN_WIDTH + XATTN_WIDTH + N_BRANCHES * D_MODEL
D_FF = 2816
EPS = 1e-6


def rmsnorm(x, g):
    xf = x.astype(jnp.float32)
    y = xf * lax.rsqrt(jnp.mean(xf * xf, axis=-1, keepdims=True) + EPS)
    return (y * g.astype(jnp.float32)).astype(x.dtype)

def swiglu_ffn(x, w_in, w_down):
    a, b = jnp.split(x @ w_in, 2, axis=-1)
    return (jax.nn.silu(a) * b) @ w_down

def t5_causal_buckets(dist):
    dist = np.asarray(dist, np.int32)
    max_exact = REL_BUCKETS // 2
    safe = np.maximum(dist, 1).astype(np.float32)
    large = max_exact + (np.log(safe / max_exact) / np.log(REL_MAX_DIST / max_exact)
                         * (REL_BUCKETS - max_exact)).astype(np.int32)
    large = np.minimum(large, REL_BUCKETS - 1)
    return np.where(dist < max_exact, dist, large).astype(np.int32)

def pattern_offsets():
    return np.stack([np.arange(N_KEYS, dtype=np.int32) * d for (_, d) in ATTN_PATTERNS])

def s5_scan(u, a_re, a_im, log_dt, b_re, b_im, c_re, c_im, d_skip):
    bsz, seqlen, _ = u.shape
    f32 = jnp.float32
    uf = u.astype(f32).reshape(bsz, seqlen, SSM_GROUPS, SSM_GROUP)
    a_re = a_re.astype(f32); a_im = a_im.astype(f32)
    dt = jnp.exp(log_dt.astype(f32))[:, None]
    mag = jnp.exp(a_re * dt)
    ang = a_im * dt
    abar_re = mag * jnp.cos(ang)
    abar_im = mag * jnp.sin(ang)
    nr = abar_re - 1.0
    ni = abar_im
    den = a_re * a_re + a_im * a_im
    coef_re = (nr * a_re + ni * a_im) / den
    coef_im = (ni * a_re - nr * a_im) / den
    b_re = b_re.astype(f32); b_im = b_im.astype(f32)
    bbar_re = coef_re[..., None] * b_re - coef_im[..., None] * b_im
    bbar_im = coef_re[..., None] * b_im + coef_im[..., None] * b_re
    bu_re = jnp.einsum('blgh,gph->blgp', uf, bbar_re)
    bu_im = jnp.einsum('blgh,gph->blgp', uf, bbar_im)
    a_seq_re = jnp.broadcast_to(abar_re[None, None], (1, seqlen, SSM_GROUPS, SSM_STATE))
    a_seq_im = jnp.broadcast_to(abar_im[None, None], (1, seqlen, SSM_GROUPS, SSM_STATE))

    def combine(e1, e2):
        a1r, a1i, b1r, b1i = e1
        a2r, a2i, b2r, b2i = e2
        return (a2r * a1r - a2i * a1i,
                a2r * a1i + a2i * a1r,
                a2r * b1r - a2i * b1i + b2r,
                a2r * b1i + a2i * b1r + b2i)

    _, _, x_re, x_im = lax.associative_scan(combine, (a_seq_re, a_seq_im, bu_re, bu_im), axis=1)
    y = (jnp.einsum('blgp,ghp->blgh', x_re, c_re.astype(f32))
         - jnp.einsum('blgp,ghp->blgh', x_im, c_im.astype(f32))
         + uf * d_skip.astype(f32))
    return y.reshape(bsz, seqlen, SSM_WIDTH).astype(u.dtype)

def dilated_mixture_attention(q, k, v, rel_table):
    bsz, seqlen = q.shape[0], q.shape[1]
    f32 = jnp.float32
    offsets = pattern_offsets()
    buckets = t5_causal_buckets(offsets)
    table = rel_table.astype(f32).reshape(REL_BUCKETS, N_PATTERNS, HEADS_PER_PATTERN)
    grp = np.arange(N_PATTERNS)[:, None]
    bias = jnp.transpose(table[buckets, grp], (0, 2, 1))
    grp3 = np.arange(N_PATTERNS)[:, None, None]
    scale = HEAD_DIM ** -0.5

    def block(start):
        qb = lax.dynamic_slice_in_dim(q, start, Q_BLOCK, axis=1).astype(f32)
        pos = start + jnp.arange(Q_BLOCK, dtype=jnp.int32)
        idx = pos[None, :, None] - offsets[:, None, :]
        valid = idx >= 0
        idx = jnp.maximum(idx, 0)
        kb = k[:, idx, grp3].astype(f32)
        vb = v[:, idx, grp3].astype(f32)
        logits = jnp.einsum('bqghd,bgqkhd->bghqk', qb, kb) * scale + bias[None, :, :, None, :]
        logits = jnp.where(valid[None, :, None], logits, -jnp.inf)
        lse = jax.nn.logsumexp(logits, axis=-1)
        probs = jnp.exp(logits - lse[..., None])
        out = jnp.einsum('bghqk,bgqkhd->bqghd', probs, vb)
        mix = jax.nn.softmax(lse, axis=1)
        return jnp.einsum('bghq,bqghd->bqhd', mix, out).astype(q.dtype)

    starts = jnp.arange(seqlen // Q_BLOCK, dtype=jnp.int32) * Q_BLOCK
    out = lax.map(block, starts)
    return out.transpose(1, 0, 2, 3, 4).reshape(bsz, seqlen, ATTN_OUT_WIDTH)

def memory_cross_attention(xq, mem_n, w_kv):
    bsz, seqlen, _ = xq.shape
    f32 = jnp.float32
    mk, mv = jnp.split(mem_n @ w_kv, 2, axis=-1)
    mk = mk.reshape(bsz, -1, XATTN_HEADS, XATTN_HEAD_DIM).astype(f32)
    mv = mv.reshape(bsz, -1, XATTN_HEADS, XATTN_HEAD_DIM).astype(f32)
    qh = xq.reshape(bsz, seqlen, XATTN_HEADS, XATTN_HEAD_DIM).astype(f32)
    logits = jnp.einsum('bqhd,bkhd->bhqk', qh, mk) * (XATTN_HEAD_DIM ** -0.5)
    probs = jax.nn.softmax(logits, axis=-1)
    out = jnp.einsum('bhqk,bkhd->bqhd', probs, mv)
    return out.reshape(bsz, seqlen, XATTN_WIDTH).astype(xq.dtype)

def hybrid_layer_2(x, mem, rel_table, ffn1_norm, ffn1_w_in, ffn1_w_down, mix_norm, w_in,
                 ssm_a_re, ssm_a_im, ssm_log_dt, ssm_b_re, ssm_b_im, ssm_c_re, ssm_c_im, ssm_d, ssm_w_glu,
                 attn_w_up, mem_norm, xattn_w_kv, xattn_w_up, w_out, ffn2_norm, ffn2_w_in, ffn2_w_down):
    bsz, seqlen, _ = x.shape
    x = x + 0.5 * swiglu_ffn(rmsnorm(x, ffn1_norm), ffn1_w_in, ffn1_w_down)
    u = rmsnorm(x, mix_norm)
    proj = u @ w_in
    cuts = np.cumsum([SSM_WIDTH, ATTN_WIDTH, ATTN_WIDTH, ATTN_WIDTH, XATTN_WIDTH, D_MODEL, D_MODEL]).tolist()
    u_ssm, q, k, v, xq, g_ssm, g_attn, g_mem = jnp.split(proj, cuts, axis=-1)
    y_ssm = jax.nn.gelu(s5_scan(u_ssm, ssm_a_re, ssm_a_im, ssm_log_dt, ssm_b_re, ssm_b_im,
                                ssm_c_re, ssm_c_im, ssm_d))
    glu_a, glu_b = jnp.split(y_ssm @ ssm_w_glu, 2, axis=-1)
    br_ssm = glu_a * jax.nn.sigmoid(glu_b)
    hshape = (bsz, seqlen, N_PATTERNS, HEADS_PER_PATTERN, HEAD_DIM)
    br_attn = dilated_mixture_attention(q.reshape(hshape), k.reshape(hshape), v.reshape(hshape),
                                        rel_table) @ attn_w_up
    br_mem = memory_cross_attention(xq, rmsnorm(mem, mem_norm), xattn_w_kv) @ xattn_w_up
    merged = (jax.nn.sigmoid(g_ssm) * br_ssm + jax.nn.sigmoid(g_attn) * br_attn
              + jax.nn.sigmoid(g_mem) * br_mem)
    x = x + merged @ w_out
    x = x + 0.5 * swiglu_ffn(rmsnorm(x, ffn2_norm), ffn2_w_in, ffn2_w_down)
    return x

def second_inputs(seed: int = 0) -> dict:
    key = jax.random.key(seed)
    ks = jax.random.split(key, 32)
    f32 = jnp.float32

    def nrm(k, shape, fan_in):
        return jax.random.normal(k, shape, f32) * (fan_in ** -0.5)

    def gain(k, shape):
        return 1.0 + 0.02 * jax.random.normal(k, shape, f32)

    L = DEPTH_2
    a_im_init = jnp.pi * jnp.arange(SSM_STATE, dtype=f32)
    return {
        "x": jax.random.normal(ks[0], (BATCH, SEQ, D_MODEL), f32),
        "mem": jax.random.normal(ks[1], (BATCH, MEM_LEN, D_MODEL), f32),
        "ffn1_norm": gain(ks[2], (L, D_MODEL)),
        "ffn1_w_in": nrm(ks[3], (L, D_MODEL, 2 * D_FF), D_MODEL),
        "ffn1_w_down": nrm(ks[4], (L, D_FF, D_MODEL), D_FF),
        "mix_norm": gain(ks[5], (L, D_MODEL)),
        "w_in": nrm(ks[6], (L, D_MODEL, IN_WIDTH), D_MODEL),
        "ssm_a_re": -0.5 + 0.01 * jax.random.normal(ks[7], (L, SSM_GROUPS, SSM_STATE), f32),
        "ssm_a_im": a_im_init + 0.01 * jax.random.normal(ks[8], (L, SSM_GROUPS, SSM_STATE), f32),
        "ssm_log_dt": jax.random.uniform(ks[9], (L, SSM_GROUPS), f32,
                                         float(np.log(DT_MIN)), float(np.log(DT_MAX))),
        "ssm_b_re": nrm(ks[10], (L, SSM_GROUPS, SSM_STATE, SSM_GROUP), 2 * SSM_GROUP),
        "ssm_b_im": nrm(ks[11], (L, SSM_GROUPS, SSM_STATE, SSM_GROUP), 2 * SSM_GROUP),
        "ssm_c_re": nrm(ks[12], (L, SSM_GROUPS, SSM_GROUP, SSM_STATE), SSM_STATE),
        "ssm_c_im": nrm(ks[13], (L, SSM_GROUPS, SSM_GROUP, SSM_STATE), SSM_STATE),
        "ssm_d": jax.random.normal(ks[14], (L, SSM_GROUPS, SSM_GROUP), f32),
        "ssm_w_glu": nrm(ks[15], (L, SSM_WIDTH, 2 * D_MODEL), SSM_WIDTH),
        "rel_table": 0.5 * jax.random.normal(ks[16], (REL_BUCKETS, N_ATTN_HEADS), f32),
        "attn_w_up": nrm(ks[17], (L, ATTN_OUT_WIDTH, D_MODEL), ATTN_OUT_WIDTH),
        "mem_norm": gain(ks[18], (L, D_MODEL)),
        "xattn_w_kv": nrm(ks[19], (L, D_MODEL, 2 * XATTN_WIDTH), D_MODEL),
        "xattn_w_up": nrm(ks[20], (L, XATTN_WIDTH, D_MODEL), XATTN_WIDTH),
        "w_out": nrm(ks[21], (L, D_MODEL, D_MODEL), D_MODEL),
        "ffn2_norm": gain(ks[22], (L, D_MODEL)),
        "ffn2_w_in": nrm(ks[23], (L, D_MODEL, 2 * D_FF), D_MODEL),
        "ffn2_w_down": nrm(ks[24], (L, D_FF, D_MODEL), D_FF),
        "final_norm": gain(ks[25], (D_MODEL,)),
    }

def second_block(x, mem, ffn1_norm, ffn1_w_in, ffn1_w_down, mix_norm, w_in,
              ssm_a_re, ssm_a_im, ssm_log_dt, ssm_b_re, ssm_b_im, ssm_c_re, ssm_c_im, ssm_d, ssm_w_glu,
              rel_table, attn_w_up, mem_norm, xattn_w_kv, xattn_w_up, w_out,
              ffn2_norm, ffn2_w_in, ffn2_w_down, final_norm):
    h = x
    for l in range(DEPTH_2):
        h = hybrid_layer_2(h, mem, rel_table, ffn1_norm[l], ffn1_w_in[l], ffn1_w_down[l], mix_norm[l], w_in[l],
                         ssm_a_re[l], ssm_a_im[l], ssm_log_dt[l], ssm_b_re[l], ssm_b_im[l],
                         ssm_c_re[l], ssm_c_im[l], ssm_d[l], ssm_w_glu[l],
                         attn_w_up[l], mem_norm[l], xattn_w_kv[l], xattn_w_up[l], w_out[l],
                         ffn2_norm[l], ffn2_w_in[l], ffn2_w_down[l])
    return rmsnorm(h, final_norm)


def setup_inputs(seed=0):
    out = dict(first_inputs(seed))
    for name, value in second_inputs(seed + 1).items():
        if name != "x":
            out[name + "_2"] = value
    return out


def reference(
    x, w_in, w_dsa_uk, w_dsa_uv, dsa_kv_norm_w, ml_conv_w, ml_i_bias, ml_f_bias, ml_norm_w,
    w_branch, w_out, norm_w, final_norm_w, mem_2, ffn1_norm_2, ffn1_w_in_2, ffn1_w_down_2,
    mix_norm_2, w_in_2, ssm_a_re_2, ssm_a_im_2, ssm_log_dt_2, ssm_b_re_2, ssm_b_im_2,
    ssm_c_re_2, ssm_c_im_2, ssm_d_2, ssm_w_glu_2, rel_table_2, attn_w_up_2, mem_norm_2,
    xattn_w_kv_2, xattn_w_up_2, w_out_2, ffn2_norm_2, ffn2_w_in_2, ffn2_w_down_2, final_norm_2,
):
    x = first_block(
        x, w_in, w_dsa_uk, w_dsa_uv, dsa_kv_norm_w, ml_conv_w, ml_i_bias, ml_f_bias, ml_norm_w,
        w_branch, w_out, norm_w, final_norm_w,
    )
    return second_block(
        x, mem_2, ffn1_norm_2, ffn1_w_in_2, ffn1_w_down_2, mix_norm_2, w_in_2, ssm_a_re_2,
        ssm_a_im_2, ssm_log_dt_2, ssm_b_re_2, ssm_b_im_2, ssm_c_re_2, ssm_c_im_2, ssm_d_2,
        ssm_w_glu_2, rel_table_2, attn_w_up_2, mem_norm_2, xattn_w_kv_2, xattn_w_up_2, w_out_2,
        ffn2_norm_2, ffn2_w_in_2, ffn2_w_down_2, final_norm_2,
    )


_drawn_inputs = setup_inputs


def setup_inputs(seed=0):
    import zlib

    import numpy as np

    out = dict(_drawn_inputs(seed))
    spreads = {}
    factors = {'dsa_kv_norm_w': 8.0,
     'ml_i_bias': 64.0,
     'ml_norm_w': 8.0,
     'norm_w': 3.214,
     'ffn1_norm_2': 6.685,
     'mix_norm_2': 8.0,
     'ssm_a_re_2': 64.0,
     'ssm_a_im_2': 29.832,
     'ssm_log_dt_2': 30.272,
     'ssm_b_re_2': 41.848,
     'ssm_b_im_2': 42.584,
     'ssm_c_re_2': 42.624,
     'ssm_c_im_2': 42.392,
     'mem_norm_2': 8.0,
     'ffn2_norm_2': 20.89,
     'final_norm_2': 7.954}
    for name, (base, spread) in spreads.items():
        noise = np.random.default_rng([zlib.crc32(name.encode()), seed]).standard_normal(out[name].shape)
        drawn = base * np.exp(spread * noise) if base else spread * noise
        out[name] = __import__('jax').numpy.asarray(drawn.astype(out[name].dtype))
    for name, factor in factors.items():
        out[name] = (out[name] * factor).astype(out[name].dtype)
    return out
```

```python
from contextlib import ExitStack

import numpy as np

import concourse.bass as bass
from concourse import mybir

F32 = mybir.dt.float32
ALU = mybir.AluOpType
ACT = mybir.ActivationFunctionType
AX = mybir.AxisListType

P = 128
T = 512
D = 1024
KD = D // P
TB = T // P
DEPTH = 2
EPS = 1e-6
HEADS, HD = 8, 64
ML_H, ML_D = 4, 128
IDX_H = 4
TOPK = 128
ROPE = 16
NEG = -1e30
DROPPED = -2e38
TAKEN = -3e38
ALIVE = -2.5e38

WQ = [P * (b + 1) for b in range(TB)]
OQ = [sum(WQ[:b]) for b in range(TB)]
WK = [T - P * s for s in range(TB)]
CAUSAL = sum(WQ)
KPLACE = [(0, 0), (1, 0), (2, 0), (1, 384)]
KOFF = [0, 512, 1024, 896]
BANKS = [(0, 512, 0), (1, 512, 512), (2, 256, 1024)]

SLOT = 4096
SLOTS = 3


class Signal:

    def __init__(self, sem):
        self.sem, self.count = sem, 0

    def on(self, ins, by=1):
        ins.then_inc(self.sem, by)
        self.count += by
        return self.count


def settle(eng, signal):
    eng.wait_ge(signal.sem, signal.count)


WIDE = ["idx", "q", "za", "zb", "sbq", "sbk", "sbv", "mlq", "mlk", "mlv", "mlo", "zc"]
CHUNKS = ["idx", "misc"] + WIDE[1:]
for _p in range(KD // 2):
    CHUNKS += [f"merge{2 * _p}", f"branch{_p}", f"merge{2 * _p + 1}"]
CHUNKS += ["out0", "out1"]


def layer_groups():
    g = [("ms", "a")]
    g += [(f"idx{i}", "a") for i in range(4)] + [("misc", "a"), ("q0", "a")]
    g += [(f"ridx{i}", "v") for i in range(3)]
    g += [(f"q{i}", "a") for i in range(1, 4)] + [("iwt", "v")]
    g += [(f"sc{b}{h}", "a") for b in range(1, TB) for h in range(IDX_H)]
    g += [(f"rq{i}", "v") for i in range(4)] + [("rkr", "v"), ("cms", "a")]
    g += [(f"za{i}", "a") for i in range(4)]
    g += [("at", "v")]
    g += [(f"kk{i}", "a") for i in range(4)] + [(f"vv{i}", "a") for i in range(TB)]
    g += [(f"{n}{i}", "a") for n in ("zb", "sbq", "sbk", "sbv") for i in range(4)]
    for h in range(HEADS):
        g += [(("mlq" if h < 4 else "mlk") + str(h % 4), "a"), (f"dsa{h}", "v")]
    for h in range(HEADS):
        if h % 2 == 0:
            g += [(f"mlv{h // 2}", "a")]
        if h >= 1:
            g += [(f"sb{h - 1}", "v")]
    g += [(f"sb{HEADS - 1}", "v")]
    g += [(f"mlo{i}", "a") for i in range(4)] + [(f"zc{i}", "a") for i in range(4)]
    for h in range(ML_H):
        g += [(f"mu{h}", "a"), (f"mm{h}", "a"), (f"den{h}", "a"), (f"num{h}", "v"), (f"mean{h}", "v"), (f"var{h}", "a")]
    for d in range(KD):
        for k in range(3):
            g += [(f"gate{d}{k}", "a"), (f"proj{d}{k}", "v")]
    g += [(f"out{d}", "v") for d in range(KD)]
    return g


class Groups:

    def __init__(self, names, banks, done, freed):
        self.names, self.banks, self.done, self.freed = names, banks, done, freed
        self.at = {n: i for i, (n, _) in enumerate(names)}
        assert len(self.at) == len(names)
        self.order, seen = {}, {"a": 0, "v": 0}
        for n, e in names:
            seen[e] += 1
            self.order[n] = seen[e]
        self.issued = 0
        self.emptied = {"a": 0, "v": 0}

    def open(self, pe, name):
        i = self.at[name]
        assert i == self.issued, (name, self.names[self.issued])
        n = len(self.banks)
        if i >= n:
            old, eng = self.names[i - n]
            pe.wait_ge(self.freed[eng].sem, self.order[old])
        return self.banks[i % n]

    def close(self, ins):
        self.issued += 1
        self.done.on(ins)

    def whole(self, eng, name):
        eng.wait_ge(self.done.sem, self.at[name] + 1)
        return self.banks[self.at[name] % len(self.banks)]

    def empty(self, ins, name):
        e = self.names[self.at[name]][1]
        self.emptied[e] += 1
        assert self.emptied[e] == self.order[name], name
        self.freed[e].on(ins)

    def moved(self, eng, name):
        eng.wait_ge(self.freed[self.names[self.at[name]][1]].sem, self.order[name])


CONST = {}
_c = 0
for _n, _w in (("ident", P), ("rot", P), ("dup", P), ("tri", P), ("negones", P), ("ones", P),
               ("cmask", P), ("cos", T), ("sin", T), ("sel", ML_H * P)):
    CONST[_n] = (_c, _c + _w)
    _c += _w
N_CONST = _c

VEC = {"norm": (0, 8), "kvnorm": (8, 9), "conv": (9, 41), "mlnorm": (41, 45), "ibias": (45, 46), "fbias": (46, 47)}
N_VEC = 47


def hybrid_layers(nc, stack, xT, A, consts, mark):
    def sb(name, shape, dt=F32):
        return stack.enter_context(nc.sbuf_tensor(name, shape, dt))

    every = []

    def sem(name):
        every.append(Signal(stack.enter_context(nc.semaphore(name))))
        return every[-1]

    def c(name):
        a, b = CONST[name]
        return consts[:, a:b]

    ident, rot, dup, tri, negones, ones, cmask, cosT, sinT, sel = (
        c(n) for n in ("ident", "rot", "dup", "tri", "negones", "ones", "cmask", "cos", "sin", "sel"))

    hT = sb("hT", [P, KD, T])
    ring = sb("ring", [P, SLOTS, SLOT])
    vecs = sb("vecs", [P, N_VEC])
    dq = sb("dq", [P, 4, T])
    dk = sb("dk", [P, 4, T])
    dv = sb("dv", [P, TB, T])
    sq_ = sb("sq_", [P, 4, T])
    sk = sb("sk", [P, 4, T])
    sv = sb("sv", [P, TB, T])
    za = sb("za", [P, 4, T])
    zb = sb("zb", [P, 4, T])
    idx = sb("idx", [P, 4, T])
    misc = sb("misc", [P, T])
    raw = sb("raw", [P, 8, T + 4])
    probs = sb("probs", [P, 2, CAUSAL])
    turned = sb("turned", [P, 2, CAUSAL])
    bias = sb("bias", [P, CAUSAL])
    rstd = sb("rstd", [P, T])
    small = sb("small", [P, 64])
    iwt = sb("iwt", [P, TB, IDX_H])
    acol = sb("acol", [P, TB, ML_H])
    top8 = sb("top8", [P, TB, 8])

    flat = raw[:].rearrange("p a b -> p (a b)")
    score = flat[:, 0:CAUSAL]
    relu = flat[:, CAUSAL:CAUSAL + 2 * T].rearrange("p (a b) -> p a b", a=2)
    wuk = flat[:, CAUSAL + 2 * T:CAUSAL + 3 * T]
    wuv = flat[:, CAUSAL + 3 * T:CAUSAL + 3 * T + T]
    mixed = flat[:, 0:KD * T].rearrange("p (a b) -> p a b", a=KD)
    mlo, zc = sq_, sk
    mq, mk, mv = dq, dk, dv
    ckv = idx[:, 3, :]
    gate = probs[:].rearrange("p a b -> p (a b)")[:, 0:3 * T].rearrange("p (a b) -> p a b", a=3)
    part = turned[:].rearrange("p a b -> p (a b)")[:, 0:2 * T].rearrange("p (a b) -> p a b", a=2)
    hml, dn, hsq, em = (flat[:, i * T:(i + 1) * T] for i in range(4))
    csq = dk[:, 0, :]
    tflat = turned[:].rearrange("p a b -> p (a b)")
    g_i, g_f, g_sum = (tflat[0:ML_H, i * T:(i + 1) * T] for i in range(3))
    g_mu, g_m, g_a = (idx[0:ML_H, i, :] for i in range(3))

    proj = [stack.enter_context(nc.psum_tensor(f"proj{i}", [P, T], F32)) for i in range(2)]
    att = [stack.enter_context(nc.psum_tensor(f"att{i}", [P, T], F32)) for i in range(6)]

    s_vec, s_lat = sem("s_vec"), sem("s_lat")
    s_w = [sem(f"s_w{i}") for i in range(SLOTS)]
    s_done, s_a, s_v = sem("s_done"), sem("s_act_moved"), sem("s_dve_moved")
    s_sq, s_h, s_ac, s_vc, s_pc = sem("s_square"), sem("s_h"), sem("s_act"), sem("s_dve"), sem("s_pool")
    s_ridx, s_rq, s_ckv, s_scused = sem("s_ridx"), sem("s_rq"), sem("s_ckv"), sem("s_scused")
    s_ln, s_gates, s_score, s_masked = sem("s_ln"), sem("s_gates"), sem("s_score"), sem("s_masked")
    s_csq, s_ir, s_rkr, s_bias = sem("s_csq"), sem("s_ir"), sem("s_rkr"), sem("s_bias")
    s_S, s_logit, s_exp, s_rinv, s_scaled, s_T, s_TA, s_TV = (sem(n) for n in (
        "s_S", "s_logit", "s_exp", "s_rinv", "s_scaled", "s_T", "s_TA", "s_TV"))
    s_Z, s_soft, s_sp, s_spm, s_tri, s_a_exp, s_am = (sem(n) for n in (
        "s_Z", "s_soft", "s_sp", "s_spm", "s_tri", "s_aexp", "s_am"))
    s_conv, s_silu, s_K, s_w8, s_w8m, s_ws, s_sq2, s_mlz, s_pad = (sem(n) for n in (
        "s_conv", "s_silu", "s_K", "s_w8", "s_w8m", "s_ws", "s_sq2", "s_mlz", "s_pad"))
    s_mix = sem("s_mix")

    G = Groups(layer_groups(), proj, s_done, {"a": s_a, "v": s_v})

    last_of = {"idx": "idx3", "misc": "misc", "q": "q3"}
    for n in ("za", "zb", "sbq", "sbk", "sbv", "mlq", "mlk", "mlv", "mlo", "zc"):
        last_of[n] = n + "3"
    for d in range(KD):
        last_of[f"merge{d}"] = f"gate{d}2"
    for p in range(KD // 2):
        last_of[f"branch{p}"] = f"proj{2 * p + 1}2"
    last_of["out0"], last_of["out1"] = "out3", "out7"

    def slot(chunk):
        return ring[:, CHUNKS.index(chunk) % SLOTS, :]

    def landed(eng, chunk):
        n = CHUNKS.index(chunk)
        eng.wait_ge(s_w[n % SLOTS].sem, 16 * (n // SLOTS + 1))

    with nc.Fori(0, DEPTH) as layer:
        with nc.Block() as block:

            @block.sync
            def _(sp):
                s_vec.on(sp.dma_start(vecs[:], A["vec"][layer]), 16)
                for n, chunk in enumerate(CHUNKS):
                    if n >= SLOTS:
                        sp.wait_ge(s_done.sem, G.at[last_of[CHUNKS[n - SLOTS]]] + 1)
                    dst = ring[:, n % SLOTS, :]
                    if chunk in WIDE:
                        src = A["wide"][layer, WIDE.index(chunk)]
                    elif chunk == "misc":
                        src, dst = A["misc"][layer], dst[:, 0:KD * P]
                    elif chunk.startswith("merge"):
                        src, dst = A["merge"][layer, int(chunk[5:])], dst[:, 0:KD * 3 * P]
                    elif chunk.startswith("branch"):
                        src, dst = A["branch"][layer, int(chunk[6:])], dst[:, 0:KD * 3 * P]
                    else:
                        src = A["out"][layer, int(chunk[3:])]
                    s_w[n % SLOTS].on(sp.dma_start(dst, src), 16)
                    if n == 1:
                        s_lat.on(sp.dma_start(wuk, A["wuk"][layer]), 16)
                        s_lat.on(sp.dma_start(wuv, A["wuv"][layer]), 16)

            @block.tensor
            def _(pe):
                def dense(name, chunk, width, col):
                    out = G.open(pe, name)
                    landed(pe, chunk)
                    w = slot(chunk)
                    for k in range(KD):
                        if name == "idx0":
                            pe.wait_ge(s_h.sem, k + 1)
                        mm = pe.matmul(out[:, :], w[:, k * width + col:k * width + col + P], hT[:, k, :],
                                       start=(k == 0), stop=(k == KD - 1))
                    G.close(mm)

                def dense_tokens(name, chunk, b):
                    out = G.open(pe, name)
                    landed(pe, chunk)
                    w = slot(chunk)
                    for k in range(KD):
                        mm = pe.matmul(out[:, :], hT[:, k, b * P:(b + 1) * P], w[:, k * T:(k + 1) * T],
                                       start=(k == 0), stop=(k == KD - 1))
                    G.close(mm)

                out = G.open(pe, "ms")
                for k in range(KD):
                    pe.wait_ge(s_sq.sem, k + 1)
                    mm = pe.matmul(out[:, :], ones, hT[:, k, :], start=(k == 0), stop=(k == KD - 1))
                G.close(mm)
                for i in range(4):
                    dense(f"idx{i}", "idx", T, i * P)
                dense("misc", "misc", P, 0)
                dense("q0", "q", T, 0)
                for i in range(3):
                    out = G.open(pe, f"ridx{i}")
                    G.moved(pe, f"idx{i}")
                    G.close(pe.matmul(out[:, :], rot, idx[:, i, :], start=True, stop=True))
                for i in range(1, 4):
                    dense(f"q{i}", "q", T, i * P)
                out = G.open(pe, "iwt")
                for b in range(TB):
                    tr = pe.transpose(out[:, b * IDX_H:(b + 1) * IDX_H], misc[96:96 + IDX_H, b * P:(b + 1) * P],
                                      ident[96:96 + IDX_H, 96:96 + IDX_H])
                G.close(tr)
                pe.wait_ge(s_ridx.sem, 3)
                for b in range(1, TB):
                    for h in range(IDX_H):
                        out = G.open(pe, f"sc{b}{h}")
                        r = slice(64 * (h % 2), 64 * (h % 2) + 64)
                        G.close(pe.matmul(out[:, 0:WQ[b]], idx[r, h // 2, b * P:(b + 1) * P], idx[r, 2, 0:WQ[b]],
                                          start=True, stop=True))
                for i in range(4):
                    out = G.open(pe, f"rq{i}")
                    G.moved(pe, f"q{i}")
                    G.close(pe.matmul(out[:, :], rot, dq[:, i, :], start=True, stop=True))
                out = G.open(pe, "rkr")
                G.close(pe.matmul(out[0:ROPE, :], rot[0:ROPE, 0:ROPE], misc[0:ROPE, :], start=True, stop=True))
                out = G.open(pe, "cms")
                pe.wait_ge(s_csq.sem, 1)
                G.close(pe.matmul(out[:, :], ones, csq, start=True, stop=True))
                for i in range(4):
                    dense(f"za{i}", "za", T, i * P)
                out = G.open(pe, "at")
                pe.wait_ge(s_gates.sem, 1)
                for b in range(TB):
                    tr = pe.transpose(out[:, b * ML_H:(b + 1) * ML_H], g_a[:, b * P:(b + 1) * P], ident[0:ML_H, 0:ML_H])
                G.close(tr)
                pe.wait_ge(s_ckv.sem, 1)
                pe.wait_ge(s_rkr.sem, 1)
                pe.wait_ge(s_lat.sem, 32)
                for i in range(4):
                    out = G.open(pe, f"kk{i}")
                    pe.matmul(out[:, :], wuk[:, i * P:(i + 1) * P], ckv, start=True, stop=False)
                    G.close(pe.matmul(out[:, :], dup[0:ROPE, :], misc[0:ROPE, :], start=False, stop=True))
                for b in range(TB):
                    out = G.open(pe, f"vv{b}")
                    G.close(pe.matmul(out[:, :], ckv[:, b * P:(b + 1) * P], wuv, start=True, stop=True))
                for n in ("zb", "sbq", "sbk"):
                    for i in range(4):
                        dense(f"{n}{i}", n, T, i * P)
                for b in range(TB):
                    dense_tokens(f"sbv{b}", "sbv", b)

                def dsa_scores(h):
                    if h >= 1:
                        pe.wait_ge(s_logit.sem, TB * h)
                    r = slice(64 * (h % 2), 64 * (h % 2) + 64)
                    for b in range(TB):
                        bank, col = KPLACE[TB - 1 - b]
                        mm = pe.matmul(att[bank][:, col:col + WQ[b]], dq[r, h // 2, b * P:(b + 1) * P],
                                       dk[r, h // 2, 0:WQ[b]], start=True, stop=True)
                    s_S.on(mm)

                pe.wait_ge(s_rq.sem, 4)
                G.moved(pe, "kk3")
                dsa_scores(0)
                for h in range(HEADS):
                    if h + 1 < HEADS:
                        dsa_scores(h + 1)
                    n = "mlq" if h < 4 else "mlk"
                    dense(f"{n}{h % 4}", n, T, (h % 4) * P)
                    pe.wait_ge(s_scaled.sem, TB * (h + 1))
                    if h >= 1:
                        pe.wait_ge(s_TA.sem, h)
                        pe.wait_ge(s_TV.sem, 2 * h)
                    for s in range(TB):
                        bank, col = KPLACE[s]
                        for b in range(s, TB):
                            tr = pe.transpose(att[3 + bank][:, col + (b - s) * P:col + (b - s + 1) * P],
                                              probs[:, h % 2, OQ[b] + s * P:OQ[b] + (s + 1) * P], ident)
                    s_T.on(tr)
                    out = G.open(pe, f"dsa{h}")
                    G.moved(pe, "vv3")
                    pe.wait_ge(s_TA.sem, h + 1)
                    pe.wait_ge(s_TV.sem, 2 * h + 2)
                    r = slice(64 * (h % 2), 64 * (h % 2) + 64)
                    for s in range(TB):
                        mm = pe.matmul(out[r, s * P:T], dv[:, s, h * HD:(h + 1) * HD],
                                       turned[:, h % 2, KOFF[s]:KOFF[s] + WK[s]], start=(s == 0), stop=(s == TB - 1),
                                       skip_group_check=True)
                    G.close(mm)

                def sb_scores(h):
                    if h == 0:
                        pe.wait_ge(s_logit.sem, TB * HEADS)
                    if h == 1:
                        pe.wait_ge(s_TA.sem, HEADS)
                        pe.wait_ge(s_TV.sem, 2 * HEADS)
                    if h >= 2:
                        pe.wait_ge(s_a_exp.sem, 3 * (h - 1))
                    r = slice(64 * (h % 2), 64 * (h % 2) + 64)
                    for s in range(TB):
                        bank, col = KPLACE[s]
                        mm = pe.matmul(att[3 * (h % 2) + bank][:, col:col + WK[s]], sk[r, h // 2, s * P:(s + 1) * P],
                                       sq_[r, h // 2, s * P:T], start=(s != 3), stop=False, skip_group_check=True)
                    s_Z.on(mm)

                def sb_values(h):
                    out = G.open(pe, f"sb{h}")
                    pe.wait_ge(s_am.sem, TB * (h + 1))
                    r = slice(64 * (h % 2), 64 * (h % 2) + 64)
                    for s in range(TB):
                        mm = pe.matmul(out[r, s * P:T], sv[:, s, h * HD:(h + 1) * HD],
                                       turned[:, h % 2, KOFF[s]:KOFF[s] + WK[s]], start=(s == 0), stop=(s == TB - 1),
                                       skip_group_check=True)
                    G.close(mm)

                G.moved(pe, "sbv3")
                sb_scores(0)
                for h in range(HEADS):
                    if h + 1 < HEADS:
                        sb_scores(h + 1)
                    if h % 2 == 0:
                        dense_tokens(f"mlv{h // 2}", "mlv", h // 2)
                    if h >= 1:
                        sb_values(h - 1)
                    pe.wait_ge(s_spm.sem, TB * (h + 1))
                    for s in range(TB):
                        bank, col = KPLACE[s]
                        for u in range(s, TB):
                            mm = pe.matmul(att[3 * (h % 2) + bank][:, col + (u - s) * P:col + WK[s]],
                                           tri if u == s else negones,
                                           probs[:, h % 2, KOFF[u]:KOFF[u] + WK[u]], start=False,
                                           stop=(u == TB - 1), skip_group_check=True)
                    s_tri.on(mm)
                sb_values(HEADS - 1)
                for n in ("mlo", "zc"):
                    for i in range(4):
                        dense(f"{n}{i}", n, T, i * P)

                G.moved(pe, "mlv3")
                for h in range(ML_H):
                    if h == 0:
                        pe.wait_ge(s_a_exp.sem, 3 * (HEADS - 1))
                        pe.wait_ge(s_silu.sem, 2)
                    else:
                        pe.wait_ge(s_ws.sem, 3 * h)
                    for s in range(TB):
                        bank, col = KPLACE[s]
                        mm = pe.matmul(att[bank][:, col:col + WK[s]], mk[:, h, s * P:(s + 1) * P], mq[:, h, s * P:T],
                                       start=True, stop=True)
                    s_K.on(mm)
                    for n, row in (("mu", g_mu), ("mm", g_m)):
                        out = G.open(pe, f"{n}{h}")
                        G.close(pe.matmul(out[:, :], sel[0:ML_H, h * P:(h + 1) * P], row, start=True, stop=True))
                    pe.wait_ge(s_ws.sem, 3 * (h + 1))
                    for n in ("den", "num"):
                        out = G.open(pe, f"{n}{h}")
                        for s in range(TB):
                            w = ones if n == "den" else mv[:, s, h * P:(h + 1) * P]
                            mm = pe.matmul(out[:, s * P:T], w, probs[:, h % 2, KOFF[s]:KOFF[s] + WK[s]],
                                           start=(s == 0), stop=(s == TB - 1), skip_group_check=True)
                        G.close(mm)
                    out = G.open(pe, f"mean{h}")
                    G.moved(pe, f"num{h}")
                    G.close(pe.matmul(out[:, :], ones, hml, start=True, stop=True))
                    out = G.open(pe, f"var{h}")
                    pe.wait_ge(s_sq2.sem, h + 1)
                    G.close(pe.matmul(out[:, :], ones, hsq, start=True, stop=True))

                for d in range(KD):
                    for k in range(3):
                        dense(f"gate{d}{k}", f"merge{d}", 3 * P, k * P)
                        out = G.open(pe, f"proj{d}{k}")
                        landed(pe, f"branch{d // 2}")
                        if d == 0 and k == 2:
                            pe.wait_ge(s_mlz.sem, ML_H)
                        if d == 0:
                            G.moved(pe, "dsa7" if k == 0 else "sb7")
                        w = slot(f"branch{d // 2}")
                        y = (za, zb, zc)[k]
                        for j in range(4):
                            at = (k * 4 + j) * 2 * P + (d % 2) * P
                            mm = pe.matmul(out[:, :], w[:, at:at + P], y[:, j, :], start=(j == 0), stop=(j == 3))
                        G.close(mm)
                for d in range(KD):
                    out = G.open(pe, f"out{d}")
                    landed(pe, f"out{d // 4}")
                    w = slot(f"out{d // 4}")
                    for k in range(KD):
                        if d == 0:
                            pe.wait_ge(s_mix.sem, k + 1)
                        mm = pe.matmul(out[:, :], w[:, k * T + (d % 4) * P:k * T + (d % 4 + 1) * P], mixed[:, k, :],
                                       start=(k == 0), stop=(k == KD - 1))
                    G.close(mm)

            @block.scalar
            def _(act):
                def move(name, out, func=ACT.Copy, rows_=None, **kw):
                    bank = G.whole(act, name)
                    src = bank[:, 0:T] if rows_ is None else bank[:, rows_]
                    G.empty(act.activation(out, src, func, **kw), name)

                for k in range(KD):
                    s_sq.on(act.activation(hT[:, k, :], xT[:, k, :], ACT.Square))
                move("ms", rstd[:], ACT.Sqrt, scale=1.0 / D, bias=mark["eps"])
                for i in range(4):
                    move(f"idx{i}", idx[:, i, :])
                move("misc", misc[:])
                move("q0", dq[:, 0, :], scale=HD ** -0.5)
                settle(act, s_a)
                s_csq.on(act.activation(csq, ckv, ACT.Square))
                act.wait_ge(s_vec.sem, 16)
                s_ir.on(act.activation(g_i, misc[32:32 + ML_H, :], ACT.Identity, bias=vecs[32:32 + ML_H, 45:46]))
                s_ir.on(act.activation(g_f, misc[64:64 + ML_H, :], ACT.Identity, bias=vecs[64:64 + ML_H, 46:47]))
                for i in range(1, 4):
                    move(f"q{i}", dq[:, i, :], scale=HD ** -0.5)
                n = 0
                for b in range(1, TB):
                    for h in range(IDX_H):
                        if n >= 2:
                            act.wait_ge(s_scused.sem, n - 1)
                        move(f"sc{b}{h}", relu[:, n % 2, 0:WQ[b]], ACT.Relu, rows_=slice(0, WQ[b]))
                        n += 1
                act.preload_act_table_set("natural_log_exp_and_others")
                s_ac.on(act.activation(g_sum, g_f, ACT.Abs))
                settle(act, s_ac)
                s_ac.on(act.activation(g_sum, g_sum, ACT.Exp, scale=-1.0))
                settle(act, s_ac)
                s_ln.on(act.activation(g_sum, g_sum, ACT.Ln, bias=1.0))
                move("cms", rstd[:], ACT.Sqrt, scale=1.0 / P, bias=mark["eps"])
                for i in range(4):
                    move(f"za{i}", za[:, i, :], ACT.Silu)
                for i in range(4):
                    move(f"kk{i}", dk[:, i, :])
                for b in range(TB):
                    move(f"vv{b}", dv[:, b, :])
                for i in range(4):
                    move(f"zb{i}", zb[:, i, :], ACT.Silu)
                for i in range(4):
                    move(f"sbq{i}", sq_[:, i, :], scale=HD ** -0.5)
                for i in range(4):
                    move(f"sbk{i}", sk[:, i, :])
                for i in range(4):
                    move(f"sbv{i}", sv[:, i, :])
                act.preload_act_table_set("natural_log_exp_and_others")
                for h in range(HEADS):
                    act.wait_ge(s_logit.sem, TB * (h + 1))
                    act.wait_ge(s_rinv.sem, 2 * h + 1)
                    for b in range(TB):
                        s_exp.on(act.activation(probs[:, h % 2, OQ[b]:OQ[b] + WQ[b]], probs[:, h % 2, OQ[b]:OQ[b] + WQ[b]],
                                                ACT.Exp, bias=small[:, 8 + 4 * (h % 2) + b:9 + 4 * (h % 2) + b],
                                                accum_out=small[:, 16 + 4 * (h % 2) + b:17 + 4 * (h % 2) + b]))
                    n = "mlq" if h < 4 else "mlk"
                    if h == 0:
                        act.wait_ge(s_bias.sem, TB)
                        act.wait_ge(s_pad.sem, 1)
                        G.moved(act, "vv3")
                    move(f"{n}{h % 4}", raw[:, h, 3:3 + T])
                    act.wait_ge(s_T.sem, h + 1)
                    if h >= 2:
                        G.whole(act, f"dsa{h - 2}")
                    s_TA.on(act.activation(turned[:, h % 2, 0:T], att[3][:, :], ACT.Copy))
                for h in range(HEADS):
                    act.wait_ge(s_Z.sem, h + 1)
                    if h <= 1:
                        act.wait_ge(s_T.sem, HEADS)
                    else:
                        act.wait_ge(s_tri.sem, h - 1)
                    for bank, n, at in BANKS:
                        s_ac.on(act.activation(probs[:, h % 2, at:at + n], att[3 * (h % 2) + bank][:, 0:n], ACT.Abs))
                    settle(act, s_ac)
                    s_ac.on(act.activation(probs[:, h % 2, :], probs[:, h % 2, :], ACT.Exp, scale=-1.0))
                    settle(act, s_ac)
                    s_soft.on(act.activation(probs[:, h % 2, :], probs[:, h % 2, :], ACT.Ln, bias=1.0))
                    if h % 2 == 0:
                        move(f"mlv{h // 2}", mv[:, h // 2, :])
                    act.wait_ge(s_tri.sem, h + 1)
                    if h >= 2:
                        G.whole(act, f"sb{h - 2}")
                    else:
                        G.whole(act, f"dsa{HEADS - 2 + h}")
                    for bank, n, at in BANKS:
                        s_a_exp.on(act.activation(turned[:, h % 2, at:at + n], att[3 * (h % 2) + bank][:, 0:n], ACT.Exp))
                for i in range(4):
                    move(f"mlo{i}", mlo[:, i, :], ACT.Sigmoid)
                for i in range(4):
                    move(f"zc{i}", zc[:, i, :], ACT.Silu)
                act.wait_ge(s_conv.sem, 4)
                s_silu.on(act.activation(mq[:], mq[:], ACT.Silu))
                act.wait_ge(s_conv.sem, 8)
                s_silu.on(act.activation(mk[:], mk[:], ACT.Silu))
                for h in range(ML_H):
                    bank = G.whole(act, f"mu{h}")
                    if h <= 1:
                        G.whole(act, f"sb{HEADS - 2 + h}")
                        act.wait_ge(s_tri.sem, HEADS)
                    else:
                        act.wait_ge(s_ws.sem, 3 * (h - 1))
                    for s in range(TB):
                        ins = act.activation(turned[:, h % 2, KOFF[s]:KOFF[s] + WK[s]], bank[:, s * P:T], ACT.Exp,
                                             bias=acol[:, s, h:h + 1])
                        if s < TB - 1:
                            s_w8.on(ins)
                    G.empty(ins, f"mu{h}")
                    bank = G.whole(act, f"mm{h}")
                    if h >= 1:
                        G.moved(act, f"num{h - 1}")
                    G.empty(act.activation(em, bank[:, :], ACT.Exp), f"mm{h}")
                    move(f"den{h}", dn, ACT.Abs)
                    G.moved(act, f"mean{h}")
                    s_sq2.on(act.activation(hsq, hml, ACT.Square))
                    move(f"var{h}", rstd[:], ACT.Sqrt, scale=1.0 / ML_D, bias=mark["eps"])
                for d in range(KD):
                    for k in range(3):
                        if d >= 1:
                            G.moved(act, f"proj{d - 1}{k}")
                        elif k == 0:
                            G.whole(act, f"num{ML_H - 1}")
                        move(f"gate{d}{k}", gate[:, k, :], ACT.Sigmoid)

            @block.vector
            def _(dve):
                def link(ins):
                    s_vc.on(ins)
                    settle(dve, s_vc)

                def rotate(name, x, n, ready):
                    bank = G.whole(dve, name)
                    turn = dv[0:n, 0, :]
                    G.empty(dve.tensor_tensor(turn, bank[0:n, :], sinT[0:n, :], ALU.mult), name)
                    link(dve.tensor_tensor(x, x, cosT[0:n, :], ALU.mult))
                    settle(dve, s_v)
                    ready.on(dve.tensor_tensor(x, x, turn, ALU.add))
                    settle(dve, ready)

                dve.wait_ge(s_vec.sem, 16)
                G.moved(dve, "ms")
                link(dve.reciprocal(rstd[:], rstd[:]))
                for k in range(KD):
                    s_h.on(dve.scalar_tensor_tensor(hT[:, k, :], xT[:, k, :], vecs[:, k:k + 1], rstd[:], ALU.mult, ALU.mult))
                for i in range(3):
                    rotate(f"ridx{i}", idx[:, i, :], P, s_ridx)
                bank = G.whole(dve, "iwt")
                G.empty(dve.tensor_copy(iwt[:].rearrange("p a b -> p (a b)"), bank[:, 0:TB * IDX_H]), "iwt")
                settle(dve, s_v)
                n = 0
                for b in range(1, TB):
                    out = score[:, OQ[b]:OQ[b] + WQ[b]]
                    for h in range(IDX_H):
                        G.moved(dve, f"sc{b}{h}")
                        r, w = relu[:, n % 2, 0:WQ[b]], iwt[:, b, h:h + 1]
                        if h == 0:
                            s_scused.on(dve.tensor_scalar(out, r, w, None, ALU.mult))
                        else:
                            s_scused.on(dve.scalar_tensor_tensor(out, r, w, out, ALU.mult, ALU.add))
                        settle(dve, s_scused)
                        n += 1
                for i in range(4):
                    rotate(f"rq{i}", dq[:, i, :], P, s_rq)
                rotate("rkr", misc[0:ROPE, :], ROPE, s_rkr)
                link(dve.memset(g_mu, 1.0))
                dve.wait_ge(s_ln.sem, 1)
                link(dve.scalar_tensor_tensor(g_f, g_f, 0.0, g_sum, ALU.min, ALU.subtract))
                link(dve.tensor_tensor_scan(g_sum, g_mu, g_f, 0.0, ALU.mult, ALU.add))
                link(dve.tensor_tensor(g_a, g_i, g_sum, ALU.subtract))
                link(dve.tensor_tensor_scan(g_m, g_a, g_a, 0.0, ALU.max, ALU.max))
                link(dve.tensor_scalar(g_mu, g_m, -1.0, None, ALU.mult))
                s_gates.on(dve.scalar_tensor_tensor(g_m, g_sum, -1.0, g_m, ALU.mult, ALU.subtract))
                G.moved(dve, "cms")
                link(dve.reciprocal(rstd[:], rstd[:]))
                s_ckv.on(dve.scalar_tensor_tensor(ckv, ckv, vecs[:, 8:9], rstd[:], ALU.mult, ALU.mult))
                bank = G.whole(dve, "at")
                G.empty(dve.tensor_copy(acol[:].rearrange("p a b -> p (a b)"), bank[:, 0:TB * ML_H]), "at")
                dve.wait_ge(s_masked.sem, TB - 1)
                for _ in range(TOPK // 8):
                    for b in range(1, TB):
                        x = score[:, OQ[b]:OQ[b] + WQ[b]]
                        link(dve.max(top8[:, b, :], x))
                        link(dve.match_replace(out=x, in_to_replace=top8[:, b, :], in_values=x, imm_value=TAKEN))
                s_bias.on(dve.tensor_copy(bias[:, 0:P], cmask))
                for b in range(1, TB):
                    o = slice(OQ[b], OQ[b] + WQ[b])
                    s_bias.on(dve.tensor_scalar(bias[:, o], score[:, o], ALIVE, NEG, ALU.is_gt, ALU.mult))
                settle(dve, s_bias)
                G.moved(dve, "vv3")
                s_pad.on(dve.memset(raw[:, :, 0:3], 0.0))

                def dsa_logits(h):
                    o = 4 * (h % 2)
                    dve.wait_ge(s_S.sem, h + 1)
                    if h >= 2:
                        dve.wait_ge(s_T.sem, h - 1)
                    for b in range(TB):
                        bank, col = KPLACE[TB - 1 - b]
                        s = slice(OQ[b], OQ[b] + WQ[b])
                        s_logit.on(dve.tensor_tensor_reduce(
                            out=probs[:, h % 2, s], in0=att[bank][:, col:col + WQ[b]], in1=bias[:, s], scale=1.0,
                            scalar=TAKEN, op0=ALU.add, op1=ALU.max, accum_out=small[:, o + b:o + b + 1]))
                    settle(dve, s_logit)
                    s_rinv.on(dve.tensor_scalar(small[:, 8 + o:12 + o], small[:, o:o + 4], -1.0, None, ALU.mult))

                def dsa_turned(h):
                    dve.wait_ge(s_T.sem, h + 1)
                    if h >= 2:
                        G.whole(dve, f"dsa{h - 2}")
                    for bank, n, at in BANKS[1:]:
                        s_TV.on(dve.tensor_copy(turned[:, h % 2, at:at + n], att[3 + bank][:, 0:n]))

                def gated(name, h, z):
                    bank = G.whole(dve, name)
                    r = slice(64 * (h % 2), 64 * (h % 2) + 64)
                    G.empty(dve.tensor_tensor(z[r, h // 2, :], bank[r, :], z[r, h // 2, :], ALU.mult), name)

                G.moved(dve, "za3")
                for h in range(HEADS + 1):
                    if h < HEADS:
                        dsa_logits(h)
                    if h >= 1:
                        dsa_turned(h - 1)
                        gated(f"dsa{h - 1}", h - 1, za)
                    if h < HEADS:
                        o = 4 * (h % 2)
                        dve.wait_ge(s_exp.sem, TB * (h + 1))
                        s_rinv.on(dve.reciprocal(small[:, 24 + o:28 + o], small[:, 16 + o:20 + o]))
                for h in range(HEADS + 1):
                    if h < HEADS:
                        dve.wait_ge(s_soft.sem, h + 1)
                        for bank, n, at in BANKS:
                            s_sp.on(dve.scalar_tensor_tensor(probs[:, h % 2, at:at + n], att[3 * (h % 2) + bank][:, 0:n], 0.0,
                                                             probs[:, h % 2, at:at + n], ALU.max, ALU.add))
                        G.moved(dve, ("mlq" if h < 4 else "mlk") + str(h % 4))
                        dst = (mq if h < 4 else mk)[:, h % 4, :]
                        link(dve.tensor_scalar(dst, raw[:, h, 0:T], vecs[:, 9 + h:10 + h], None, ALU.mult))
                        for j in range(1, 4):
                            s_conv_ = s_conv if j == 3 else s_vc
                            s_conv_.on(dve.scalar_tensor_tensor(dst, raw[:, h, j:j + T], vecs[:, 9 + 8 * j + h:10 + 8 * j + h],
                                                                dst, ALU.mult, ALU.add))
                            settle(dve, s_conv_)
                    if h >= 1:
                        gated(f"sb{h - 1}", h - 1, zb)
                G.moved(dve, "zc3")
                for h in range(ML_H):
                    dve.wait_ge(s_w8m.sem, TB * (h + 1))
                    dve.wait_ge(s_K.sem, h + 1)
                    if h >= 2:
                        G.whole(dve, f"num{h - 2}")
                    for bank, n, at in BANKS:
                        s_ws.on(dve.scalar_tensor_tensor(probs[:, h % 2, at:at + n], att[bank][:, 0:n], ML_D ** -0.5,
                                                         turned[:, h % 2, at:at + n], ALU.mult, ALU.mult))
                    G.moved(dve, f"mm{h}")
                    G.moved(dve, f"den{h}")
                    link(dve.tensor_tensor(dn, dn, em, ALU.max))
                    link(dve.reciprocal(dn, dn))
                    bank = G.whole(dve, f"num{h}")
                    G.empty(dve.tensor_tensor(hml, bank[:, :], dn, ALU.mult), f"num{h}")
                    settle(dve, s_v)
                    bank = G.whole(dve, f"mean{h}")
                    G.empty(dve.scalar_tensor_tensor(hml, bank[:, :], -1.0 / ML_D, hml, ALU.mult, ALU.add), f"mean{h}")
                    settle(dve, s_v)
                    G.moved(dve, f"var{h}")
                    link(dve.reciprocal(rstd[:], rstd[:]))
                    link(dve.scalar_tensor_tensor(hml, hml, vecs[:, 41 + h:42 + h], rstd[:], ALU.mult, ALU.mult))
                    link(dve.tensor_tensor(hml, hml, mlo[:, h, :], ALU.mult))
                    s_mlz.on(dve.tensor_tensor(zc[:, h, :], zc[:, h, :], hml, ALU.mult))
                    settle(dve, s_mlz)
                for d in range(KD):
                    for k in range(3):
                        n = f"proj{d}{k}"
                        bank = G.whole(dve, n)
                        G.moved(dve, f"gate{d}{k}")
                        out = mixed[:, d, :] if k == 0 else part[:, k - 1, :]
                        G.empty(dve.tensor_tensor(out, bank[:, :], gate[:, k, :], ALU.mult), n)
                        settle(dve, s_v)
                        if k == 1:
                            link(dve.tensor_tensor(mixed[:, d, :], mixed[:, d, :], part[:, 0, :], ALU.add))
                        if k == 2:
                            s_mix.on(dve.tensor_tensor(mixed[:, d, :], mixed[:, d, :], part[:, 1, :], ALU.add))
                for d in range(KD):
                    n = f"out{d}"
                    bank = G.whole(dve, n)
                    G.empty(dve.tensor_tensor(xT[:, d, :], bank[:, :], xT[:, d, :], ALU.add), n)

            @block.gpsimd
            def _(pool):
                def triangle(x, op, sign, fill):
                    return pool.affine_select(out=x, in_=x, compare_op=op, fill=fill, base=0, pattern=[[sign, P]],
                                              channel_multiplier=-sign)

                for b in range(1, TB):
                    pool.wait_ge(s_scused.sem, IDX_H * b)
                    s_masked.on(triangle(score[:, OQ[b] + b * P:OQ[b] + (b + 1) * P], ALU.is_ge, -1, DROPPED))
                for h in range(HEADS):
                    pool.wait_ge(s_rinv.sem, 2 * h + 2)
                    for b in range(TB):
                        x = probs[:, h % 2, OQ[b]:OQ[b] + WQ[b]]
                        o = 24 + 4 * (h % 2) + b
                        s_scaled.on(pool.tensor_scalar(x, x, small[:, o:o + 1], 1.0, ALU.mult, ALU.mult))
                for h in range(HEADS):
                    pool.wait_ge(s_sp.sem, 3 * (h + 1))
                    for s in range(TB):
                        s_spm.on(triangle(probs[:, h % 2, KOFF[s]:KOFF[s] + P], ALU.is_gt, 1, 0.0))
                    pool.wait_ge(s_a_exp.sem, 3 * (h + 1))
                    for s in range(TB):
                        s_am.on(triangle(turned[:, h % 2, KOFF[s]:KOFF[s] + P], ALU.is_gt, 1, 0.0))
                for h in range(ML_H):
                    G.moved(pool, f"mu{h}")
                    for s in range(TB):
                        s_w8m.on(triangle(turned[:, h % 2, KOFF[s]:KOFF[s] + P], ALU.is_ge, 1, 0.0))

        with nc.Block() as block:

            @block.sync
            def _(sp):
                for s in every:
                    sp.sem_clear(s.sem)



FF = 2816
KF = FF // P
PATTERNS = 3
SLOTS_H = 4
XH, XD, MEM = 4, 128, 256
SG, SS = 32, 64
NT = SG * SS // P
AW = PATTERNS * SLOTS_H * HD
CHUNK = 3072
RING = 3
MAGIC = 12582912.0
TWO_PI = 6.283185
HALF_PI = 1.5707963
PI_A, PI_B = 6.28125, 0.0019350051879882812
PI_C = 2 * np.pi - PI_A - PI_B
TOEP = 640

DIL = [[(max(0, b - 1) * P, P * (1 + (b > 0))) for b in range(TB)]] + [[(0, WQ[b]) for b in range(TB)]] * 2
DOFF, _at = [], 0
for _g in range(PATTERNS):
    DOFF.append([])
    for _b in range(TB):
        DOFF[_g].append(_at)
        _at += DIL[_g][_b][1]
DALL = _at

VEC2 = {}
_c = 0
for _n, _w in (("fin1", KD), ("ffn1", KD), ("mix", KD), ("ffn2", KD), ("fin2", KD), ("mem", KD), ("skip", 4),
               ("are", NT), ("aim", NT), ("ldt", NT)):
    VEC2[_n] = (_c, _c + _w)
    _c += _w
N_VEC2 = _c
NORMS = ["fin1", "ffn1", "mix", "ffn2", "fin2"]

FILLERS = [("q", i) for i in range(6)] + [("k", i) for i in range(6)] + [("v", i) for i in range(2 * TB)] + [("xq", i) for i in range(4)]


def fillers_of(j):
    return FILLERS[j * len(FILLERS) // NT:(j + 1) * len(FILLERS) // NT]


def stream():
    tiles = []
    def ffn(n):
        for i in range(KF):
            tiles.append((f"{n}a{i}", KD * P)); tiles.append((f"{n}b{i}", KD * P))
        for d in range(KD):
            tiles.append((f"{n}d{d}", KF * P))
    ffn("f1")
    for i in range(4):
        tiles.append((f"mk{i}", KD * P))
    for i in range(4):
        tiles.append((f"mv{i}", KD * P))
    for i in range(4):
        tiles.append((f"u{i}", KD * P))
    for n, c in (("q", 6), ("k", 6)):
        for i in range(c):
            tiles.append((f"{n}{i}", KD * P))
    for i in range(2):
        tiles.append((f"v{i}", KD * 3 * P))
    for i in range(4):
        tiles.append((f"xq{i}", KD * P))
    for d in range(KD):
        for k in range(3):
            tiles.append((f"g{k}{d}", KD * P))
        tiles += [(f"glb{d}", 4 * P), (f"gla{d}", 4 * P), (f"up{d}", 2 * P), (f"xup{d}", 4 * P)]
    for d in range(KD):
        tiles.append((f"o{d}", KD * P))
    ffn("f2")
    place, chunk, used = {}, 0, 0
    for n, size in tiles:
        if used + size > CHUNK:
            chunk, used = chunk + 1, 0
        place[n] = (chunk, used)
        used += size
    return place, chunk + 1


STREAM, N_STREAM = stream()


def block_groups():
    def ffn(n):
        g = []
        for i in range(KF):
            g += [(f"{n}a{i}", "a"), (f"{n}b{i}", "v")]
        return g + [(f"{n}d{d}", "v") for d in range(KD)]
    g = [(f"toep{i}", "a") for i in range(4)]
    g += [("ms_fin1", "a"), ("ms_ffn1", "a")] + ffn("f1")
    g += [("ms_mem", "a")] + [(f"mk{i}", "a") for i in range(4)] + [(f"mv{i}", "a") for i in range(2)]
    g += [("ms_mix", "a")] + [(f"u{i}", "a") for i in range(4)]
    for j in range(NT):
        g += [(f"{n}{i}", "a") for n, i in fillers_of(j)]
    g += [(f"att{h}", "v") for h in range(SLOTS_H)]
    g += [(f"xo{h}", "v") for h in range(XH)]
    for d in range(KD):
        g += [(f"g0{d}", "a"), (f"glb{d}", "a"), (f"gla{d}", "v"), (f"g1{d}", "a"), (f"up{d}", "v"), (f"g2{d}", "a"), (f"xup{d}", "v")]
    g += [(f"o{d}", "v") for d in range(KD)]
    g += [("ms_ffn2", "a")] + ffn("f2") + [("ms_fin2", "a")]
    return g


CONST2 = {"ident": (0, P), "ones": (P, 2 * P), "iota": (2 * P, 2 * P + T)}
N_CONST2 = 2 * P + T


def second_block(nc, stack, xT, A, scratch, out_dram):
    def sb(name, shape, dt=F32):
        return stack.enter_context(nc.sbuf_tensor("b2_" + name, shape, dt))

    def sem(name):
        return Signal(stack.enter_context(nc.semaphore("b2_" + name)))

    hT = sb("hT", [P, KD, T])
    ring = sb("ring", [P, RING, CHUNK])
    vecs = sb("vecs", [P, N_VEC2])
    consts = sb("consts", [P, N_CONST2])
    ident, ones, iota = (consts[:, a:b] for a, b in CONST2.values())
    big = sb("big", [P, KF, T])
    uT = sb("uT", [P, 4, T])
    qk = sb("qk", [P, 12, T])
    v = sb("v", [P, TB, AW])
    xq = sb("xq", [P, XH, T])
    mk = sb("mk", [P, XH, MEM])
    logits = sb("logits", [P, DALL])
    turned = sb("turned", [P, 2, CAUSAL])
    biases = sb("biases", [P, PATTERNS, T])
    rstd = sb("rstd", [P, T])
    st = sb("st", [P, 24, NT])
    am = sb("am", [P, 64])
    q, k = qk[:, 0:6, :], qk[:, 6:12, :]
    merged = qk[:, 0:KD, :]
    memT = logits[:, 0:KD * MEM].rearrange("p (a b) -> p a b", a=KD)
    memsq = turned[:].rearrange("p a b -> p (a b)")[:, 0:KD * MEM].rearrange("p (a b) -> p a b", a=KD)
    onehot = logits[:, 0:3 * TOEP]
    table = logits[0:33, 3 * TOEP:3 * TOEP + 12]
    toep = big[0:12, 0:4, :].rearrange("p a b -> p (a b)")[:, 0:3 * TOEP]
    gates = turned[:].rearrange("p a b -> p (a b)")[:, 0:4 * T].rearrange("p (a b) -> p a b", a=4)
    parts = logits[:, 0:2 * T].rearrange("p (a b) -> p a b", a=2)
    bflat = big[:].rearrange("p a b -> p (a b)")
    work = [[big[:, 6 * s + i, :] for i in range(6)] for s in range(2)]
    b_in = [bflat[:, (12 + i) * T:(13 + i) * T] for i in range(2)]
    c_raw = [bflat[:, (14 + i) * T:(15 + i) * T].rearrange("p (a b) -> p a b", a=NT) for i in range(2)]
    c_out = [bflat[:, (16 + i) * T:(17 + i) * T].rearrange("p (a b) -> p a b", a=NT) for i in range(2)]
    yatt, mv = big[:, 18:20, :], big[:, 20:22, :]
    halfpi, epsc = st[:, 23, 0:1], st[:, 23, 1:2]

    proj = [stack.enter_context(nc.psum_tensor(f"b2_proj{i}", [P, T], F32)) for i in range(2)]
    att = [stack.enter_context(nc.psum_tensor(f"b2_att{i}", [P, T], F32)) for i in range(6)]

    (s_const, s_onehot, s_done, s_a, s_v, s_sq, s_h, s_vc, s_ac, s_pc, s_set, s_toep, s_ssm, s_mem, s_msq, s_mh, s_out,
     s_dt, s_r, s_trig, s_cw, s_ph, s_tab, s_bu, s_rot, s_w, s_z, s_x, s_y, s_yv, s_yg,
     s_S, s_lg, s_neg, s_exp, s_rinv, s_scaled, s_T, s_TA, s_TV, s_am2,
     s_xS, s_xneg, s_xexp, s_xrinv, s_xscaled, s_xT, s_xTA, s_xTV, s_merged) = (sem(n) for n in (
         "const onehot done act_moved dve_moved square h dve act pool set toep ssm mem msq mh out "
         "dt r trig cw phase table bu rot w z x y yv yg "
         "S logit neg exp rinv scaled T TA TV am2 "
         "xS xneg xexp xrinv xscaled xT xTA xTV merged").split())
    s_w8 = [sem(f"w{i}") for i in range(RING)]
    s_bias = [sem(f"bias{i}") for i in range(PATTERNS)]

    G = Groups(block_groups(), proj, s_done, {"a": s_a, "v": s_v})
    after_last = {}
    for n, _ in block_groups():
        key = {"v": f"v{int(n[1:]) % 2}"}.get(n[0]) if n[0] == "v" else n
        if n in ("mv0", "mv1"):
            after_last[STREAM["mv3"][0]] = n
            after_last[STREAM["mv0"][0]] = n
            after_last[STREAM["mv1"][0]] = after_last[STREAM["mv2"][0]] = n
        elif key in STREAM:
            after_last[STREAM[key][0]] = n

    def vec(name, i=0, n=1):
        a = VEC2[name][0] + i
        return vecs[:, a:a + n]

    def weight(eng, name):
        chunk, off = STREAM[name]
        eng.wait_ge(s_w8[chunk % RING].sem, 16 * (chunk // RING + 1))
        return ring[:, chunk % RING, off:]

    with nc.Block() as block:

        @block.sync
        def _(sp):
            s_const.on(sp.dma_start(consts[:], A["const2"]), 16)
            s_const.on(sp.dma_start(vecs[:], A["vec2"]), 16)
            s_onehot.on(sp.dma_start(onehot[0:33, :], A["onehot"]), 16)
            s_onehot.on(sp.dma_start(table, A["table"]), 16)
            for c in range(N_STREAM):
                if c >= RING:
                    sp.wait_ge(s_done.sem, G.at[after_last[c - RING]] + 1)
                s_w8[c % RING].on(sp.dma_start(ring[:, c % RING, :], A["stream"][c]), 16)
            G.moved(sp, "ms_fin2")
            sp.wait_ge(s_h.sem, KD * len(NORMS))
            s_out.on(sp.dma_start(out_dram, hT[:]), 16)
            sp.wait_ge(s_out.sem, 16)

        @block.gpsimd
        def _(pool):
            G.moved(pool, "toep3")
            for r in range(PATTERNS * SLOTS_H):
                g = r // SLOTS_H
                row = toep[r:r + 1, g * TOEP:(g + 1) * TOEP].unsqueeze(1).to_broadcast([1, P, TOEP])
                s_toep.on(pool.dma_start(scratch[r:r + 1], row), 16)
            pool.wait_ge(s_toep.sem, 16 * PATTERNS * SLOTS_H)
            s_mem.on(pool.dma_start(memT, A["mem"]), 16)
            G.whole(pool, "f1d7")
            for i, n in enumerate(("bre", "bim")):
                s_ssm.on(pool.dma_start(b_in[i], A[n]), 16)
            for i, n in enumerate(("cre", "cim")):
                s_ssm.on(pool.dma_start(c_raw[i], A[n]), 16)

            def link(ins):
                s_pc.on(ins)
                settle(pool, s_pc)

            def load_bias(n):
                h, g = divmod(n, PATTERNS)
                if h >= 1:
                    pool.wait_ge(s_lg.sem, TB * (n - PATTERNS + 1))
                width = 2 * P if g == 0 else T
                row = (g * SLOTS_H + h) * P * TOEP
                src = bass.AP(scratch.tensor, row + P - 1, [[TOEP - 1, P], [1, width]])
                s_bias[g].on(pool.dma_start(biases[:, g, 0:width], src), 16)

            for n in range(PATTERNS):
                load_bias(n)
            for j in range(NT):
                c, s, t1, t2, t3, t4 = work[j % 2]
                pool.wait_ge(s_rot.sem, 4 * (j + 1))
                s_w.on(pool.tensor_tensor(t1, t1, t2, ALU.add))
                s_w.on(pool.tensor_tensor(t3, t3, t4, ALU.subtract))
                pool.wait_ge(s_z.sem, 2 * (j + 1))
                s_pc.on(pool.tensor_tensor(t2, t1, c, ALU.mult))
                link(pool.tensor_tensor(t4, t3, s, ALU.mult))
                s_pc.on(pool.tensor_tensor(t2, t2, t4, ALU.subtract))
                s_pc.on(pool.tensor_tensor(t1, t1, s, ALU.mult))
                link(pool.tensor_tensor(t3, t3, c, ALU.mult))
                s_x.on(pool.tensor_tensor(t1, t1, t3, ALU.add))
            for h in range(SLOTS_H):
                pool.wait_ge(s_rinv.sem, h + 1)
                for g in range(PATTERNS):
                    for b in range(TB):
                        x = logits[:, DOFF[g][b]:DOFF[g][b] + DIL[g][b][1]]
                        s_scaled.on(pool.tensor_scalar(x, x, am[:, 28 + b:29 + b], 1.0, ALU.mult, ALU.mult))
                if h + 1 < SLOTS_H:
                    for g in range(PATTERNS):
                        load_bias((h + 1) * PATTERNS + g)
            for h in range(XH):
                pool.wait_ge(s_xrinv.sem, h + 1)
                for b in range(TB):
                    x = logits[:, (h % 2) * TB * MEM + b * MEM:(h % 2) * TB * MEM + (b + 1) * MEM]
                    s_xscaled.on(pool.tensor_scalar(x, x, am[:, 60 - 4 * (h % 2) + b:61 - 4 * (h % 2) + b], 1.0, ALU.mult, ALU.mult))
            for i in range(PATTERNS):
                pool.wait_ge(s_bias[i].sem, 16 * SLOTS_H)

        @block.tensor
        def _(pe):
            def product(name, w, xs, rhs=None):
                out = G.open(pe, name)
                n = len(xs)
                for i, x in enumerate(xs):
                    mm = pe.matmul(out[:, 0:x.shape[-1]], w[:, i * P:(i + 1) * P], x, start=(i == 0), stop=(i == n - 1))
                G.close(mm)

            def dense(name, first=None):
                w = weight(pe, name)
                out = G.open(pe, name)
                for i in range(KD):
                    if first is not None:
                        pe.wait_ge(s_h.sem, KD * NORMS.index(first) + i + 1)
                    mm = pe.matmul(out[:, :], w[:, i * P:(i + 1) * P], hT[:, i, :], start=(i == 0), stop=(i == KD - 1))
                G.close(mm)

            def norm(n):
                out = G.open(pe, f"ms_{n}")
                for i in range(KD):
                    pe.wait_ge(s_sq.sem, KD * NORMS.index(n) + i + 1)
                    mm = pe.matmul(out[:, :], ones, hT[:, i, :], start=(i == 0), stop=(i == KD - 1))
                G.close(mm)

            def ffn(n, norm_name):
                for i in range(KF):
                    dense(f"{n}a{i}", norm_name if i == 0 else None)
                    dense(f"{n}b{i}")
                for d in range(KD):
                    w = weight(pe, f"{n}d{d}")
                    out = G.open(pe, f"{n}d{d}")
                    for i in range(KF):
                        if d == 0:
                            G.moved(pe, f"{n}b{i}")
                        mm = pe.matmul(out[:, :], w[:, i * P:(i + 1) * P], big[:, i, :], start=(i == 0), stop=(i == KF - 1))
                    G.close(mm)

            pe.wait_ge(s_const.sem, 32)
            pe.wait_ge(s_onehot.sem, 32)
            for i in range(4):
                out = G.open(pe, f"toep{i}")
                G.close(pe.matmul(out[0:12, 0:480], table, onehot[0:33, i * 480:(i + 1) * 480], start=True, stop=True))
            norm("fin1")
            norm("ffn1")
            ffn("f1", "ffn1")
            out = G.open(pe, "ms_mem")
            pe.wait_ge(s_msq.sem, KD)
            for i in range(KD):
                mm = pe.matmul(out[:, 0:MEM], ones, memsq[:, i, :], start=(i == 0), stop=(i == KD - 1))
            G.close(mm)
            pe.wait_ge(s_mh.sem, KD)
            for i in range(XH):
                product(f"mk{i}", weight(pe, f"mk{i}"), [memT[:, j, :] for j in range(KD)])
            for b in range(MEM // P):
                out = G.open(pe, f"mv{b}")
                for c in range(4):
                    w = weight(pe, f"mv{c}")
                    for i in range(KD):
                        mm = pe.matmul(out[:, c * P:(c + 1) * P], memT[:, i, b * P:(b + 1) * P], w[:, i * P:(i + 1) * P],
                                       start=(i == 0), stop=(i == KD - 1))
                G.close(mm)
            norm("mix")
            for i in range(4):
                dense(f"u{i}", "mix" if i == 0 else None)

            def ssm_in(j):
                r = slice(32 * (j % 4), 32 * (j % 4) + 32)
                if j >= 2:
                    pe.wait_ge(s_rot.sem, 4 * (j - 1))
                for i in range(2):
                    mm = pe.matmul(att[2 * (j % 2) + i][:, :], b_in[i][r, (j // 4) * P:(j // 4 + 1) * P], uT[r, j // 4, :],
                                   start=True, stop=True)
                s_bu.on(mm)

            def ssm_out(j):
                c, s, t1, t2, t3, t4 = work[j % 2]
                r = slice(32 * (j % 4), 32 * (j % 4) + 32)
                pe.wait_ge(s_x.sem, j + 1)
                if j >= 8:
                    pe.wait_ge(s_yv.sem, j // 4 - 1)
                bank = att[4 + (j // 4) % 2]
                pe.matmul(bank[r, :], c_out[0][:, j, :], t2, start=True, stop=False)
                s_y.on(pe.matmul(bank[r, :], c_out[1][:, j, :], t1, start=False, stop=True))

            pe.wait_ge(s_ssm.sem, 64)
            G.moved(pe, "u3")
            ssm_in(0)
            ssm_in(1)
            pe.wait_ge(s_cw.sem, 1)
            for j in range(NT):
                for n, i in fillers_of(j):
                    if n == "v":
                        b, half = divmod(i, 2)
                        w = weight(pe, f"v{half}")
                        out = G.open(pe, f"v{i}")
                        for kk in range(KD):
                            mm = pe.matmul(out[:, 0:3 * P], hT[:, kk, b * P:(b + 1) * P], w[:, kk * 3 * P:(kk + 1) * 3 * P],
                                           start=(kk == 0), stop=(kk == KD - 1))
                        G.close(mm)
                    else:
                        dense(f"{n}{i}")
                ssm_out(j)
                if j + 2 < NT:
                    ssm_in(j + 2)

            G.moved(pe, "xq3")
            pe.wait_ge(s_yv.sem, 4)
            for h in range(SLOTS_H):
                r = slice(64 * (h % 2), 64 * (h % 2) + 64)
                for g in range(PATTERNS):
                    tile = (g * SLOTS_H + h) // 2
                    if PATTERNS * h + g >= 1:
                        pe.wait_ge(s_lg.sem, TB * (PATTERNS * h + g))
                    for b in range(TB):
                        bank, col = KPLACE[TB - 1 - b]
                        k0, w = DIL[g][b]
                        mm = pe.matmul(att[bank][:, col:col + w], q[r, tile, b * P:(b + 1) * P], k[r, tile, k0:k0 + w],
                                       start=True, stop=True)
                    s_S.on(mm)
                out = G.open(pe, f"att{h}")
                for g in range(PATTERNS):
                    n = PATTERNS * h + g
                    pe.wait_ge(s_scaled.sem, TB * PATTERNS * h + TB * (g + 1))
                    if n >= 1:
                        pe.wait_ge(s_TA.sem, n)
                        pe.wait_ge(s_TV.sem, 2 * n)
                    for s in range(TB):
                        bank, col = KPLACE[s]
                        for b in range(s, TB):
                            k0, w = DIL[g][b]
                            if s * P < k0:
                                continue
                            o = DOFF[g][b] + s * P - k0
                            tr = pe.transpose(att[3 + bank][:, col + (b - s) * P:col + (b - s + 1) * P],
                                              logits[:, o:o + P], ident)
                    s_T.on(tr)
                    pe.wait_ge(s_TA.sem, n + 1)
                    pe.wait_ge(s_TV.sem, 2 * n + 2)
                    c0 = (g * SLOTS_H + h) * HD
                    for s in range(TB):
                        w = WK[s] if g else min(WK[s], 2 * P)
                        mm = pe.matmul(out[r, s * P:s * P + w], v[:, s, c0:c0 + HD],
                                       turned[:, n % 2, KOFF[s]:KOFF[s] + w],
                                       start=(g == 0 and s == 0), stop=(g == PATTERNS - 1 and s == TB - 1),
                                       skip_group_check=True)
                G.close(mm)

            def cross_scores(h):
                if h == 0:
                    pe.wait_ge(s_lg.sem, TB * PATTERNS * SLOTS_H)
                else:
                    pe.wait_ge(s_xexp.sem, TB * h)
                for b in range(TB):
                    mm = pe.matmul(att[b // 2][:, (b % 2) * MEM:(b % 2 + 1) * MEM], xq[:, h, b * P:(b + 1) * P], mk[:, h, :],
                                   start=True, stop=True)
                s_xS.on(mm)

            cross_scores(0)
            for h in range(XH):
                if h + 1 < XH:
                    cross_scores(h + 1)
                pe.wait_ge(s_xscaled.sem, TB * (h + 1))
                if h == 0:
                    pe.wait_ge(s_TA.sem, PATTERNS * SLOTS_H)
                    pe.wait_ge(s_TV.sem, 2 * PATTERNS * SLOTS_H)
                else:
                    pe.wait_ge(s_xTA.sem, h)
                    pe.wait_ge(s_xTV.sem, h)
                for m in range(MEM // P):
                    for b in range(TB):
                        o = (h % 2) * TB * MEM + b * MEM + m * P
                        tr = pe.transpose(att[3 + m][:, b * P:(b + 1) * P], logits[:, o:o + P], ident)
                s_xT.on(tr)
                out = G.open(pe, f"xo{h}")
                pe.wait_ge(s_xTA.sem, h + 1)
                pe.wait_ge(s_xTV.sem, h + 1)
                for m in range(MEM // P):
                    mm = pe.matmul(out[:, :], mv[:, m, h * XD:(h + 1) * XD], turned[:, h % 2, m * T:(m + 1) * T],
                                   start=(m == 0), stop=(m == MEM // P - 1))
                G.close(mm)

            pe.wait_ge(s_yg.sem, 4)
            for d in range(KD):
                dense(f"g0{d}")
                product(f"glb{d}", weight(pe, f"glb{d}"), [uT[:, i, :] for i in range(4)])
                product(f"gla{d}", weight(pe, f"gla{d}"), [uT[:, i, :] for i in range(4)])
                dense(f"g1{d}")
                if d == 0:
                    G.moved(pe, "att3")
                product(f"up{d}", weight(pe, f"up{d}"), [yatt[:, i, :] for i in range(2)])
                dense(f"g2{d}")
                if d == 0:
                    G.moved(pe, "xo3")
                product(f"xup{d}", weight(pe, f"xup{d}"), [xq[:, i, :] for i in range(4)])
            pe.wait_ge(s_merged.sem, KD)
            for d in range(KD):
                product(f"o{d}", weight(pe, f"o{d}"), [merged[:, i, :] for i in range(KD)])
            norm("ffn2")
            ffn("f2", "ffn2")
            norm("fin2")

        @block.scalar
        def _(act):
            def move(name, out, func=ACT.Copy, src=None, **kw):
                bank = G.whole(act, name)
                G.empty(act.activation(out, bank[:, :] if src is None else src(bank), func, **kw), name)

            def squares(n, ready):
                for i in range(KD):
                    ready(i)
                    s_sq.on(act.activation(hT[:, i, :], xT[:, i, :], ACT.Square))
                if n != "fin1":
                    act.wait_ge(s_h.sem, KD * NORMS.index(n))
                move(f"ms_{n}", rstd[:], ACT.Sqrt, scale=1.0 / D, bias=epsc)

            def ffn(n):
                for i in range(KF):
                    move(f"{n}a{i}", big[:, i, :], ACT.Silu)

            for i in range(4):
                move(f"toep{i}", toep[:, i * 480:(i + 1) * 480], src=lambda b: b[0:12, 0:480])
            act.wait_ge(s_set.sem, 2)
            squares("fin1", lambda i: None)
            squares("ffn1", lambda i: act.wait_ge(s_h.sem, i + 1))
            act.wait_ge(s_toep.sem, 16 * PATTERNS * SLOTS_H)
            ffn("f1")
            act.wait_ge(s_mem.sem, 16)
            for i in range(KD):
                s_msq.on(act.activation(memsq[:, i, :], memT[:, i, :], ACT.Square))
            act.wait_ge(s_h.sem, 2 * KD)
            move("ms_mem", rstd[:, 0:MEM], ACT.Sqrt, src=lambda b: b[:, 0:MEM], scale=1.0 / D, bias=epsc)
            for i in range(XH):
                move(f"mk{i}", mk[:, i, :], src=lambda b: b[:, 0:MEM])
            for i in range(MEM // P):
                move(f"mv{i}", mv[:, i, :])
            act.wait_ge(s_const.sem, 32)
            s_dt.on(act.activation(st[:, 0, :], vec("ldt", 0, NT), ACT.Exp))
            act.wait_ge(s_r.sem, 1)
            s_trig.on(act.activation(st[:, 3, :], st[:, 1, :], ACT.Exp))
            s_trig.on(act.activation(st[:, 4, :], st[:, 1, :], ACT.Tanh, scale=0.5))
            act.wait_ge(s_r.sem, 2)
            s_ac.on(act.activation(st[:, 5, :], st[:, 8, :], ACT.Abs))
            settle(act, s_ac)
            s_trig.on(act.activation(st[:, 6, :], st[:, 8, :], ACT.Sin))
            s_trig.on(act.activation(st[:, 7, :], st[:, 8, :], ACT.Sin, scale=0.5))
            s_trig.on(act.activation(st[:, 5, :], st[:, 5, :], ACT.Sin, scale=-1.0, bias=halfpi))

            squares("mix", lambda i: G.moved(act, f"f1d{i}"))
            for i in range(4):
                move(f"u{i}", uT[:, i, :])

            def table(j):
                c, s, t1, t2, t3, t4 = work[j % 2]
                act.wait_ge(s_ph.sem, j + 1)
                if j >= 2:
                    act.wait_ge(s_x.sem, j - 1)
                s_ac.on(act.activation(c, t2, ACT.Abs))
                settle(act, s_ac)
                s_tab.on(act.activation(s, t2, ACT.Sin, scale=TWO_PI))
                s_tab.on(act.activation(c, c, ACT.Sin, scale=-TWO_PI, bias=halfpi))

            table(0)
            table(1)
            for j in range(NT):
                for n, i in fillers_of(j):
                    if n == "v":
                        b, half = divmod(i, 2)
                        move(f"v{i}", v[:, b, half * 3 * P:(half + 1) * 3 * P], src=lambda b: b[:, 0:3 * P])
                    else:
                        dst = {"q": q, "k": k, "xq": xq}[n][:, i, :]
                        move(f"{n}{i}", dst, scale={"q": HD ** -0.5, "k": 1.0, "xq": 1.0}[n])
                if j + 2 < NT:
                    table(j + 2)
            for i in range(4):
                act.wait_ge(s_yv.sem, i + 1)
                s_yg.on(act.activation(uT[:, i, :], uT[:, i, :], ACT.Gelu_apprx_tanh))
            for h in range(SLOTS_H):
                act.wait_ge(s_neg.sem, h + 1)
                for g in range(PATTERNS):
                    for b in range(TB):
                        x = logits[:, DOFF[g][b]:DOFF[g][b] + DIL[g][b][1]]
                        s_exp.on(act.activation(x, x, ACT.Exp, bias=am[:, 12 + b:13 + b],
                                                accum_out=am[:, 16 + 4 * g + b:17 + 4 * g + b]))
                for g in range(PATTERNS):
                    n = PATTERNS * h + g
                    act.wait_ge(s_T.sem, n + 1)
                    w = T if g else 2 * P
                    s_TA.on(act.activation(turned[:, n % 2, 0:w], att[3][:, 0:w], ACT.Copy))
            for h in range(XH):
                act.wait_ge(s_xneg.sem, h + 1)
                if h >= 2:
                    act.wait_ge(s_xT.sem, h - 1)
                for b in range(TB):
                    o = (h % 2) * TB * MEM + b * MEM
                    s_xexp.on(act.activation(logits[:, o:o + MEM], att[b // 2][:, (b % 2) * MEM:(b % 2 + 1) * MEM], ACT.Exp,
                                             scale=XD ** -0.5, bias=am[:, 36 + 4 * (h % 2) + b:37 + 4 * (h % 2) + b],
                                             accum_out=am[:, 44 + 4 * (h % 2) + b:45 + 4 * (h % 2) + b]))
                act.wait_ge(s_xT.sem, h + 1)
                if h >= 2:
                    G.whole(act, f"xo{h - 2}")
                s_xTA.on(act.activation(turned[:, h % 2, 0:T], att[3][:, :], ACT.Copy))
            G.whole(act, f"xo{XH - 1}")
            for d in range(KD):
                for i, n in enumerate(("g0", "glb", "g1", "g2")):
                    if d >= 1:
                        G.moved(act, f"{('up', 'gla', 'up', 'xup')[i]}{d - 1}")
                    move(f"{n}{d}", gates[:, i, :], ACT.Sigmoid)
            def ready(i):
                if i == 0:
                    G.whole(act, "g27")
                G.moved(act, f"o{i}")
            squares("ffn2", ready)
            ffn("f2")
            squares("fin2", lambda i: G.moved(act, f"f2d{i}"))

        @block.vector
        def _(dve):
            def link(ins):
                s_vc.on(ins)
                settle(dve, s_vc)

            def norm(n, out):
                G.moved(dve, f"ms_{n}")
                link(dve.reciprocal(rstd[:], rstd[:]))
                for i in range(KD):
                    s_h.on(dve.scalar_tensor_tensor(out[:, i, :], xT[:, i, :], vec(n, i), rstd[:], ALU.mult, ALU.mult))
                settle(dve, s_h)

            def ffn(n):
                for i in range(KF):
                    bank = G.whole(dve, f"{n}b{i}")
                    G.moved(dve, f"{n}a{i}")
                    G.empty(dve.tensor_tensor(big[:, i, :], bank[:, :], big[:, i, :], ALU.mult), f"{n}b{i}")
                for d in range(KD):
                    bank = G.whole(dve, f"{n}d{d}")
                    G.empty(dve.scalar_tensor_tensor(xT[:, d, :], bank[:, :], 0.5, xT[:, d, :], ALU.mult, ALU.add), f"{n}d{d}")

            s_set.on(dve.memset(halfpi, HALF_PI))
            s_set.on(dve.memset(epsc, EPS))
            dve.wait_ge(s_const.sem, 32)
            norm("fin1", xT)
            norm("ffn1", hT)
            ffn("f1")
            G.moved(dve, "ms_mem")
            link(dve.reciprocal(rstd[:, 0:MEM], rstd[:, 0:MEM]))
            for i in range(KD):
                s_mh.on(dve.scalar_tensor_tensor(memT[:, i, :], memT[:, i, :], vec("mem", i), rstd[:, 0:MEM], ALU.mult, ALU.mult))
            settle(dve, s_mh)

            S = lambda i: st[:, i, :]
            tt = lambda o, a, b, op: link(dve.tensor_tensor(S(o), S(a) if isinstance(a, int) else a, S(b) if isinstance(b, int) else b, op))
            are, aim = vec("are", 0, NT), vec("aim", 0, NT)
            dve.wait_ge(s_dt.sem, 1)
            link(dve.tensor_tensor(S(1), are, S(0), ALU.mult))
            s_r.on(dve.tensor_tensor(S(2), aim, S(0), ALU.mult))
            settle(dve, s_r)
            link(dve.tensor_scalar(S(9), S(2), float(1 / (2 * np.pi)), MAGIC, ALU.mult, ALU.add))
            link(dve.tensor_scalar(S(9), S(9), MAGIC, None, ALU.subtract))
            link(dve.scalar_tensor_tensor(S(8), S(9), -PI_A, S(2), ALU.mult, ALU.add))
            link(dve.scalar_tensor_tensor(S(8), S(9), -PI_B, S(8), ALU.mult, ALU.add))
            link(dve.scalar_tensor_tensor(S(8), S(9), -float(PI_C), S(8), ALU.mult, ALU.add))
            s_r.on(dve.tensor_scalar(S(8), S(8), 3.1415925, -3.1415925, ALU.min, ALU.max))
            settle(dve, s_r)
            link(dve.tensor_scalar(S(10), S(8), float(1 / (2 * np.pi)), None, ALU.mult))
            link(dve.tensor_scalar(S(11), S(10), MAGIC / 16384, None, ALU.add))
            link(dve.tensor_scalar(S(11), S(11), MAGIC / 16384, None, ALU.subtract))
            link(dve.tensor_tensor(S(12), S(10), S(11), ALU.subtract))
            dve.wait_ge(s_trig.sem, 5)
            link(dve.scalar_tensor_tensor(S(13), S(3), 1.0, S(4), ALU.add, ALU.mult))
            tt(13, 13, 5, ALU.mult)
            tt(14, 7, 7, ALU.mult)
            link(dve.scalar_tensor_tensor(S(13), S(14), -2.0, S(13), ALU.mult, ALU.add))
            tt(14, 3, 6, ALU.mult)
            tt(15, are, are, ALU.mult)
            tt(16, aim, aim, ALU.mult)
            tt(15, 15, 16, ALU.add)
            link(dve.reciprocal(S(15), S(15)))
            tt(16, 13, are, ALU.mult)
            tt(17, 14, aim, ALU.mult)
            tt(16, 16, 17, ALU.add)
            tt(16, 16, 15, ALU.mult)
            tt(17, 14, are, ALU.mult)
            tt(18, 13, aim, ALU.mult)
            tt(17, 17, 18, ALU.subtract)
            tt(17, 17, 15, ALU.mult)
            dve.wait_ge(s_ssm.sem, 64)
            wide = lambda i: st[:, i, :].unsqueeze(2).to_broadcast([P, NT, 32])
            t1 = work[0][2].rearrange("p (a b) -> p a b", a=NT)
            link(dve.tensor_tensor(t1, c_raw[1], wide(17), ALU.mult))
            link(dve.tensor_tensor(c_out[0], c_raw[0], wide(16), ALU.mult))
            link(dve.tensor_tensor(c_out[0], c_out[0], t1, ALU.subtract))
            link(dve.tensor_tensor(t1, c_raw[1], wide(16), ALU.mult))
            link(dve.tensor_tensor(c_out[1], c_raw[0], wide(17), ALU.mult))
            s_cw.on(dve.scalar_tensor_tensor(c_out[1], c_out[1], -1.0, t1, ALU.mult, ALU.subtract))
            settle(dve, s_cw)

            norm("mix", hT)

            def phase(j):
                c, s, t1, t2, t3, t4 = work[j % 2]
                if j >= 2:
                    dve.wait_ge(s_y.sem, j - 1)
                link(dve.tensor_scalar(t1, iota, st[:, 10, j:j + 1], MAGIC, ALU.mult, ALU.add))
                link(dve.tensor_scalar(t1, t1, MAGIC, None, ALU.subtract))
                link(dve.scalar_tensor_tensor(t2, iota, st[:, 11, j:j + 1], t1, ALU.mult, ALU.subtract))
                link(dve.scalar_tensor_tensor(t2, iota, st[:, 12, j:j + 1], t2, ALU.mult, ALU.add))
                s_ph.on(dve.tensor_scalar(t2, t2, 0.5, -0.5, ALU.min, ALU.max))

            phase(0)
            phase(1)
            for j in range(NT):
                c, s, t1, t2, t3, t4 = work[j % 2]
                re, im = att[2 * (j % 2)], att[2 * (j % 2) + 1]
                dve.wait_ge(s_tab.sem, 2 * (j + 1))
                dve.wait_ge(s_bu.sem, j + 1)
                s_rot.on(dve.tensor_tensor(t1, re[:, :], c, ALU.mult))
                s_rot.on(dve.tensor_tensor(t2, im[:, :], s, ALU.mult))
                s_rot.on(dve.tensor_tensor(t3, im[:, :], c, ALU.mult))
                s_rot.on(dve.tensor_tensor(t4, re[:, :], s, ALU.mult))
                mag = st[:, 3, j:j + 1].to_broadcast([P, T])
                dve.wait_ge(s_w.sem, 2 * j + 1)
                s_z.on(dve.tensor_tensor_scan(t1, mag, t1, 0.0, ALU.mult, ALU.add))
                dve.wait_ge(s_w.sem, 2 * j + 2)
                s_z.on(dve.tensor_tensor_scan(t3, mag, t3, 0.0, ALU.mult, ALU.add))
                if j >= 4 and j % 4 == 0:
                    i = j // 4 - 1
                    dve.wait_ge(s_y.sem, j)
                    s_yv.on(dve.scalar_tensor_tensor(uT[:, i, :], uT[:, i, :], vec("skip", i), att[4 + i % 2][:, :], ALU.mult, ALU.add))
                if j >= 1 and j + 1 < NT:
                    phase(j + 1)
            dve.wait_ge(s_y.sem, NT)
            s_yv.on(dve.scalar_tensor_tensor(uT[:, 3, :], uT[:, 3, :], vec("skip", 3), att[5][:, :], ALU.mult, ALU.add))

            def dil_logits(h):
                for g in range(PATTERNS):
                    n = PATTERNS * h + g
                    dve.wait_ge(s_S.sem, n + 1)
                    dve.wait_ge(s_bias[g].sem, 16 * (h + 1))
                    if h >= 1:
                        dve.wait_ge(s_T.sem, PATTERNS * (h - 1) + g + 1)
                    for b in range(TB):
                        bank, col = KPLACE[TB - 1 - b]
                        w = DIL[g][b][1]
                        end = 2 * P if g == 0 else T
                        s_lg.on(dve.tensor_tensor_reduce(
                            out=logits[:, DOFF[g][b]:DOFF[g][b] + w], in0=att[bank][:, col:col + w],
                            in1=biases[:, g, end - w:end], scale=1.0, scalar=TAKEN, op0=ALU.add, op1=ALU.max,
                            accum_out=am[:, 4 * g + b:4 * g + b + 1]))
                settle(dve, s_lg)
                link(dve.tensor_tensor(am[:, 0:4], am[:, 0:4], am[:, 4:8], ALU.max))
                link(dve.tensor_tensor(am[:, 0:4], am[:, 0:4], am[:, 8:12], ALU.max))
                s_neg.on(dve.tensor_scalar(am[:, 12:16], am[:, 0:4], -1.0, None, ALU.mult))
                dve.wait_ge(s_exp.sem, TB * PATTERNS * (h + 1))
                link(dve.tensor_tensor(am[:, 16:20], am[:, 16:20], am[:, 20:24], ALU.add))
                link(dve.tensor_tensor(am[:, 16:20], am[:, 16:20], am[:, 24:28], ALU.add))
                s_rinv.on(dve.reciprocal(am[:, 28:32], am[:, 16:20]))

            for h in range(SLOTS_H):
                dil_logits(h)
                for g in range(PATTERNS):
                    n = PATTERNS * h + g
                    dve.wait_ge(s_T.sem, n + 1)
                    if g:
                        s_TV.on(dve.tensor_copy(turned[:, n % 2, 512:1024], att[4][:, :]))
                        s_TV.on(dve.tensor_copy(turned[:, n % 2, 1024:1280], att[5][:, 0:256]))
                    else:
                        s_TV.on(dve.tensor_copy(turned[:, n % 2, 512:768], att[4][:, 0:256]))
                        s_am2.on(dve.tensor_copy(turned[:, n % 2, 896:1024], att[4][:, 384:512]))
                        settle(dve, s_am2)
                        s_TV.on(dve.tensor_copy(turned[:, n % 2, 1024:1280], att[5][:, 0:256]))
                r = slice(64 * (h % 2), 64 * (h % 2) + 64)
                bank = G.whole(dve, f"att{h}")
                G.empty(dve.tensor_copy(yatt[r, h // 2, :], bank[r, :]), f"att{h}")

            def cross_max(h):
                o = 32 + 0
                dve.wait_ge(s_xS.sem, h + 1)
                mx = am[:, 52:56]
                for i in range(2):
                    ins = dve.tensor_reduce(mx[:, 2 * i:2 * i + 2], att[i][:, :].rearrange("p (a b) -> p a b", a=2), AX.X, ALU.max)
                    link(ins)
                s_xneg.on(dve.tensor_scalar(am[:, 36 + 4 * (h % 2):40 + 4 * (h % 2)], mx, -(XD ** -0.5), None, ALU.mult))

            def cross_rinv(h):
                dve.wait_ge(s_xexp.sem, TB * (h + 1))
                o = 60 - 4 * (h % 2)
                s_xrinv.on(dve.reciprocal(am[:, o:o + 4], am[:, 44 + 4 * (h % 2):48 + 4 * (h % 2)]))

            cross_max(0)
            cross_rinv(0)
            for h in range(XH):
                if h + 1 < XH:
                    cross_max(h + 1)
                dve.wait_ge(s_xT.sem, h + 1)
                if h >= 2:
                    G.whole(dve, f"xo{h - 2}")
                s_xTV.on(dve.tensor_copy(turned[:, h % 2, T:2 * T], att[4][:, :]))
                if h + 1 < XH:
                    cross_rinv(h + 1)
                bank = G.whole(dve, f"xo{h}")
                G.empty(dve.tensor_copy(xq[:, h, :], bank[:, :]), f"xo{h}")
            for d in range(KD):
                bank = G.whole(dve, f"gla{d}")
                G.moved(dve, f"glb{d}")
                G.empty(dve.tensor_tensor(merged[:, d, :], bank[:, :], gates[:, 1, :], ALU.mult), f"gla{d}")
                settle(dve, s_v)
                link(dve.tensor_tensor(merged[:, d, :], merged[:, d, :], gates[:, 0, :], ALU.mult))
                for i, n in ((2, "up"), (3, "xup")):
                    bank = G.whole(dve, f"{n}{d}")
                    G.moved(dve, f"g{i - 1}{d}")
                    G.empty(dve.tensor_tensor(parts[:, i - 2, :], bank[:, :], gates[:, i, :], ALU.mult), f"{n}{d}")
                    settle(dve, s_v)
                    ins = dve.tensor_tensor(merged[:, d, :], merged[:, d, :], parts[:, i - 2, :], ALU.add)
                    if i == 2:
                        link(ins)
                    else:
                        s_merged.on(ins)
            for d in range(KD):
                bank = G.whole(dve, f"o{d}")
                G.empty(dve.tensor_tensor(xT[:, d, :], bank[:, :], xT[:, d, :], ALU.add), f"o{d}")
            settle(dve, s_v)
            norm("ffn2", hT)
            ffn("f2")
            settle(dve, s_v)
            norm("fin2", hT)


def tile_k(w):
    k, c = w.shape
    return w.reshape(k // P, P, c).transpose(1, 0, 2).reshape(P, -1)


def columns():
    widths = [("q", 512), ("ckv", 128), ("kr", 16), ("iq", 256), ("ik", 64), ("iw", 4), ("za", 512), ("sbq", 512),
              ("sbk", 512), ("sbv", 512), ("zb", 512), ("mlq", 512), ("mlk", 512), ("mlv", 512), ("mi", 4), ("mf", 4),
              ("mlo", 512), ("zc", 512), ("merge", 3072)]
    out, at = {}, 0
    for n, w in widths:
        out[n] = (at, at + w)
        at += w
    return out


def lay_out_first(I):
    C = columns()
    A = {k: [] for k in ("wide", "misc", "merge", "branch", "out", "vec", "wuk", "wuv")}
    for l in range(DEPTH):
        def c(n):
            return I["w_in"][l][:, C[n][0]:C[n][1]]
        wide = [tile_k(np.concatenate([c("iq"), c("ik"), c("ik"), c("ckv")], 1))]
        wide += [tile_k(c(n)) for n in WIDE[1:]]
        A["wide"].append(np.stack(wide))
        m = np.zeros((D, P), np.float32)
        m[:, 0:16], m[:, 32:36], m[:, 64:68], m[:, 96:100] = c("kr"), c("mi"), c("mf"), c("iw")
        A["misc"].append(tile_k(m))
        mg = c("merge").reshape(D, 3, KD, P)
        A["merge"].append(np.stack([tile_k(mg[:, :, d].reshape(D, 3 * P)) for d in range(KD)]))
        br = I["w_branch"][l].reshape(3, 4, P, KD // 2, 2 * P)
        A["branch"].append(br.transpose(3, 2, 0, 1, 4).reshape(KD // 2, P, -1))
        A["out"].append(np.stack([tile_k(I["w_out"][l][:, i * T:(i + 1) * T]) for i in range(2)]))
        v = np.zeros((P, N_VEC), np.float32)
        v[:, 0:8] = I["norm_w"][l].reshape(KD, P).T
        v[:, 8] = I["dsa_kv_norm_w"][l]
        v[:, 9:41] = I["ml_conv_w"][l].reshape(4, 8, P).transpose(2, 0, 1).reshape(P, 32)
        v[:, 41:45] = I["ml_norm_w"][l].reshape(4, P).T
        v[32:36, 45] = I["ml_i_bias"][l]
        v[64:68, 46] = I["ml_f_bias"][l]
        A["vec"].append(v)
        uk = np.zeros((P, HEADS, HD), np.float32)
        uk[:, :, ROPE:] = I["w_dsa_uk"][l]
        A["wuk"].append(uk.reshape(P, -1))
        A["wuv"].append(I["w_dsa_uv"][l].reshape(P, -1))
    return {k: np.ascontiguousarray(np.stack(v)) for k, v in A.items()}


def constants():
    out = np.zeros((P, N_CONST), np.float32)

    def put(n, v):
        a, b = CONST[n]
        out[:v.shape[0], a:b] = v
    put("ident", np.eye(P))
    R = np.zeros((P, P))
    for h in (0, 64):
        for i in range(8):
            R[h + i, h + i + 8] = -1
            R[h + i + 8, h + i] = 1
    put("rot", R.T)
    E = np.zeros((ROPE, P))
    for h in (0, 64):
        E[np.arange(16), h + np.arange(16)] = 1
    put("dup", E)
    i = np.arange(P)
    put("tri", -(i[:, None] >= i[None, :]).astype(float))
    put("negones", -np.ones((P, P)))
    put("ones", np.ones((P, P)))
    put("cmask", np.where(i[None, :] <= i[:, None], 0, NEG))
    f = np.float32
    inv = f(500000.0) ** (-np.arange(0, ROPE, 2, dtype=f) / f(ROPE))
    ang = np.arange(T, dtype=f)[:, None] * inv[None]
    cos, sin = np.ones((P, T), f), np.zeros((P, T), f)
    for h in (0, 8, 64, 72):
        cos[h:h + 8] = np.cos(ang).T
        sin[h:h + 8] = np.sin(ang).T
    put("cos", cos)
    put("sin", sin)
    s = np.zeros((ML_H, ML_H, P))
    s[np.arange(ML_H), np.arange(ML_H)] = 1
    put("sel", s.reshape(ML_H, -1))
    return out


def t5_buckets(dist):
    dist = np.asarray(dist, np.int32)
    exact = 16
    safe = np.maximum(dist, 1).astype(np.float32)
    large = exact + (np.log(safe / exact) / np.log(2048 / exact) * (32 - exact)).astype(np.int32)
    return np.where(dist < exact, dist, np.minimum(large, 31)).astype(np.int32)


def onehot_rows():
    out = np.zeros((33, PATTERNS, TOEP), np.float32)
    i = np.arange(TOEP)
    for g, (top, step, win) in enumerate([(255, 1, 128), (511, 4, 512), (511, 16, 2048)]):
        d = top - i
        ok = (d >= 0) & (d % step == 0) & (d <= win)
        out[t5_buckets(np.where(ok, d, 0))[ok], g, i[ok]] = 1
        out[32, g, ~ok] = NEG
    return out.reshape(33, -1)


def lay_out_second(I):
    A = {}
    c = np.zeros((P, N_CONST2), np.float32)
    c[:, 0:P], c[:, P:2 * P], c[:, 2 * P:] = np.eye(P), 1, np.arange(T)
    A["const2"] = c
    A["onehot"] = onehot_rows()
    A["table"] = np.concatenate([I["rel_table_2"], np.ones((1, PATTERNS * SLOTS_H), np.float32)])
    v = np.zeros((P, N_VEC2), np.float32)

    def put(n, x):
        a, b = VEC2[n]
        v[:, a:b] = x
    for n, k in (("fin1", "final_norm_w"), ("ffn1", "ffn1_norm_2"), ("mix", "mix_norm_2"), ("ffn2", "ffn2_norm_2"),
                 ("fin2", "final_norm_2"), ("mem", "mem_norm_2")):
        put(n, I[k].reshape(KD, P).T)
    put("skip", I["ssm_d_2"].reshape(4, P).T)
    put("are", I["ssm_a_re_2"].reshape(NT, P).T)
    put("aim", I["ssm_a_im_2"].reshape(NT, P).T)
    put("ldt", np.repeat(I["ssm_log_dt_2"].reshape(SG), SS).reshape(NT, P).T)
    A["vec2"] = v
    A["mem"] = np.ascontiguousarray(I["mem_2"][0].T.reshape(KD, P, MEM).transpose(1, 0, 2))
    for n in ("re", "im"):
        b, cc = I[f"ssm_b_{n}_2"][0], I[f"ssm_c_{n}_2"][0]
        B, C = np.zeros((P, 4, P), np.float32), np.zeros((P, NT, 32), np.float32)
        for j in range(NT):
            for g in range(2):
                r = 32 * (j % 4) + 16 * g
                B[r:r + 16, j // 4, 64 * g:64 * g + 64] = b[2 * j + g].T
                C[64 * g:64 * g + 64, j, 16 * g:16 * g + 16] = cc[2 * j + g].T
        A["b" + n], A["c" + n] = B.reshape(P, -1), C
    W = np.zeros((N_STREAM, P, CHUNK), np.float32)

    def w(n, x):
        t = tile_k(x)
        chunk, o = STREAM[n]
        W[chunk, :, o:o + t.shape[1]] = t
    for n, a, b in (("f1", "ffn1_w_in_2", "ffn1_w_down_2"), ("f2", "ffn2_w_in_2", "ffn2_w_down_2")):
        for i in range(KF):
            w(f"{n}a{i}", I[a][0][:, i * P:(i + 1) * P])
            w(f"{n}b{i}", I[a][0][:, FF + i * P:FF + (i + 1) * P])
        for d in range(KD):
            w(f"{n}d{d}", I[b][0][:, d * P:(d + 1) * P])
    kv, win = I["xattn_w_kv_2"][0], I["w_in_2"][0]
    kv_w = XH * XD
    q0, xq0 = T, T + 3 * AW
    for i in range(4):
        w(f"mk{i}", kv[:, i * P:(i + 1) * P])
        w(f"mv{i}", kv[:, kv_w + i * P:kv_w + (i + 1) * P])
        w(f"u{i}", win[:, i * P:(i + 1) * P])
        w(f"xq{i}", win[:, xq0 + i * P:xq0 + (i + 1) * P])
    for i in range(6):
        w(f"q{i}", win[:, q0 + i * P:q0 + (i + 1) * P])
        w(f"k{i}", win[:, q0 + AW + i * P:q0 + AW + (i + 1) * P])
    for i in range(2):
        w(f"v{i}", win[:, q0 + 2 * AW + i * 3 * P:q0 + 2 * AW + (i + 1) * 3 * P])
    g0 = xq0 + kv_w
    glu = I["ssm_w_glu_2"][0]
    for d in range(KD):
        cols = slice(d * P, (d + 1) * P)
        for k in range(3):
            w(f"g{k}{d}", win[:, g0 + k * D + d * P:g0 + k * D + (d + 1) * P])
        w(f"gla{d}", glu[:, cols])
        w(f"glb{d}", glu[:, D + d * P:D + (d + 1) * P])
        w(f"up{d}", I["attn_w_up_2"][0][:, cols])
        w(f"xup{d}", I["xattn_w_up_2"][0][:, cols])
        w(f"o{d}", I["w_out_2"][0][:, cols])
    A["stream"] = W
    return A


def both_blocks(nc, A, scratch, out_dram):
    with ExitStack() as stack:
        xT = stack.enter_context(nc.sbuf_tensor("xT", [P, KD, T], F32))
        s_load = Signal(stack.enter_context(nc.semaphore("load")))
        s_eps = Signal(stack.enter_context(nc.semaphore("eps_set")))
        with ExitStack() as first:
            consts = first.enter_context(nc.sbuf_tensor("consts", [P, N_CONST], F32))
            eps = first.enter_context(nc.sbuf_tensor("eps", [P, 1], F32))
            with nc.Block() as block:

                @block.sync
                def _(sp):
                    s_load.on(sp.dma_start(xT[:], A["x"]), 16)
                    s_load.on(sp.dma_start(consts[:], A["const"]), 16)
                    sp.wait_ge(s_load.sem, 32)

                @block.vector
                def _(dve):
                    s_eps.on(dve.memset(eps[:], EPS))
                    settle(dve, s_eps)

            hybrid_layers(nc, first, xT, A, consts, {"eps": eps[:, 0:1]})
        second_block(nc, stack, xT, A, scratch, out_dram)


def kernel(**inputs):
    from concourse import bacc
    from concourse.bass_utils import run_bass_kernel_spmd

    I = {n: np.asarray(a) for n, a in inputs.items()}
    A = lay_out_first(I)
    A.update(lay_out_second(I))
    A["const"] = constants()
    A["x"] = np.ascontiguousarray(I["x"][0].T.reshape(KD, P, T).transpose(1, 0, 2))

    nc = bacc.Bacc("TRN2", target_bir_lowering=False, num_devices=1)
    aps = {n: nc.dram_tensor("in_" + n, a.shape, F32, kind="ExternalInput").ap() for n, a in A.items()}
    out = nc.dram_tensor("out", (P, KD, T), F32, kind="ExternalOutput").ap()
    scratch = nc.dram_tensor("bias_rows", (PATTERNS * SLOTS_H, P, TOEP), F32, kind="Internal").ap()
    both_blocks(nc, aps, scratch, out)
    r = run_bass_kernel_spmd(nc, [{"in_" + n: a for n, a in A.items()}], core_ids=[0])
    y = r.results[0]["out"]
    return np.ascontiguousarray(y.transpose(1, 0, 2).reshape(D, T).T).reshape(1, T, D)
```

```python
from contextlib import ExitStack

import numpy as np

import concourse.bass as bass
from concourse import mybir

F32 = mybir.dt.float32
F32R = mybir.dt.float32r
ALU = mybir.AluOpType
ACT = mybir.ActivationFunctionType
AX = mybir.AxisListType

P = 128
T = 512
D = 1024
KD = D // P
TB = T // P
DEPTH = 2
EPS = 1e-6
HEADS, HD = 8, 64
ML_H, ML_D = 4, 128
IDX_H = 4
TOPK = 128
ROPE = 16
NEG = -1e30
DROPPED = -2e38
TAKEN = -3e38
ALIVE = -2.5e38

WQ = [P * (b + 1) for b in range(TB)]
OQ = [sum(WQ[:b]) for b in range(TB)]
WK = [T - P * s for s in range(TB)]
CAUSAL = sum(WQ)
KPLACE = [(0, 0), (1, 0), (2, 0), (1, 384)]
KOFF = [0, 512, 1024, 896]
BANKS = [(0, 512, 0), (1, 512, 512), (2, 256, 1024)]

UNIT = 1024
RAW, RAW2, HIGH = 5, 4, 3
HALF = 256


class Signal:

    def __init__(self, sem):
        self.sem, self.count = sem, 0

    def on(self, ins, by=1):
        ins.then_inc(self.sem, by)
        self.count += by
        return self.count


def settle(eng, signal):
    eng.wait_ge(signal.sem, signal.count)


class Weights:

    def __init__(self, tiles, groups, tile_of, slots, raw, high, low, s_load, s_used, s_high, s_low):
        self.G, self.tile_of = groups, tile_of
        self.slots, self.raw, self.high, self.low = slots, raw, high, low
        self.s_load, self.s_used, self.s_high, self.s_low = s_load, s_used, s_high, s_low
        self.place, self.n_chunks = place_tiles(tiles)
        last = {}
        for result, _ in groups.names:
            if result in tile_of:
                pos, n, width = self.place[tile_of[result]]
                for k in range(n):
                    last[(pos + k * width) // UNIT] = (result, k)
        self.free, self.inside = [], set()
        for c in range(self.n_chunks):
            result, k = last[c]
            at = groups.at[result]
            if k == self.place[tile_of[result]][1] - 1:
                self.free.append((groups.done, at + 1, at))
            else:
                self.inside.add((result, k))
                self.free.append((s_used, len(self.inside), at))
        self.n_high = self.n_low = self.n_seen = 0

    def used(self, eng, c):
        signal, value, _ = self.free[c]
        eng.wait_ge(signal.sem, value)

    def load(self, sp, c, src):
        if c >= self.slots:
            self.used(sp, c - self.slots)
        self.s_load[c % self.slots].on(sp.dma_start(self.raw[:, c % self.slots, :], src), 16)

    def due(self, c, slots, result):
        if c >= self.n_chunks:
            return False
        if c < slots or self.free[c - slots][2] < self.G.at[result]:
            return True
        if self.free[c - slots][0] is self.s_used and self.free[c - slots][2] == self.G.at[result]:
            return True
        return False

    def round(self, act, result):
        while self.due(self.n_high, HIGH, result):
            c = self.n_high
            act.wait_ge(self.s_load[c % self.slots].sem, 16 * (c // self.slots + 1))
            if c >= HIGH:
                self.used(act, c - HIGH)
            self.s_high.on(act.activation(self.high[:, c % HIGH, :], self.raw[:, c % self.slots, :], ACT.Copy))
            self.n_high += 1

    def rest(self, pool, result):
        while self.due(self.n_low, HIGH, result):
            c = self.n_low
            pool.wait_ge(self.s_high.sem, c + 1)
            self.s_low.on(pool.tensor_tensor(self.low[:, c % self.slots, :], self.raw[:, c % self.slots, :],
                                             self.high[:, c % HIGH, :], ALU.subtract))
            self.n_low += 1

    def parts(self, pe, result, k):
        pos, n, width = self.place[self.tile_of[result]]
        c, off = divmod(pos + k * width, UNIT)
        if c >= self.n_seen:
            pe.wait_ge(self.s_low.sem, c + 1)
            self.n_seen = c + 1
        return self.high[:, c % HIGH, off:off + width], self.low[:, c % self.slots, off:off + width]

    def product(self, pe, result, out, xs, tokens=False, ready=None):
        n = len(xs)
        for k, (xh, xl) in enumerate(xs):
            if ready is not None:
                ready(k)
            wh, wl = self.parts(pe, result, k)
            for i, (w, x) in enumerate(((wh, xh), (wl, xh), (wh, xl))):
                a, b = (x, w) if tokens else (w, x)
                mm = pe.matmul(out, a, b, start=(k == 0 and i == 0), stop=(k == n - 1 and i == 2))
            if (result, k) in self.inside:
                self.s_used.on(mm)
        self.G.close(mm)


def place_tiles(tiles):
    place, pos = {}, 0
    for name, n, width in tiles:
        assert pos % width == 0
        place[name] = (pos, n, width)
        pos += n * width
    return place, -(-pos // UNIT)


def layer_tiles():
    t = [(f"idx{i}", KD, P) for i in range(4)] + [("misc", KD, P)]
    t += [(f"{n}{i}", KD, P) for n in ("q", "za", "zb", "sbq", "sbk") for i in range(4)]
    t += [(f"sbv_half{c}", KD, HALF) for c in range(2)]
    t += [(f"{n}{i}", KD, P) for n in ("mlq", "mlk") for i in range(4)]
    t += [(f"mlv_half{c}", KD, HALF) for c in range(2)]
    t += [(f"{n}{i}", KD, P) for n in ("mlo", "zc") for i in range(4)]
    for d in range(KD):
        t += [(f"gate{d}0", KD, P), (f"proj{d}0", 4, P)]
    for d in range(KD):
        for k in (1, 2):
            t += [(f"gate{d}{k}", KD, P), (f"proj{d}{k}", 4, P)]
    return t + [(f"out{d}", KD, P) for d in range(KD)]


def layer_tile_of():
    of = {n: n for n, _, _ in layer_tiles()}
    for n in ("sbv", "mlv"):
        for i in range(2 * TB):
            of[f"{n}{i}"] = f"{n}_half{i // TB}"
    return of


def layer_groups():
    g = [("ms", "a")]
    g += [(f"idx{i}", "a") for i in range(4)] + [("misc", "a"), ("q0", "a")]
    g += [(f"ridx{i}", "v") for i in range(3)]
    g += [(f"q{i}", "a") for i in range(1, 4)] + [("iwt", "v")]
    g += [(f"sc{b}{h}", "a") for b in range(1, TB) for h in range(IDX_H)]
    g += [(f"rq{i}", "v") for i in range(4)] + [("rkr", "v"), ("cms", "a")]
    g += [(f"za{i}", "a") for i in range(4)]
    g += [("at", "v")]
    g += [(f"kk{i}", "a") for i in range(4)] + [(f"vv{i}", "a") for i in range(TB)]
    g += [(f"{n}{i}", "a") for n in ("zb", "sbq", "sbk") for i in range(4)]
    g += [(f"sbv{i}", "a") for i in range(2 * TB)]
    for h in range(HEADS):
        g += [(("mlq" if h < 4 else "mlk") + str(h % 4), "a"), (f"dsa{h}", "v")]
    for h in range(HEADS):
        g += [(f"mlv{h}", "a")]
        if h >= 1:
            g += [(f"sb{h - 1}", "v")]
    g += [(f"sb{HEADS - 1}", "v")]
    g += [(f"mlo{i}", "a") for i in range(4)] + [(f"zc{i}", "a") for i in range(4)]
    for h in range(ML_H):
        g += [(f"mu{h}", "a"), (f"mm{h}", "a"), (f"gate{2 * h}0", "a"), (f"proj{2 * h}0", "v")]
        g += [(f"den{h}", "a"), (f"num{h}", "v"), (f"gate{2 * h + 1}0", "a"), (f"mean{h}", "v"), (f"proj{2 * h + 1}0", "v")]
        g += [(f"var{h}", "a")]
    for d in range(KD):
        for k in (1, 2):
            g += [(f"gate{d}{k}", "a"), (f"proj{d}{k}", "v")]
    g += [(f"out{d}", "v") for d in range(KD)]
    return g


class Groups:

    def __init__(self, names, banks, done, freed):
        self.names, self.banks, self.done, self.freed = names, banks, done, freed
        self.at = {n: i for i, (n, _) in enumerate(names)}
        assert len(self.at) == len(names)
        self.order, seen = {}, {"a": 0, "v": 0}
        for n, e in names:
            seen[e] += 1
            self.order[n] = seen[e]
        self.issued = 0
        self.emptied = {"a": 0, "v": 0}

    def open(self, pe, name):
        i = self.at[name]
        assert i == self.issued, (name, self.names[self.issued])
        n = len(self.banks)
        if i >= n:
            old, eng = self.names[i - n]
            pe.wait_ge(self.freed[eng].sem, self.order[old])
        return self.banks[i % n]

    def close(self, ins):
        self.issued += 1
        self.done.on(ins)

    def whole(self, eng, name):
        eng.wait_ge(self.done.sem, self.at[name] + 1)
        return self.banks[self.at[name] % len(self.banks)]

    def empty(self, ins, name):
        e = self.names[self.at[name]][1]
        self.emptied[e] += 1
        assert self.emptied[e] == self.order[name], name
        self.freed[e].on(ins)

    def moved(self, eng, name):
        eng.wait_ge(self.freed[self.names[self.at[name]][1]].sem, self.order[name])


CONST = {}
_c = 0
for _n, _w in (("ident", P), ("rot", P), ("dup", P), ("tri", P), ("negones", P), ("ones", P),
               ("cmask", P), ("cos", T), ("sin", T), ("sel", ML_H * P)):
    CONST[_n] = (_c, _c + _w)
    _c += _w
N_CONST = _c

VEC = {"norm": (0, 8), "kvnorm": (8, 9), "conv": (9, 41), "mlnorm": (41, 45), "ibias": (45, 46), "fbias": (46, 47)}
N_VEC = 47


def hybrid_layers(nc, stack, xT, A, consts, mark):
    def sb(name, shape, dt=F32):
        return stack.enter_context(nc.sbuf_tensor(name, shape, dt))

    every = []

    def here():
        return -(-nc.sbuf_base // 32) * 32

    def rounded(name, shape, at):
        return nc.alloc_sbuf_tensor_at(name, shape, F32R, offset=at)

    def sem(name):
        every.append(Signal(stack.enter_context(nc.semaphore(name))))
        return every[-1]

    def c(name):
        a, b = CONST[name]
        return consts[:, a:b]

    ident, rot, dup, tri, negones, ones, cmask, cosT, sinT, sel = (
        c(n) for n in ("ident", "rot", "dup", "tri", "negones", "ones", "cmask", "cos", "sin", "sel"))

    hT_at, hT = here(), sb("hT", [P, KD, T])
    raw_at, ring = here(), sb("ring", [P, RAW, UNIT])
    low = rounded("weight_low", [P, RAW, UNIT], raw_at)
    high = stack.enter_context(nc.sbuf_tensor("weight_high", [P, HIGH, UNIT], F32R))
    h_low = rounded("h_low", [P, KD, T], hT_at)
    h_high = stack.enter_context(nc.sbuf_tensor("h_high", [P, KD, T], F32R))
    h_parts = [(h_high[:, k, :], h_low[:, k, :]) for k in range(KD)]
    vecs = sb("vecs", [P, N_VEC])
    dq = sb("dq", [P, 4, T])
    dk_at, dk = here(), sb("dk", [P, 4, T])
    dv_at, dv = here(), sb("dv", [P, TB, T])
    sq_at, sq_ = here(), sb("sq_", [P, 4, T])
    sk_at, sk = here(), sb("sk", [P, 4, T])
    sv_at, sv = here(), sb("sv", [P, TB, T])
    za_at, za = here(), sb("za", [P, 4, T])
    zb_at, zb = here(), sb("zb", [P, 4, T])
    idx = sb("idx", [P, 4, T])
    misc_at, misc = here(), sb("misc", [P, T])
    mix_at, raw = here(), sb("raw", [P, 8, T + 4])
    probs_at, probs = here(), sb("probs", [P, 2, CAUSAL])
    turned = sb("turned", [P, 2, CAUSAL])
    bias_at, bias = here(), sb("bias", [P, CAUSAL])
    rstd = sb("rstd", [P, T])
    small = sb("small", [P, 64])
    iwt = sb("iwt", [P, TB, IDX_H])
    acol = sb("acol", [P, TB, ML_H])
    top8 = sb("top8", [P, TB, 8])

    flat = raw[:].rearrange("p a b -> p (a b)")
    score = flat[:, 0:CAUSAL]
    relu = flat[:, CAUSAL:CAUSAL + 2 * T].rearrange("p (a b) -> p a b", a=2)
    wuk = flat[:, CAUSAL + 2 * T:CAUSAL + 3 * T]
    wuv = flat[:, CAUSAL + 3 * T:CAUSAL + 3 * T + T]
    mixed = flat[:, 0:KD * T].rearrange("p (a b) -> p a b", a=KD)
    soft_low, soft_high = rounded("soft_low", [P, 2, CAUSAL], probs_at), rounded("soft_high", [P, CAUSAL], bias_at)
    signs = rounded("signs", [P, 2 * P], misc_at)
    mlo, zc = sq_, sk
    z_low = [rounded(f"z_low{i}", [P, 4, T], at) for i, at in enumerate((za_at, zb_at, sk_at))]
    z_high = [rounded(f"z_high{i}", [P, 4, T], at) for i, at in enumerate((sv_at, dk_at, dv_at))]
    mix_low = rounded("mix_low", [P, KD, T], mix_at)
    mix_high2 = [rounded(f"mix_high{i}", [P, 4, T], at) for i, at in enumerate((sq_at, sv_at))]
    mix_high = [mix_high2[k // 4][:, k % 4, :] for k in range(KD)]
    mq, mk, mv = dq, dk, dv
    ckv = idx[:, 3, :]
    gate = probs[:].rearrange("p a b -> p (a b)")[:, 0:3 * T].rearrange("p (a b) -> p a b", a=3)
    part = turned[:].rearrange("p a b -> p (a b)")[:, 0:2 * T].rearrange("p (a b) -> p a b", a=2)
    hml, dn, hsq, em = bias[:, 0:T], bias[:, T:2 * T], misc[:], idx[:, 3, :]
    csq = dk[:, 0, :]
    tflat = turned[:].rearrange("p a b -> p (a b)")
    g_i, g_f, g_sum = (tflat[0:ML_H, i * T:(i + 1) * T] for i in range(3))
    g_mu, g_m, g_a = (idx[0:ML_H, i, :] for i in range(3))

    proj = [stack.enter_context(nc.psum_tensor(f"proj{i}", [P, T], F32)) for i in range(2)]
    att = [stack.enter_context(nc.psum_tensor(f"att{i}", [P, T], F32)) for i in range(6)]

    s_vec, s_lat = sem("s_vec"), sem("s_lat")
    s_load = [sem(f"s_load{i}") for i in range(RAW)]
    s_used, s_high, s_low = sem("s_chunk_used"), sem("s_weight_high"), sem("s_weight_low")
    s_sum, s_signs, s_sh, s_sl = sem("s_squares_summed"), sem("s_signs"), sem("s_soft_high"), sem("s_soft_low")
    s_hh, s_hl, s_zh, s_zl, s_mh, s_ml = (sem(n) for n in ("s_h_high", "s_h_low", "s_z_high", "s_z_low", "s_mix_high", "s_mix_low"))
    s_done, s_a, s_v = sem("s_done"), sem("s_act_moved"), sem("s_dve_moved")
    s_sq, s_h, s_ac, s_vc = sem("s_square"), sem("s_h"), sem("s_act"), sem("s_dve")
    s_ridx, s_rq, s_ckv, s_scused = sem("s_ridx"), sem("s_rq"), sem("s_ckv"), sem("s_scused")
    s_ln, s_gates, s_masked = sem("s_ln"), sem("s_gates"), sem("s_masked")
    s_csq, s_ir, s_rkr, s_bias = sem("s_csq"), sem("s_ir"), sem("s_rkr"), sem("s_bias")
    s_S, s_logit, s_exp, s_rinv, s_scaled, s_T, s_TA, s_TV = (sem(n) for n in (
        "s_S", "s_logit", "s_exp", "s_rinv", "s_scaled", "s_T", "s_TA", "s_TV"))
    s_Z, s_soft, s_sp, s_spm, s_tri, s_a_exp, s_am = (sem(n) for n in (
        "s_Z", "s_soft", "s_sp", "s_spm", "s_tri", "s_aexp", "s_am"))
    s_conv, s_silu, s_K, s_w8, s_w8m, s_ws, s_sq2, s_mlz, s_pad = (sem(n) for n in (
        "s_conv", "s_silu", "s_K", "s_w8", "s_w8m", "s_ws", "s_sq2", "s_mlz", "s_pad"))
    s_mix = sem("s_mix")

    G = Groups(layer_groups(), proj, s_done, {"a": s_a, "v": s_v})

    W = Weights(layer_tiles(), G, layer_tile_of(), RAW, ring, high, low, s_load, s_used, s_high, s_low)

    with nc.Fori(0, DEPTH) as layer:
        with nc.Block() as block:

            @block.sync
            def _(sp):
                s_vec.on(sp.dma_start(vecs[:], A["vec"][layer]), 16)
                for c in range(W.n_chunks):
                    W.load(sp, c, A["weights"][layer, c])
                    if c == RAW - 1:
                        s_lat.on(sp.dma_start(wuk, A["wuk"][layer]), 16)
                        s_lat.on(sp.dma_start(wuv, A["wuv"][layer]), 16)

            @block.tensor
            def _(pe):
                def dense(name):
                    out = G.open(pe, name)
                    ready = (lambda k: pe.wait_ge(s_hl.sem, k + 1)) if name == "idx0" else None
                    W.product(pe, name, out[:, :], h_parts, ready=ready)

                def dense_tokens(n, i):
                    b = slice((i % TB) * P, (i % TB + 1) * P)
                    out = G.open(pe, f"{n}{i}")
                    W.product(pe, f"{n}{i}", out[:, 0:HALF], [(xh[:, b], xl[:, b]) for xh, xl in h_parts], tokens=True)

                out = G.open(pe, "ms")
                pe.wait_ge(s_sum.sem, 1)
                G.close(pe.matmul(out[:, :], ones, rstd[:], start=True, stop=True))
                for i in range(4):
                    dense(f"idx{i}")
                dense("misc")
                dense("q0")
                for i in range(3):
                    out = G.open(pe, f"ridx{i}")
                    G.moved(pe, f"idx{i}")
                    G.close(pe.matmul(out[:, :], rot, idx[:, i, :], start=True, stop=True))
                for i in range(1, 4):
                    dense(f"q{i}")
                out = G.open(pe, "iwt")
                for b in range(TB):
                    tr = pe.transpose(out[:, b * IDX_H:(b + 1) * IDX_H], misc[96:96 + IDX_H, b * P:(b + 1) * P],
                                      ident[96:96 + IDX_H, 96:96 + IDX_H])
                G.close(tr)
                pe.wait_ge(s_ridx.sem, 3)
                for b in range(1, TB):
                    for h in range(IDX_H):
                        out = G.open(pe, f"sc{b}{h}")
                        r = slice(64 * (h % 2), 64 * (h % 2) + 64)
                        G.close(pe.matmul(out[:, 0:WQ[b]], idx[r, h // 2, b * P:(b + 1) * P], idx[r, 2, 0:WQ[b]],
                                          start=True, stop=True))
                for i in range(4):
                    out = G.open(pe, f"rq{i}")
                    G.moved(pe, f"q{i}")
                    G.close(pe.matmul(out[:, :], rot, dq[:, i, :], start=True, stop=True))
                out = G.open(pe, "rkr")
                G.close(pe.matmul(out[0:ROPE, :], rot[0:ROPE, 0:ROPE], misc[0:ROPE, :], start=True, stop=True))
                out = G.open(pe, "cms")
                pe.wait_ge(s_csq.sem, 1)
                G.close(pe.matmul(out[:, :], ones, csq, start=True, stop=True))
                for i in range(4):
                    dense(f"za{i}")
                out = G.open(pe, "at")
                pe.wait_ge(s_gates.sem, 1)
                for b in range(TB):
                    tr = pe.transpose(out[:, b * ML_H:(b + 1) * ML_H], g_a[:, b * P:(b + 1) * P], ident[0:ML_H, 0:ML_H])
                G.close(tr)
                pe.wait_ge(s_ckv.sem, 1)
                pe.wait_ge(s_rkr.sem, 1)
                pe.wait_ge(s_lat.sem, 32)
                for i in range(4):
                    out = G.open(pe, f"kk{i}")
                    pe.matmul(out[:, :], wuk[:, i * P:(i + 1) * P], ckv, start=True, stop=False)
                    G.close(pe.matmul(out[:, :], dup[0:ROPE, :], misc[0:ROPE, :], start=False, stop=True))
                for b in range(TB):
                    out = G.open(pe, f"vv{b}")
                    G.close(pe.matmul(out[:, :], ckv[:, b * P:(b + 1) * P], wuv, start=True, stop=True))
                for n in ("zb", "sbq", "sbk"):
                    for i in range(4):
                        dense(f"{n}{i}")
                for i in range(2 * TB):
                    dense_tokens("sbv", i)

                def dsa_scores(h):
                    if h >= 1:
                        pe.wait_ge(s_logit.sem, TB * h)
                    r = slice(64 * (h % 2), 64 * (h % 2) + 64)
                    for b in range(TB):
                        bank, col = KPLACE[TB - 1 - b]
                        mm = pe.matmul(att[bank][:, col:col + WQ[b]], dq[r, h // 2, b * P:(b + 1) * P],
                                       dk[r, h // 2, 0:WQ[b]], start=True, stop=True)
                    s_S.on(mm)

                pe.wait_ge(s_rq.sem, 4)
                G.moved(pe, "kk3")
                dsa_scores(0)
                for h in range(HEADS):
                    if h + 1 < HEADS:
                        dsa_scores(h + 1)
                    n = "mlq" if h < 4 else "mlk"
                    dense(f"{n}{h % 4}")
                    pe.wait_ge(s_scaled.sem, TB * (h + 1))
                    if h >= 1:
                        pe.wait_ge(s_TA.sem, h)
                        pe.wait_ge(s_TV.sem, 2 * h)
                    for s in range(TB):
                        bank, col = KPLACE[s]
                        for b in range(s, TB):
                            tr = pe.transpose(att[3 + bank][:, col + (b - s) * P:col + (b - s + 1) * P],
                                              probs[:, h % 2, OQ[b] + s * P:OQ[b] + (s + 1) * P], ident)
                    s_T.on(tr)
                    out = G.open(pe, f"dsa{h}")
                    G.moved(pe, "vv3")
                    pe.wait_ge(s_TA.sem, h + 1)
                    pe.wait_ge(s_TV.sem, 2 * h + 2)
                    r = slice(64 * (h % 2), 64 * (h % 2) + 64)
                    for s in range(TB):
                        mm = pe.matmul(out[r, s * P:T], dv[:, s, h * HD:(h + 1) * HD],
                                       turned[:, h % 2, KOFF[s]:KOFF[s] + WK[s]], start=(s == 0), stop=(s == TB - 1),
                                       skip_group_check=True)
                    G.close(mm)

                def sb_scores(h):
                    if h == 0:
                        pe.wait_ge(s_logit.sem, TB * HEADS)
                    if h == 1:
                        pe.wait_ge(s_TA.sem, HEADS)
                        pe.wait_ge(s_TV.sem, 2 * HEADS)
                    if h >= 2:
                        pe.wait_ge(s_a_exp.sem, 3 * (h - 1))
                    r = slice(64 * (h % 2), 64 * (h % 2) + 64)
                    for s in range(TB):
                        bank, col = KPLACE[s]
                        mm = pe.matmul(att[3 * (h % 2) + bank][:, col:col + WK[s]], sk[r, h // 2, s * P:(s + 1) * P],
                                       sq_[r, h // 2, s * P:T], start=(s != 3), stop=False, skip_group_check=True)
                    s_Z.on(mm)

                def sb_values(h):
                    out = G.open(pe, f"sb{h}")
                    pe.wait_ge(s_am.sem, TB * (h + 1))
                    r = slice(64 * (h % 2), 64 * (h % 2) + 64)
                    for s in range(TB):
                        mm = pe.matmul(out[r, s * P:T], sv[:, s, h * HD:(h + 1) * HD],
                                       turned[:, h % 2, KOFF[s]:KOFF[s] + WK[s]], start=(s == 0), stop=(s == TB - 1),
                                       skip_group_check=True)
                    G.close(mm)

                G.moved(pe, f"sbv{2 * TB - 1}")
                sb_scores(0)
                for h in range(HEADS):
                    dense_tokens("mlv", h)
                    if h + 1 < HEADS:
                        sb_scores(h + 1)
                    if h >= 1:
                        sb_values(h - 1)
                    if h == 0:
                        pe.wait_ge(s_signs.sem, 1)
                    pe.wait_ge(s_sl.sem, h + 1)
                    for s in range(TB):
                        bank, col = KPLACE[s]
                        for u in range(s, TB):
                            for i, x in enumerate((soft_high, soft_low[:, h % 2, :])):
                                mm = pe.matmul(att[3 * (h % 2) + bank][:, col + (u - s) * P:col + WK[s]],
                                               signs[:, 0:P] if u == s else signs[:, P:2 * P],
                                               x[:, KOFF[u]:KOFF[u] + WK[u]], start=False,
                                               stop=(u == TB - 1 and i == 1), skip_group_check=True)
                    s_tri.on(mm)
                sb_values(HEADS - 1)
                for n in ("mlo", "zc"):
                    for i in range(4):
                        dense(f"{n}{i}")

                def gated_product(d, k):
                    name = f"proj{d}{k}"
                    out = G.open(pe, name)
                    first = d == 0
                    ready = (lambda j: pe.wait_ge(s_zl.sem, 4 * k + j + 1)) if first else None
                    W.product(pe, name, out[:, :], [(z_high[k][:, j, :], z_low[k][:, j, :]) for j in range(4)], ready=ready)

                G.moved(pe, f"mlv{2 * TB - 1}")
                for h in range(ML_H):
                    if h == 0:
                        pe.wait_ge(s_a_exp.sem, 3 * (HEADS - 1))
                        pe.wait_ge(s_silu.sem, 2)
                    else:
                        pe.wait_ge(s_ws.sem, 3 * h)
                    for s in range(TB):
                        bank, col = KPLACE[s]
                        mm = pe.matmul(att[bank][:, col:col + WK[s]], mk[:, h, s * P:(s + 1) * P], mq[:, h, s * P:T],
                                       start=True, stop=True)
                    s_K.on(mm)
                    for n, row in (("mu", g_mu), ("mm", g_m)):
                        out = G.open(pe, f"{n}{h}")
                        G.close(pe.matmul(out[:, :], sel[0:ML_H, h * P:(h + 1) * P], row, start=True, stop=True))
                    dense(f"gate{2 * h}0")
                    gated_product(2 * h, 0)
                    pe.wait_ge(s_ws.sem, 3 * (h + 1))
                    for n in ("den", "num"):
                        out = G.open(pe, f"{n}{h}")
                        for s in range(TB):
                            w = ones if n == "den" else mv[:, s, h * P:(h + 1) * P]
                            mm = pe.matmul(out[:, s * P:T], w, probs[:, h % 2, KOFF[s]:KOFF[s] + WK[s]],
                                           start=(s == 0), stop=(s == TB - 1), skip_group_check=True)
                        G.close(mm)
                    dense(f"gate{2 * h + 1}0")
                    out = G.open(pe, f"mean{h}")
                    G.moved(pe, f"num{h}")
                    G.close(pe.matmul(out[:, :], ones, hml, start=True, stop=True))
                    gated_product(2 * h + 1, 0)
                    out = G.open(pe, f"var{h}")
                    pe.wait_ge(s_sq2.sem, h + 1)
                    G.close(pe.matmul(out[:, :], ones, hsq, start=True, stop=True))

                for d in range(KD):
                    for k in (1, 2):
                        dense(f"gate{d}{k}")
                        gated_product(d, k)
                for d in range(KD):
                    out = G.open(pe, f"out{d}")
                    ready = (lambda k: pe.wait_ge(s_ml.sem, k + 1)) if d == 0 else None
                    W.product(pe, f"out{d}", out[:, :], [(mix_high[k], mix_low[:, k, :]) for k in range(KD)], ready=ready)

            @block.scalar
            def _(act):
                def move(name, out, func=ACT.Copy, rows_=None, **kw):
                    W.round(act, name)
                    bank = G.whole(act, name)
                    src = bank[:, 0:T] if rows_ is None else bank[:, rows_]
                    G.empty(act.activation(out, src, func, **kw), name)

                act.preload_act_table_set("sqrt_and_others")
                for k in range(KD):
                    s_sq.on(act.activation(hT[:, k, :], xT[:, k, :], ACT.Square))
                move("ms", rstd[:], ACT.Sqrt, scale=1.0 / D, bias=mark["eps"])
                for k in range(KD):
                    act.wait_ge(s_h.sem, k + 1)
                    s_hh.on(act.activation(h_high[:, k, :], hT[:, k, :], ACT.Copy))
                for i in range(4):
                    move(f"idx{i}", idx[:, i, :])
                move("misc", misc[:])
                move("q0", dq[:, 0, :], scale=HD ** -0.5)
                settle(act, s_a)
                s_csq.on(act.activation(csq, ckv, ACT.Square))
                act.wait_ge(s_vec.sem, 16)
                s_ir.on(act.activation(g_i, misc[32:32 + ML_H, :], ACT.Identity, bias=vecs[32:32 + ML_H, 45:46]))
                s_ir.on(act.activation(g_f, misc[64:64 + ML_H, :], ACT.Identity, bias=vecs[64:64 + ML_H, 46:47]))
                for i in range(1, 4):
                    move(f"q{i}", dq[:, i, :], scale=HD ** -0.5)
                n = 0
                for b in range(1, TB):
                    for h in range(IDX_H):
                        if n >= 2:
                            act.wait_ge(s_scused.sem, n - 1)
                        move(f"sc{b}{h}", relu[:, n % 2, 0:WQ[b]], ACT.Relu, rows_=slice(0, WQ[b]))
                        n += 1
                act.preload_act_table_set("natural_log_exp_and_others")
                s_ac.on(act.activation(g_sum, g_f, ACT.Abs))
                settle(act, s_ac)
                s_ac.on(act.activation(g_sum, g_sum, ACT.Exp, scale=-1.0))
                settle(act, s_ac)
                s_ln.on(act.activation(g_sum, g_sum, ACT.Ln, bias=1.0))
                move("cms", rstd[:], ACT.Sqrt, scale=1.0 / P, bias=mark["eps"])
                for i in range(4):
                    move(f"za{i}", za[:, i, :], ACT.Silu)
                for i in range(4):
                    move(f"kk{i}", dk[:, i, :])
                for b in range(TB):
                    move(f"vv{b}", dv[:, b, :])
                for i in range(4):
                    move(f"zb{i}", zb[:, i, :], ACT.Silu)
                for i in range(4):
                    move(f"sbq{i}", sq_[:, i, :], scale=HD ** -0.5)
                for i in range(4):
                    move(f"sbk{i}", sk[:, i, :])
                for i in range(2 * TB):
                    move(f"sbv{i}", sv[:, i % TB, (i // TB) * HALF:(i // TB + 1) * HALF], rows_=slice(0, HALF))
                act.preload_act_table_set("natural_log_exp_and_others")
                for h in range(HEADS):
                    act.wait_ge(s_logit.sem, TB * (h + 1))
                    act.wait_ge(s_rinv.sem, 2 * h + 1)
                    for b in range(TB):
                        s_exp.on(act.activation(probs[:, h % 2, OQ[b]:OQ[b] + WQ[b]], probs[:, h % 2, OQ[b]:OQ[b] + WQ[b]],
                                                ACT.Exp, bias=small[:, 8 + 4 * (h % 2) + b:9 + 4 * (h % 2) + b],
                                                accum_out=small[:, 16 + 4 * (h % 2) + b:17 + 4 * (h % 2) + b]))
                    n = "mlq" if h < 4 else "mlk"
                    if h == 0:
                        act.wait_ge(s_bias.sem, TB)
                        act.wait_ge(s_pad.sem, 1)
                        G.moved(act, "vv3")
                    move(f"{n}{h % 4}", raw[:, h, 3:3 + T])
                    act.wait_ge(s_T.sem, h + 1)
                    if h >= 2:
                        G.whole(act, f"dsa{h - 2}")
                    s_TA.on(act.activation(turned[:, h % 2, 0:T], att[3][:, :], ACT.Copy))
                def softplus(h):
                    act.wait_ge(s_Z.sem, h + 1)
                    if h <= 1:
                        act.wait_ge(s_T.sem, HEADS)
                    else:
                        act.wait_ge(s_tri.sem, h - 1)
                    for bank, n, at in BANKS:
                        s_ac.on(act.activation(probs[:, h % 2, at:at + n], att[3 * (h % 2) + bank][:, 0:n], ACT.Abs))
                    settle(act, s_ac)
                    s_ac.on(act.activation(probs[:, h % 2, :], probs[:, h % 2, :], ACT.Exp, scale=-1.0))
                    settle(act, s_ac)
                    s_soft.on(act.activation(probs[:, h % 2, :], probs[:, h % 2, :], ACT.Ln, bias=1.0))

                def softplus_high(h):
                    act.wait_ge(s_spm.sem, TB * (h + 1))
                    s_sh.on(act.activation(soft_high[:], probs[:, h % 2, :], ACT.Copy))

                a = CONST["tri"][0]
                s_signs.on(act.activation(signs[:], consts[:, a:a + 2 * P], ACT.Copy))
                softplus(0)
                softplus_high(0)
                for h in range(HEADS):
                    if h + 1 < HEADS:
                        softplus(h + 1)
                    move(f"mlv{h}", mv[:, h % TB, (h // TB) * HALF:(h // TB + 1) * HALF], rows_=slice(0, HALF))
                    act.wait_ge(s_tri.sem, h + 1)
                    if h >= 2:
                        G.whole(act, f"sb{h - 2}")
                    else:
                        G.whole(act, f"dsa{HEADS - 2 + h}")
                    for bank, n, at in BANKS:
                        s_a_exp.on(act.activation(turned[:, h % 2, at:at + n], att[3 * (h % 2) + bank][:, 0:n], ACT.Exp))
                    if h + 1 < HEADS:
                        softplus_high(h + 1)
                for i in range(4):
                    move(f"mlo{i}", mlo[:, i, :], ACT.Sigmoid)
                for i in range(4):
                    move(f"zc{i}", zc[:, i, :], ACT.Silu)
                act.wait_ge(s_conv.sem, 4)
                s_silu.on(act.activation(mq[:], mq[:], ACT.Silu))
                act.wait_ge(s_conv.sem, 8)
                s_silu.on(act.activation(mk[:], mk[:], ACT.Silu))
                G.whole(act, f"sb{HEADS - 1}")
                G.moved(act, f"dsa{HEADS - 1}")
                for j in range(4):
                    s_zh.on(act.activation(z_high[0][:, j, :], za[:, j, :], ACT.Copy))

                def first_gate(d):
                    move(f"gate{d}0", mixed[:, d, :], ACT.Sigmoid)
                    W.round(act, f"proj{d}0")

                for h in range(ML_H):
                    bank = G.whole(act, f"mu{h}")
                    if h <= 1:
                        G.whole(act, f"sb{HEADS - 2 + h}")
                        act.wait_ge(s_tri.sem, HEADS)
                    else:
                        act.wait_ge(s_ws.sem, 3 * (h - 1))
                    for s in range(TB):
                        ins = act.activation(turned[:, h % 2, KOFF[s]:KOFF[s] + WK[s]], bank[:, s * P:T], ACT.Exp,
                                             bias=acol[:, s, h:h + 1])
                        if s < TB - 1:
                            s_w8.on(ins)
                    G.empty(ins, f"mu{h}")
                    bank = G.whole(act, f"mm{h}")
                    if h >= 1:
                        G.moved(act, f"num{h - 1}")
                    G.empty(act.activation(em, bank[:, :], ACT.Exp), f"mm{h}")
                    first_gate(2 * h)
                    move(f"den{h}", dn, ACT.Abs)
                    first_gate(2 * h + 1)
                    G.moved(act, f"mean{h}")
                    s_sq2.on(act.activation(hsq, hml, ACT.Square))
                    move(f"var{h}", rstd[:], ACT.Sqrt, scale=1.0 / ML_D, bias=mark["eps"])
                G.whole(act, f"num{ML_H - 1}")
                for d in range(KD):
                    for k in (1, 2):
                        if d >= 1:
                            G.moved(act, f"proj{d - 1}{k}")
                        move(f"gate{d}{k}", gate[:, k, :], ACT.Sigmoid)
                        W.round(act, f"proj{d}{k}")
                        if d == 0:
                            if k == 2:
                                act.wait_ge(s_mlz.sem, ML_H)
                            for j in range(4):
                                s_zh.on(act.activation(z_high[k][:, j, :], (za, zb, zc)[k][:, j, :], ACT.Copy))
                    if d >= 1:
                        act.wait_ge(s_mix.sem, d)
                        s_mh.on(act.activation(mix_high[d - 1], mixed[:, d - 1, :], ACT.Copy))
                act.wait_ge(s_mix.sem, KD)
                s_mh.on(act.activation(mix_high[KD - 1], mixed[:, KD - 1, :], ACT.Copy))
                for d in range(KD):
                    W.round(act, f"out{d}")

            @block.vector
            def _(dve):
                def link(ins):
                    s_vc.on(ins)
                    settle(dve, s_vc)

                def rotate(name, x, n, ready):
                    bank = G.whole(dve, name)
                    turn = dv[0:n, 0, :]
                    G.empty(dve.tensor_tensor(turn, bank[0:n, :], sinT[0:n, :], ALU.mult), name)
                    link(dve.tensor_tensor(x, x, cosT[0:n, :], ALU.mult))
                    settle(dve, s_v)
                    ready.on(dve.tensor_tensor(x, x, turn, ALU.add))
                    settle(dve, ready)

                def low_part(k):
                    dve.wait_ge(s_hh.sem, k + 1)
                    s_hl.on(dve.tensor_tensor(h_low[:, k, :], hT[:, k, :], h_high[:, k, :], ALU.subtract))

                for k in range(1, KD):
                    dve.wait_ge(s_sq.sem, k + 1)
                    ins = dve.tensor_tensor(rstd[:], hT[:, 0, :] if k == 1 else rstd[:], hT[:, k, :], ALU.add)
                    if k < KD - 1:
                        link(ins)
                    else:
                        s_sum.on(ins)
                dve.wait_ge(s_vec.sem, 16)
                G.moved(dve, "ms")
                link(dve.reciprocal(rstd[:], rstd[:]))
                for k in range(KD):
                    s_h.on(dve.scalar_tensor_tensor(hT[:, k, :], xT[:, k, :], vecs[:, k:k + 1], rstd[:], ALU.mult, ALU.mult))
                    if k >= 1:
                        low_part(k - 1)
                low_part(KD - 1)
                for i in range(3):
                    rotate(f"ridx{i}", idx[:, i, :], P, s_ridx)
                bank = G.whole(dve, "iwt")
                G.empty(dve.tensor_copy(iwt[:].rearrange("p a b -> p (a b)"), bank[:, 0:TB * IDX_H]), "iwt")
                settle(dve, s_v)
                n = 0
                for b in range(1, TB):
                    out = score[:, OQ[b]:OQ[b] + WQ[b]]
                    for h in range(IDX_H):
                        G.moved(dve, f"sc{b}{h}")
                        r, w = relu[:, n % 2, 0:WQ[b]], iwt[:, b, h:h + 1]
                        if h == 0:
                            s_scused.on(dve.tensor_scalar(out, r, w, None, ALU.mult))
                        else:
                            s_scused.on(dve.scalar_tensor_tensor(out, r, w, out, ALU.mult, ALU.add))
                        settle(dve, s_scused)
                        n += 1
                for i in range(4):
                    rotate(f"rq{i}", dq[:, i, :], P, s_rq)
                rotate("rkr", misc[0:ROPE, :], ROPE, s_rkr)
                link(dve.memset(g_mu, 1.0))
                dve.wait_ge(s_ln.sem, 1)
                link(dve.scalar_tensor_tensor(g_f, g_f, 0.0, g_sum, ALU.min, ALU.subtract))
                link(dve.tensor_tensor_scan(g_sum, g_mu, g_f, 0.0, ALU.mult, ALU.add))
                link(dve.tensor_tensor(g_a, g_i, g_sum, ALU.subtract))
                link(dve.tensor_tensor_scan(g_m, g_a, g_a, 0.0, ALU.max, ALU.max))
                link(dve.tensor_scalar(g_mu, g_m, -1.0, None, ALU.mult))
                s_gates.on(dve.scalar_tensor_tensor(g_m, g_sum, -1.0, g_m, ALU.mult, ALU.subtract))
                G.moved(dve, "cms")
                link(dve.reciprocal(rstd[:], rstd[:]))
                s_ckv.on(dve.scalar_tensor_tensor(ckv, ckv, vecs[:, 8:9], rstd[:], ALU.mult, ALU.mult))
                bank = G.whole(dve, "at")
                G.empty(dve.tensor_copy(acol[:].rearrange("p a b -> p (a b)"), bank[:, 0:TB * ML_H]), "at")
                dve.wait_ge(s_masked.sem, TB - 1)
                for _ in range(TOPK // 8):
                    for b in range(1, TB):
                        x = score[:, OQ[b]:OQ[b] + WQ[b]]
                        link(dve.max(top8[:, b, :], x))
                        link(dve.match_replace(out=x, in_to_replace=top8[:, b, :], in_values=x, imm_value=TAKEN))
                s_bias.on(dve.tensor_copy(bias[:, 0:P], cmask))
                for b in range(1, TB):
                    o = slice(OQ[b], OQ[b] + WQ[b])
                    s_bias.on(dve.tensor_scalar(bias[:, o], score[:, o], ALIVE, NEG, ALU.is_gt, ALU.mult))
                settle(dve, s_bias)
                G.moved(dve, "vv3")
                s_pad.on(dve.memset(raw[:, :, 0:3], 0.0))

                def dsa_logits(h):
                    o = 4 * (h % 2)
                    dve.wait_ge(s_S.sem, h + 1)
                    if h >= 2:
                        dve.wait_ge(s_T.sem, h - 1)
                    for b in range(TB):
                        bank, col = KPLACE[TB - 1 - b]
                        s = slice(OQ[b], OQ[b] + WQ[b])
                        s_logit.on(dve.tensor_tensor_reduce(
                            out=probs[:, h % 2, s], in0=att[bank][:, col:col + WQ[b]], in1=bias[:, s], scale=1.0,
                            scalar=TAKEN, op0=ALU.add, op1=ALU.max, accum_out=small[:, o + b:o + b + 1]))
                    settle(dve, s_logit)
                    s_rinv.on(dve.tensor_scalar(small[:, 8 + o:12 + o], small[:, o:o + 4], -1.0, None, ALU.mult))

                def dsa_turned(h):
                    dve.wait_ge(s_T.sem, h + 1)
                    if h >= 2:
                        G.whole(dve, f"dsa{h - 2}")
                    for bank, n, at in BANKS[1:]:
                        s_TV.on(dve.tensor_copy(turned[:, h % 2, at:at + n], att[3 + bank][:, 0:n]))

                def gated(name, h, z):
                    bank = G.whole(dve, name)
                    r = slice(64 * (h % 2), 64 * (h % 2) + 64)
                    G.empty(dve.tensor_tensor(z[r, h // 2, :], bank[r, :], z[r, h // 2, :], ALU.mult), name)

                G.moved(dve, "za3")
                for h in range(HEADS + 1):
                    if h < HEADS:
                        dsa_logits(h)
                    if h >= 1:
                        dsa_turned(h - 1)
                        gated(f"dsa{h - 1}", h - 1, za)
                    if h < HEADS:
                        o = 4 * (h % 2)
                        dve.wait_ge(s_exp.sem, TB * (h + 1))
                        s_rinv.on(dve.reciprocal(small[:, 24 + o:28 + o], small[:, 16 + o:20 + o]))
                for h in range(HEADS + 1):
                    if h < HEADS:
                        dve.wait_ge(s_soft.sem, h + 1)
                        for bank, n, at in BANKS:
                            s_sp.on(dve.scalar_tensor_tensor(probs[:, h % 2, at:at + n], att[3 * (h % 2) + bank][:, 0:n], 0.0,
                                                             probs[:, h % 2, at:at + n], ALU.max, ALU.add))
                        G.moved(dve, ("mlq" if h < 4 else "mlk") + str(h % 4))
                        dst = (mq if h < 4 else mk)[:, h % 4, :]
                        link(dve.tensor_scalar(dst, raw[:, h, 0:T], vecs[:, 9 + h:10 + h], None, ALU.mult))
                        for j in range(1, 4):
                            s_conv_ = s_conv if j == 3 else s_vc
                            s_conv_.on(dve.scalar_tensor_tensor(dst, raw[:, h, j:j + T], vecs[:, 9 + 8 * j + h:10 + 8 * j + h],
                                                                dst, ALU.mult, ALU.add))
                            settle(dve, s_conv_)
                    if h < HEADS:
                        dve.wait_ge(s_sh.sem, h + 1)
                        s_sl.on(dve.tensor_tensor(soft_low[:, h % 2, :], probs[:, h % 2, :], soft_high[:], ALU.subtract))
                    if h >= 1:
                        gated(f"sb{h - 1}", h - 1, zb)
                def branch_low(k):
                    for j in range(4):
                        dve.wait_ge(s_zh.sem, 4 * k + j + 1)
                        s_zl.on(dve.tensor_tensor(z_low[k][:, j, :], (za, zb, zc)[k][:, j, :], z_high[k][:, j, :], ALU.subtract))

                def first_gated(d):
                    bank = G.whole(dve, f"proj{d}0")
                    G.moved(dve, f"gate{d}0")
                    G.empty(dve.tensor_tensor(mixed[:, d, :], bank[:, :], mixed[:, d, :], ALU.mult), f"proj{d}0")

                branch_low(0)
                G.moved(dve, "zc3")
                for h in range(ML_H):
                    dve.wait_ge(s_w8m.sem, TB * (h + 1))
                    dve.wait_ge(s_K.sem, h + 1)
                    if h >= 2:
                        G.whole(dve, f"num{h - 2}")
                    for bank, n, at in BANKS:
                        s_ws.on(dve.scalar_tensor_tensor(probs[:, h % 2, at:at + n], att[bank][:, 0:n], ML_D ** -0.5,
                                                         turned[:, h % 2, at:at + n], ALU.mult, ALU.mult))
                    first_gated(2 * h)
                    G.moved(dve, f"mm{h}")
                    G.moved(dve, f"den{h}")
                    link(dve.tensor_tensor(dn, dn, em, ALU.max))
                    link(dve.reciprocal(dn, dn))
                    bank = G.whole(dve, f"num{h}")
                    G.empty(dve.tensor_tensor(hml, bank[:, :], dn, ALU.mult), f"num{h}")
                    settle(dve, s_v)
                    bank = G.whole(dve, f"mean{h}")
                    G.empty(dve.scalar_tensor_tensor(hml, bank[:, :], -1.0 / ML_D, hml, ALU.mult, ALU.add), f"mean{h}")
                    first_gated(2 * h + 1)
                    settle(dve, s_v)
                    G.moved(dve, f"var{h}")
                    link(dve.reciprocal(rstd[:], rstd[:]))
                    link(dve.scalar_tensor_tensor(hml, hml, vecs[:, 41 + h:42 + h], rstd[:], ALU.mult, ALU.mult))
                    link(dve.tensor_tensor(hml, hml, mlo[:, h, :], ALU.mult))
                    s_mlz.on(dve.tensor_tensor(zc[:, h, :], zc[:, h, :], hml, ALU.mult))
                    settle(dve, s_mlz)
                def mixed_low(d):
                    dve.wait_ge(s_mh.sem, d + 1)
                    s_ml.on(dve.tensor_tensor(mix_low[:, d, :], mixed[:, d, :], mix_high[d], ALU.subtract))

                for d in range(KD):
                    for k in (1, 2):
                        n = f"proj{d}{k}"
                        if d == 0:
                            branch_low(k)
                        bank = G.whole(dve, n)
                        G.moved(dve, f"gate{d}{k}")
                        G.empty(dve.tensor_tensor(part[:, k - 1, :], bank[:, :], gate[:, k, :], ALU.mult), n)
                        settle(dve, s_v)
                        if k == 1:
                            link(dve.tensor_tensor(mixed[:, d, :], mixed[:, d, :], part[:, 0, :], ALU.add))
                        if k == 2:
                            s_mix.on(dve.tensor_tensor(mixed[:, d, :], mixed[:, d, :], part[:, 1, :], ALU.add))
                    if d >= 1:
                        mixed_low(d - 1)
                mixed_low(KD - 1)
                for d in range(KD):
                    n = f"out{d}"
                    bank = G.whole(dve, n)
                    G.empty(dve.tensor_tensor(xT[:, d, :], bank[:, :], xT[:, d, :], ALU.add), n)

            @block.gpsimd
            def _(pool):
                def triangle(x, op, sign, fill):
                    return pool.affine_select(out=x, in_=x, compare_op=op, fill=fill, base=0, pattern=[[sign, P]],
                                              channel_multiplier=-sign)

                for b in range(1, TB):
                    W.rest(pool, f"sc{b}0")
                    pool.wait_ge(s_scused.sem, IDX_H * b)
                    s_masked.on(triangle(score[:, OQ[b] + b * P:OQ[b] + (b + 1) * P], ALU.is_ge, -1, DROPPED))
                for h in range(HEADS):
                    W.rest(pool, ("mlq" if h < 4 else "mlk") + str(h % 4))
                    pool.wait_ge(s_rinv.sem, 2 * h + 2)
                    for b in range(TB):
                        x = probs[:, h % 2, OQ[b]:OQ[b] + WQ[b]]
                        o = 24 + 4 * (h % 2) + b
                        s_scaled.on(pool.tensor_scalar(x, x, small[:, o:o + 1], 1.0, ALU.mult, ALU.mult))
                def mask_softplus(h):
                    pool.wait_ge(s_sp.sem, 3 * (h + 1))
                    for s in range(TB):
                        s_spm.on(triangle(probs[:, h % 2, KOFF[s]:KOFF[s] + P], ALU.is_gt, 1, 0.0))

                W.rest(pool, "mlk3")
                mask_softplus(0)
                for h in range(HEADS):
                    if h + 1 < HEADS:
                        mask_softplus(h + 1)
                    W.rest(pool, f"mlv{h}")
                    pool.wait_ge(s_a_exp.sem, 3 * (h + 1))
                    for s in range(TB):
                        s_am.on(triangle(turned[:, h % 2, KOFF[s]:KOFF[s] + P], ALU.is_gt, 1, 0.0))
                for h in range(ML_H):
                    W.rest(pool, f"mu{h}")
                    G.moved(pool, f"mu{h}")
                    for s in range(TB):
                        s_w8m.on(triangle(turned[:, h % 2, KOFF[s]:KOFF[s] + P], ALU.is_ge, 1, 0.0))
                W.rest(pool, f"out{KD - 1}")

        with nc.Block() as block:

            @block.sync
            def _(sp):
                for s in every:
                    sp.sem_clear(s.sem)



FF = 2816
KF = FF // P
PATTERNS = 3
SLOTS_H = 4
XH, XD, MEM = 4, 128, 256
SG, SS = 32, 64
NT = SG * SS // P
AW = PATTERNS * SLOTS_H * HD
MAGIC = 12582912.0
TWO_PI = 6.283185
HALF_PI = 1.5707963
PI_A, PI_B = 6.28125, 0.0019350051879882812
PI_C = 2 * np.pi - PI_A - PI_B
TOEP = 640

DIL = [[(max(0, b - 1) * P, P * (1 + (b > 0))) for b in range(TB)]] + [[(0, WQ[b]) for b in range(TB)]] * 2
DOFF, _at = [], 0
for _g in range(PATTERNS):
    DOFF.append([])
    for _b in range(TB):
        DOFF[_g].append(_at)
        _at += DIL[_g][_b][1]
DALL = _at

VEC2 = {}
_c = 0
for _n, _w in (("fin1", KD), ("ffn1", KD), ("mix", KD), ("ffn2", KD), ("fin2", KD), ("mem", KD), ("skip", 4),
               ("are", NT), ("aim", NT), ("ldt", NT)):
    VEC2[_n] = (_c, _c + _w)
    _c += _w
N_VEC2 = _c
NORMS = ["fin1", "ffn1", "mix", "ffn2", "fin2"]
SPLIT_NORMS = ["ffn1", "mix", "ffn2"]

FILLERS = [("q", i) for i in range(6)] + [("k", i) for i in range(6)] + [("v", i) for i in range(3 * TB)] + [("xq", i) for i in range(4)]


def fillers_of(j):
    return FILLERS[j * len(FILLERS) // NT:(j + 1) * len(FILLERS) // NT]


def block_tiles():
    def ffn(n):
        t = []
        for i in range(KF):
            t += [(f"{n}a{i}", KD, P), (f"{n}b{i}", KD, P)]
        return t + [(f"{n}d{d}", KF, P) for d in range(KD)]
    t = ffn("f1") + [(f"mk{i}", KD, P) for i in range(XH)] + [(f"mv_part{c}", KD, HALF) for c in range(2)]
    t += [(f"{n}{i}", KD, P) for n, c in (("u", 4), ("q", 6), ("k", 6)) for i in range(c)]
    t += [(f"v_part{c}", KD, HALF) for c in range(3)] + [(f"xq{i}", KD, P) for i in range(XH)]
    for d in range(KD):
        t += [(f"g0{d}", KD, P), (f"glb{d}", 4, P), (f"gla{d}", 4, P)]
    for d in range(KD):
        t += [(f"g1{d}", KD, P), (f"up{d}", 2, P), (f"g2{d}", KD, P), (f"xup{d}", 4, P)]
    return t + [(f"o{d}", KD, P) for d in range(KD)] + ffn("f2")


def block_tile_of():
    of = {n: n for n, _, _ in block_tiles()}
    for i in range(2 * (MEM // P)):
        of[f"mv{i}"] = f"mv_part{i // (MEM // P)}"
    for i in range(3 * TB):
        of[f"v{i}"] = f"v_part{i // TB}"
    return of


def block_groups():
    def ffn(n, between=[]):
        g = []
        for i in range(KF):
            g += [(f"{n}a{i}", "a"), (f"{n}b{i}", "v")]
        return g + between + [(f"{n}d{d}", "v") for d in range(KD)]
    g = [(f"toep{i}", "a") for i in range(4)]
    g += [("ms_fin1", "a"), ("ms_ffn1", "a")] + ffn("f1", [("ms_mem", "a")])
    g += [(f"mk{i}", "a") for i in range(4)] + [(f"mv{i}", "a") for i in range(4)]
    g += [("ms_mix", "a")] + [(f"u{i}", "a") for i in range(4)]
    for j in range(NT):
        g += [(f"{n}{i}", "a") for n, i in fillers_of(j)]
    for d in range(KD):
        g += [(f"g0{d}", "a"), (f"glb{d}", "a"), (f"gla{d}", "v")]
    g += [(f"xo{h}", "v") for h in range(XH)]
    for d in range(KD):
        g += [(f"g1{d}", "a"), (f"up{d}", "v"), (f"g2{d}", "a"), (f"xup{d}", "v")]
    g += [(f"o{d}", "v") for d in range(KD)]
    g += [("ms_ffn2", "a")] + ffn("f2") + [("ms_fin2", "a")]
    return g


CONST2 = {"ident": (0, P), "ones": (P, 2 * P), "iota": (2 * P, 2 * P + T)}
N_CONST2 = 2 * P + T


def second_block(nc, stack, xT, A, scratch, out_dram):
    def sb(name, shape, dt=F32):
        return stack.enter_context(nc.sbuf_tensor("b2_" + name, shape, dt))

    def sem(name):
        return Signal(stack.enter_context(nc.semaphore("b2_" + name)))

    def here():
        return -(-nc.sbuf_base // 32) * 32

    def rounded(name, shape, at):
        return nc.alloc_sbuf_tensor_at("b2_" + name, shape, F32R, offset=at)

    hT_at, hT = here(), sb("hT", [P, KD, T])
    raw_at, ring = here(), sb("ring", [P, RAW2, UNIT])
    low = rounded("weight_low", [P, RAW2, UNIT], raw_at)
    high = sb("weight_high", [P, HIGH, UNIT], F32R)
    h_low = rounded("h_low", [P, KD, T], hT_at)
    h_high = sb("h_high", [P, KD, T], F32R)
    h_parts = [(h_high[:, k, :], h_low[:, k, :]) for k in range(KD)]
    vecs = sb("vecs", [P, N_VEC2])
    consts = sb("consts", [P, N_CONST2])
    ident, ones, iota = (consts[:, a:b] for a, b in CONST2.values())
    big_at, big = here(), sb("big", [P, KF, T])
    uT_at, uT = here(), sb("uT", [P, 4, T])
    qkvx_at, qkvx = here(), sb("qkvx", [P, KF, T])
    qk = qkvx[:, 0:12, :]
    v = qkvx[:, 12:18, :].rearrange("p a b -> p (a b)").rearrange("p (a b) -> p a b", a=TB)
    xq = qkvx[:, 18:22, :]
    mk = sb("mk", [P, XH, MEM])
    logits_at, logits = here(), sb("logits", [P, DALL])
    turned_at, turned = here(), sb("turned", [P, 2, CAUSAL])
    rstd = sb("rstd", [P, T])
    st = sb("st", [P, 24, NT])
    am = sb("am", [P, 64])
    q, k = qk[:, 0:6, :], qk[:, 6:12, :]
    merged = big[:, 4:4 + KD, :]
    memT = logits[:, 0:KD * MEM].rearrange("p (a b) -> p a b", a=KD)
    memsq = turned[:].rearrange("p a b -> p (a b)")[:, 0:KD * MEM].rearrange("p (a b) -> p a b", a=KD)
    onehot = logits[:, 0:3 * TOEP]
    table = logits[0:33, 3 * TOEP:3 * TOEP + 12]
    toep = qkvx[0:12, 18:22, :].rearrange("p a b -> p (a b)")[:, 0:3 * TOEP]
    ssm_gates = big[:, 12:14, :]
    gates = turned[:].rearrange("p a b -> p (a b)")[:, 0:2 * T].rearrange("p (a b) -> p a b", a=2)
    parts = logits[:, 0:2 * T].rearrange("p (a b) -> p a b", a=2)
    bflat = big[:].rearrange("p a b -> p (a b)")
    work = [[big[:, 6 * s + i, :] for i in range(6)] for s in range(2)]
    b_in = [bflat[:, (12 + i) * T:(13 + i) * T] for i in range(2)]
    c_raw = [bflat[:, (14 + i) * T:(15 + i) * T].rearrange("p (a b) -> p a b", a=NT) for i in range(2)]
    c_out = [bflat[:, (16 + i) * T:(17 + i) * T].rearrange("p (a b) -> p a b", a=NT) for i in range(2)]
    yatt, mv = big[:, 18:20, :], big[:, 20:22, :]
    biases = [sb("bias0", [P, 2 * P])[:], big[:, 14, :], big[:, 15, :]]
    act_low, act_high = rounded("act_low", [P, KF, T], big_at), rounded("act_high", [P, KF, T], qkvx_at)
    mem_low = rounded("mem_low", [P, KD, MEM], logits_at)
    mem_high = rounded("mem_high", [P, KD, MEM], turned_at)
    u_low, u_high = rounded("u_low", [P, 4, T], uT_at), rounded("u_high", [P, 4, T], big_at)
    tile = 4 * T
    yatt_low, yatt_high = rounded("yatt_low", [P, 2, T], big_at + 18 * tile), rounded("yatt_high", [P, 2, T], qkvx_at + 8 * tile)
    x_low, x_high = rounded("x_low", [P, XH, T], qkvx_at + 18 * tile), rounded("x_high", [P, XH, T], qkvx_at + 10 * tile)
    merged_low = rounded("merged_low", [P, KD, T], big_at + 4 * tile)
    merged_high = rounded("merged_high", [P, KD, T], qkvx_at)
    halfpi, epsc = st[:, 23, 0:1], st[:, 23, 1:2]

    proj = [stack.enter_context(nc.psum_tensor(f"b2_proj{i}", [P, T], F32)) for i in range(2)]
    att = [stack.enter_context(nc.psum_tensor(f"b2_att{i}", [P, T], F32)) for i in range(6)]

    (s_const, s_onehot, s_done, s_a, s_v, s_sq, s_h, s_vc, s_ac, s_pc, s_set, s_toep, s_ssm, s_mem, s_msq, s_mh, s_out,
     s_dt, s_r, s_trig, s_cw, s_ph, s_tab, s_bu, s_rot, s_w, s_z, s_x, s_y, s_yv, s_yg,
     s_S, s_lg, s_neg, s_exp, s_rinv, s_scaled, s_T, s_TA, s_TV, s_am2,
     s_xS, s_xneg, s_xexp, s_xrinv, s_xscaled, s_xT, s_xTA, s_xTV, s_merged) = (sem(n) for n in (
         "const onehot done act_moved dve_moved square h dve act pool set toep ssm mem msq mh out "
         "dt r trig cw phase table bu rot w z x y yv yg "
         "S logit neg exp rinv scaled T TA TV am2 "
         "xS xneg xexp xrinv xscaled xT xTA xTV merged").split())
    s_sum, s_glu, s_att, s_att_moved = (sem(n) for n in ("squares_summed glu_gated att_out att_moved").split())
    s_load = [sem(f"load{i}") for i in range(RAW2)]
    s_used, s_high, s_low = sem("chunk_used"), sem("weight_high"), sem("weight_low")
    s_hh, s_hl, s_gh, s_gl, s_memh, s_meml, s_bh, s_bl, s_mgh, s_mgl = (sem(n) for n in (
        "h_high h_low act_high act_low mem_high mem_low branch_high branch_low merged_high merged_low").split())
    s_bias = [sem(f"bias{i}") for i in range(PATTERNS)]

    att_out = att[0]

    G = Groups(block_groups(), proj, s_done, {"a": s_a, "v": s_v})
    W = Weights(block_tiles(), G, block_tile_of(), RAW2, ring, high, low, s_load, s_used, s_high, s_low)

    def vec(name, i=0, n=1):
        a = VEC2[name][0] + i
        return vecs[:, a:a + n]

    with nc.Block() as block:

        @block.sync
        def _(sp):
            s_const.on(sp.dma_start(consts[:], A["const2"]), 16)
            s_const.on(sp.dma_start(vecs[:], A["vec2"]), 16)
            s_onehot.on(sp.dma_start(onehot[0:33, :], A["onehot"]), 16)
            s_onehot.on(sp.dma_start(table, A["table"]), 16)
            for c in range(W.n_chunks):
                W.load(sp, c, A["stream"][c])
            G.moved(sp, "ms_fin2")
            sp.wait_ge(s_h.sem, KD * len(NORMS))
            s_out.on(sp.dma_start(out_dram, hT[:]), 16)
            sp.wait_ge(s_out.sem, 16)

        @block.gpsimd
        def _(pool):
            G.moved(pool, "toep3")
            for r in range(PATTERNS * SLOTS_H):
                g = r // SLOTS_H
                row = toep[r:r + 1, g * TOEP:(g + 1) * TOEP].unsqueeze(1).to_broadcast([1, P, TOEP])
                s_toep.on(pool.dma_start(scratch[r:r + 1], row), 16)
            W.rest(pool, "f1a0")
            pool.wait_ge(s_toep.sem, 16 * PATTERNS * SLOTS_H)
            s_mem.on(pool.dma_start(memT, A["mem"]), 16)
            W.rest(pool, f"f1d{KD - 1}")
            G.whole(pool, f"f1d{KD - 1}")
            for i, n in enumerate(("bre", "bim")):
                s_ssm.on(pool.dma_start(b_in[i], A[n]), 16)
            for i, n in enumerate(("cre", "cim")):
                s_ssm.on(pool.dma_start(c_raw[i], A[n]), 16)

            def link(ins):
                s_pc.on(ins)
                settle(pool, s_pc)

            def load_bias(n):
                h, g = divmod(n, PATTERNS)
                if h >= 1:
                    pool.wait_ge(s_lg.sem, TB * (n - PATTERNS + 1))
                width = 2 * P if g == 0 else T
                row = (g * SLOTS_H + h) * P * TOEP
                src = bass.AP(scratch.tensor, row + P - 1, [[TOEP - 1, P], [1, width]])
                s_bias[g].on(pool.dma_start(biases[g][:, 0:width], src), 16)

            W.rest(pool, "u3")
            pool.wait_ge(s_cw.sem, 1)
            for n in range(PATTERNS):
                load_bias(n)
            for j in range(NT):
                c, s, t1, t2, t3, t4 = work[j % 2]
                W.rest(pool, "{}{}".format(*fillers_of(j - 1)[-1]) if j else "u3")
                pool.wait_ge(s_z.sem, 2 * (j + 1))
                s_pc.on(pool.tensor_tensor(t2, t1, c, ALU.mult))
                link(pool.tensor_tensor(t4, t3, s, ALU.mult))
                s_pc.on(pool.tensor_tensor(t2, t2, t4, ALU.subtract))
                s_pc.on(pool.tensor_tensor(t1, t1, s, ALU.mult))
                link(pool.tensor_tensor(t3, t3, c, ALU.mult))
                s_x.on(pool.tensor_tensor(t1, t1, t3, ALU.add))
            for h in range(SLOTS_H):
                W.rest(pool, f"gla{2 * h}")
                pool.wait_ge(s_rinv.sem, h + 1)
                for g in range(PATTERNS):
                    for b in range(TB):
                        x = logits[:, DOFF[g][b]:DOFF[g][b] + DIL[g][b][1]]
                        s_scaled.on(pool.tensor_scalar(x, x, am[:, 28 + b:29 + b], 1.0, ALU.mult, ALU.mult))
                W.rest(pool, f"gla{2 * h + 1}")
                if h + 1 < SLOTS_H:
                    for g in range(PATTERNS):
                        load_bias((h + 1) * PATTERNS + g)
            for h in range(XH):
                pool.wait_ge(s_xrinv.sem, h + 1)
                for b in range(TB):
                    x = logits[:, (h % 2) * TB * MEM + b * MEM:(h % 2) * TB * MEM + (b + 1) * MEM]
                    s_xscaled.on(pool.tensor_scalar(x, x, am[:, 60 - 4 * (h % 2) + b:61 - 4 * (h % 2) + b], 1.0, ALU.mult, ALU.mult))
            W.rest(pool, "ms_fin2")

        @block.tensor
        def _(pe):
            def product(name, xs, ready=None):
                out = G.open(pe, name)
                W.product(pe, name, out[:, 0:xs[0][0].shape[-1]], xs, ready=ready)

            def product_tokens(name, xs, b):
                out = G.open(pe, name)
                cols = slice(b * P, (b + 1) * P)
                W.product(pe, name, out[:, 0:HALF], [(xh[:, cols], xl[:, cols]) for xh, xl in xs], tokens=True)

            def dense(name, first=None):
                ready = None
                if first is not None:
                    ready = lambda k: pe.wait_ge(s_hl.sem, KD * SPLIT_NORMS.index(first) + k + 1)
                product(name, h_parts, ready)

            def norm(n):
                out = G.open(pe, f"ms_{n}")
                pe.wait_ge(s_sum.sem, NORMS.index(n) + 1)
                G.close(pe.matmul(out[:, :], ones, rstd[:], start=True, stop=True))

            def ffn(n, norm_name):
                for i in range(KF):
                    dense(f"{n}a{i}", norm_name if i == 0 else None)
                    dense(f"{n}b{i}")
                if n == "f1":
                    memory_sum()
                xs = [(act_high[:, i, :], act_low[:, i, :]) for i in range(KF)]
                base = 0 if n == "f1" else KF
                for d in range(KD):
                    ready = (lambda i: pe.wait_ge(s_gl.sem, base + i + 1)) if d == 0 else None
                    product(f"{n}d{d}", xs, ready)

            def memory_sum():
                out = G.open(pe, "ms_mem")
                pe.wait_ge(s_msq.sem, KD)
                for i in range(KD):
                    mm = pe.matmul(out[:, 0:MEM], ones, memsq[:, i, :], start=(i == 0), stop=(i == KD - 1))
                G.close(mm)

            pe.wait_ge(s_const.sem, 32)
            pe.wait_ge(s_onehot.sem, 32)
            for i in range(4):
                out = G.open(pe, f"toep{i}")
                G.close(pe.matmul(out[0:12, 0:480], table, onehot[0:33, i * 480:(i + 1) * 480], start=True, stop=True))
            norm("fin1")
            norm("ffn1")
            ffn("f1", "ffn1")
            pe.wait_ge(s_meml.sem, KD)
            mem_parts = [(mem_high[:, j, :], mem_low[:, j, :]) for j in range(KD)]
            for i in range(XH):
                product(f"mk{i}", mem_parts)
            for i in range(2 * (MEM // P)):
                product_tokens(f"mv{i}", mem_parts, i % (MEM // P))
            norm("mix")
            for i in range(4):
                dense(f"u{i}", "mix" if i == 0 else None)

            def ssm_in(j):
                r = slice(32 * (j % 4), 32 * (j % 4) + 32)
                if j >= 2:
                    pe.wait_ge(s_rot.sem, 4 * (j - 1))
                for i in range(2):
                    mm = pe.matmul(att[2 * (j % 2) + i][:, :], b_in[i][r, (j // 4) * P:(j // 4 + 1) * P], uT[r, j // 4, :],
                                   start=True, stop=True)
                s_bu.on(mm)

            def ssm_out(j):
                c, s, t1, t2, t3, t4 = work[j % 2]
                r = slice(32 * (j % 4), 32 * (j % 4) + 32)
                pe.wait_ge(s_x.sem, j + 1)
                if j >= 8:
                    pe.wait_ge(s_yv.sem, j // 4 - 1)
                bank = att[4 + (j // 4) % 2]
                pe.matmul(bank[r, :], c_out[0][:, j, :], t2, start=True, stop=False)
                s_y.on(pe.matmul(bank[r, :], c_out[1][:, j, :], t1, start=False, stop=True))

            pe.wait_ge(s_ssm.sem, 64)
            G.moved(pe, "u3")
            ssm_in(0)
            ssm_in(1)
            pe.wait_ge(s_cw.sem, 1)
            for j in range(NT):
                for n, i in fillers_of(j):
                    if n == "v":
                        product_tokens(f"v{i}", h_parts, i % TB)
                    else:
                        dense(f"{n}{i}")
                ssm_out(j)
                if j + 2 < NT:
                    ssm_in(j + 2)

            G.moved(pe, "xq3")
            pe.wait_ge(s_yv.sem, 4)
            u_parts = [(u_high[:, i, :], u_low[:, i, :]) for i in range(4)]
            glu = [f"{n}{d}" for d in range(KD) for n in ("g0", "glb", "gla")]

            def glu_products(n):
                for _ in range(n):
                    name = glu.pop(0)
                    if name == "glb0":
                        pe.wait_ge(s_bl.sem, 4)
                    product(name, h_parts if name.startswith("g0") else u_parts)

            for h in range(SLOTS_H):
                r = slice(64 * (h % 2), 64 * (h % 2) + 64)
                if h >= 1:
                    pe.wait_ge(s_att_moved.sem, h)
                for g in range(PATTERNS):
                    tile = (g * SLOTS_H + h) // 2
                    if PATTERNS * h + g >= 1:
                        pe.wait_ge(s_lg.sem, TB * (PATTERNS * h + g))
                    for b in range(TB):
                        bank, col = KPLACE[TB - 1 - b]
                        k0, w = DIL[g][b]
                        mm = pe.matmul(att[bank][:, col:col + w], q[r, tile, b * P:(b + 1) * P], k[r, tile, k0:k0 + w],
                                       start=True, stop=True)
                    s_S.on(mm)
                glu_products(5)
                for g in range(PATTERNS):
                    n = PATTERNS * h + g
                    pe.wait_ge(s_scaled.sem, TB * PATTERNS * h + TB * (g + 1))
                    if n >= 1:
                        pe.wait_ge(s_TA.sem, n)
                        pe.wait_ge(s_TV.sem, 2 * n)
                    for s in range(TB):
                        bank, col = KPLACE[s]
                        for b in range(s, TB):
                            k0, w = DIL[g][b]
                            if s * P < k0:
                                continue
                            o = DOFF[g][b] + s * P - k0
                            tr = pe.transpose(att[3 + bank][:, col + (b - s) * P:col + (b - s + 1) * P],
                                              logits[:, o:o + P], ident)
                    s_T.on(tr)
                    if g == 0:
                        glu_products(1)
                    pe.wait_ge(s_TA.sem, n + 1)
                    pe.wait_ge(s_TV.sem, 2 * n + 2)
                    c0 = (g * SLOTS_H + h) * HD
                    for s in range(TB):
                        w = WK[s] if g else min(WK[s], 2 * P)
                        mm = pe.matmul(att_out[r, s * P:s * P + w], v[:, s, c0:c0 + HD],
                                       turned[:, n % 2, KOFF[s]:KOFF[s] + w],
                                       start=(g == 0 and s == 0), stop=(g == PATTERNS - 1 and s == TB - 1),
                                       skip_group_check=True)
                s_att.on(mm)

            def cross_scores(h):
                if h == 0:
                    pe.wait_ge(s_att_moved.sem, SLOTS_H)
                else:
                    pe.wait_ge(s_xexp.sem, TB * h)
                for b in range(TB):
                    mm = pe.matmul(att[b // 2][:, (b % 2) * MEM:(b % 2 + 1) * MEM], xq[:, h, b * P:(b + 1) * P], mk[:, h, :],
                                   start=True, stop=True)
                s_xS.on(mm)

            cross_scores(0)
            for h in range(XH):
                if h + 1 < XH:
                    cross_scores(h + 1)
                pe.wait_ge(s_xscaled.sem, TB * (h + 1))
                if h == 0:
                    pe.wait_ge(s_TA.sem, PATTERNS * SLOTS_H)
                    pe.wait_ge(s_TV.sem, 2 * PATTERNS * SLOTS_H)
                else:
                    pe.wait_ge(s_xTA.sem, h)
                    pe.wait_ge(s_xTV.sem, h)
                for m in range(MEM // P):
                    for b in range(TB):
                        o = (h % 2) * TB * MEM + b * MEM + m * P
                        tr = pe.transpose(att[3 + m][:, b * P:(b + 1) * P], logits[:, o:o + P], ident)
                s_xT.on(tr)
                out = G.open(pe, f"xo{h}")
                pe.wait_ge(s_xTA.sem, h + 1)
                pe.wait_ge(s_xTV.sem, h + 1)
                for m in range(MEM // P):
                    mm = pe.matmul(out[:, :], mv[:, m, h * XD:(h + 1) * XD], turned[:, h % 2, m * T:(m + 1) * T],
                                   start=(m == 0), stop=(m == MEM // P - 1))
                G.close(mm)

            y_parts = [(yatt_high[:, i, :], yatt_low[:, i, :]) for i in range(2)]
            x_parts = [(x_high[:, i, :], x_low[:, i, :]) for i in range(XH)]
            for d in range(KD):
                dense(f"g1{d}")
                if d == 0:
                    pe.wait_ge(s_bl.sem, 6)
                product(f"up{d}", y_parts)
                dense(f"g2{d}")
                if d == 0:
                    pe.wait_ge(s_bl.sem, 10)
                product(f"xup{d}", x_parts)
            for d in range(KD):
                ready = (lambda i: pe.wait_ge(s_mgl.sem, i + 1)) if d == 0 else None
                product(f"o{d}", [(merged_high[:, i, :], merged_low[:, i, :]) for i in range(KD)], ready)
            norm("ffn2")
            ffn("f2", "ffn2")
            norm("fin2")

        @block.scalar
        def _(act):
            def move(name, out, func=ACT.Copy, src=None, **kw):
                W.round(act, name)
                bank = G.whole(act, name)
                G.empty(act.activation(out, bank[:, :] if src is None else src(bank), func, **kw), name)

            def squares(n, ready):
                act.preload_act_table_set("sqrt_and_others")
                for i in range(KD):
                    ready(i)
                    s_sq.on(act.activation(hT[:, i, :], xT[:, i, :], ACT.Square))

            def root(n):
                if n != "fin1":
                    act.wait_ge(s_h.sem, KD * NORMS.index(n))
                move(f"ms_{n}", rstd[:], ACT.Sqrt, scale=1.0 / D, bias=epsc)
                if n in SPLIT_NORMS:
                    if n != "mix":
                        act.preload_act_table_set("silu_and_others")
                    for i in range(KD):
                        act.wait_ge(s_h.sem, KD * NORMS.index(n) + i + 1)
                        s_hh.on(act.activation(h_high[:, i, :], hT[:, i, :], ACT.Copy))

            def state_scalars():
                s_dt.on(act.activation(st[:, 0, :], vec("ldt", 0, NT), ACT.Exp))
                act.wait_ge(s_r.sem, 1)
                s_trig.on(act.activation(st[:, 3, :], st[:, 1, :], ACT.Exp))
                s_trig.on(act.activation(st[:, 4, :], st[:, 1, :], ACT.Tanh, scale=0.5))
                act.wait_ge(s_r.sem, 2)
                s_ac.on(act.activation(st[:, 5, :], st[:, 8, :], ACT.Abs))
                settle(act, s_ac)
                s_trig.on(act.activation(st[:, 6, :], st[:, 8, :], ACT.Sin))
                s_trig.on(act.activation(st[:, 7, :], st[:, 8, :], ACT.Sin, scale=0.5))
                s_trig.on(act.activation(st[:, 5, :], st[:, 5, :], ACT.Sin, scale=-1.0, bias=halfpi))

            def ffn(n):
                def high_part(i):
                    G.moved(act, f"{n}b{i}")
                    if n == "f1" and i == 18:
                        act.wait_ge(s_toep.sem, 16 * PATTERNS * SLOTS_H)
                    s_gh.on(act.activation(act_high[:, i, :], big[:, i, :], ACT.Copy))
                for i in range(KF):
                    if i >= 2:
                        high_part(i - 2)
                    move(f"{n}a{i}", big[:, i, :], ACT.Silu)
                    W.round(act, f"{n}b{i}")
                high_part(KF - 2)
                if n == "f1":
                    move("ms_mem", rstd[:, 0:MEM], ACT.Sqrt, src=lambda b: b[:, 0:MEM], scale=1.0 / D, bias=epsc)
                high_part(KF - 1)
                if n == "f1":
                    for i in range(KD):
                        act.wait_ge(s_mh.sem, i + 1)
                        s_memh.on(act.activation(mem_high[:, i, :], memT[:, i, :], ACT.Copy))
                    state_scalars()

            for i in range(4):
                move(f"toep{i}", toep[:, i * 480:(i + 1) * 480], src=lambda b: b[0:12, 0:480])
            act.wait_ge(s_set.sem, 2)
            squares("fin1", lambda i: None)
            root("fin1")
            squares("ffn1", lambda i: act.wait_ge(s_h.sem, i + 1))
            root("ffn1")
            W.round(act, "f1a0")
            act.wait_ge(s_mem.sem, 16)
            for i in range(KD):
                s_msq.on(act.activation(memsq[:, i, :], memT[:, i, :], ACT.Square))
            ffn("f1")
            def ready(i):
                W.round(act, f"f1d{i}")
                G.moved(act, f"f1d{i}")
            squares("mix", ready)
            for i in range(XH):
                move(f"mk{i}", mk[:, i, :], src=lambda b: b[:, 0:MEM])
            half = lambda b: b[:, 0:HALF]
            for i in range(2 * (MEM // P)):
                c, b = divmod(i, MEM // P)
                move(f"mv{i}", mv[:, b, c * HALF:(c + 1) * HALF], src=half)
            root("mix")
            for i in range(4):
                move(f"u{i}", uT[:, i, :])

            def table(j):
                c, s, t1, t2, t3, t4 = work[j % 2]
                act.wait_ge(s_ph.sem, j + 1)
                if j >= 2:
                    act.wait_ge(s_x.sem, j - 1)
                s_ac.on(act.activation(c, t2, ACT.Abs))
                settle(act, s_ac)
                s_tab.on(act.activation(s, t2, ACT.Sin, scale=TWO_PI))
                s_tab.on(act.activation(c, c, ACT.Sin, scale=-TWO_PI, bias=halfpi))

            table(0)
            table(1)
            for j in range(NT):
                for n, i in fillers_of(j):
                    if n == "v":
                        c, b = divmod(i, TB)
                        move(f"v{i}", v[:, b, c * HALF:(c + 1) * HALF], src=half)
                    else:
                        dst = {"q": q, "k": k, "xq": xq}[n][:, i, :]
                        move(f"{n}{i}", dst, scale={"q": HD ** -0.5, "k": 1.0, "xq": 1.0}[n])
                if j + 2 < NT:
                    table(j + 2)
            for i in range(4):
                act.wait_ge(s_yv.sem, i + 1)
                s_yg.on(act.activation(uT[:, i, :], uT[:, i, :], ACT.Gelu_apprx_tanh))
                settle(act, s_yg)
                s_bh.on(act.activation(u_high[:, i, :], uT[:, i, :], ACT.Copy))

            def glu_gate(i, d):
                if i == 0 and d >= 1:
                    act.wait_ge(s_glu.sem, d)
                name = f"{('g0', 'glb')[i]}{d}"
                move(name, ssm_gates[:, i, :], ACT.Sigmoid)
                if i:
                    W.round(act, f"gla{d}")

            for h in range(SLOTS_H):
                glu_gate(0, 2 * h)
                glu_gate(1, 2 * h)
                act.wait_ge(s_neg.sem, h + 1)
                for g in range(PATTERNS):
                    for b in range(TB):
                        x = logits[:, DOFF[g][b]:DOFF[g][b] + DIL[g][b][1]]
                        s_exp.on(act.activation(x, x, ACT.Exp, bias=am[:, 12 + b:13 + b],
                                                accum_out=am[:, 16 + 4 * g + b:17 + 4 * g + b]))
                glu_gate(0, 2 * h + 1)
                glu_gate(1, 2 * h + 1)
                for g in range(PATTERNS):
                    n = PATTERNS * h + g
                    act.wait_ge(s_T.sem, n + 1)
                    w = T if g else 2 * P
                    s_TA.on(act.activation(turned[:, n % 2, 0:w], att[3][:, 0:w], ACT.Copy))
            for h in range(XH):
                act.wait_ge(s_xneg.sem, h + 1)
                if h >= 2:
                    act.wait_ge(s_xT.sem, h - 1)
                for b in range(TB):
                    o = (h % 2) * TB * MEM + b * MEM
                    s_xexp.on(act.activation(logits[:, o:o + MEM], att[b // 2][:, (b % 2) * MEM:(b % 2 + 1) * MEM], ACT.Exp,
                                             scale=XD ** -0.5, bias=am[:, 36 + 4 * (h % 2) + b:37 + 4 * (h % 2) + b],
                                             accum_out=am[:, 44 + 4 * (h % 2) + b:45 + 4 * (h % 2) + b]))
                act.wait_ge(s_xT.sem, h + 1)
                if h >= 2:
                    G.whole(act, f"xo{h - 2}")
                s_xTA.on(act.activation(turned[:, h % 2, 0:T], att[3][:, :], ACT.Copy))
            act.wait_ge(s_att_moved.sem, SLOTS_H)
            for i in range(2):
                s_bh.on(act.activation(yatt_high[:, i, :], yatt[:, i, :], ACT.Copy))
            for i in range(XH):
                G.moved(act, f"xo{i}")
                s_bh.on(act.activation(x_high[:, i, :], xq[:, i, :], ACT.Copy))
            for d in range(KD):
                for i, n in enumerate(("g1", "g2")):
                    up = ("up", "xup")[i]
                    if d >= 1:
                        G.moved(act, f"{up}{d - 1}")
                    move(f"{n}{d}", gates[:, i, :], ACT.Sigmoid)
                    W.round(act, f"{up}{d}")
                if d >= 1:
                    act.wait_ge(s_merged.sem, d)
                    s_mgh.on(act.activation(merged_high[:, d - 1, :], merged[:, d - 1, :], ACT.Copy))
            act.wait_ge(s_merged.sem, KD)
            s_mgh.on(act.activation(merged_high[:, KD - 1, :], merged[:, KD - 1, :], ACT.Copy))
            def ready(i):
                if i == 0:
                    G.whole(act, "g27")
                W.round(act, f"o{i}")
                G.moved(act, f"o{i}")
            squares("ffn2", ready)
            root("ffn2")
            ffn("f2")
            def ready(i):
                W.round(act, f"f2d{i}")
                G.moved(act, f"f2d{i}")
            squares("fin2", ready)
            root("fin2")

        @block.vector
        def _(dve):
            def link(ins):
                s_vc.on(ins)
                settle(dve, s_vc)

            def sum_square(n, i):
                dve.wait_ge(s_sq.sem, KD * NORMS.index(n) + i + 1)
                if i >= 1:
                    other = hT[:, 0, :] if i == 1 else rstd[:]
                    ins = dve.tensor_tensor(rstd[:], other, hT[:, i, :], ALU.add)
                    if i < KD - 1:
                        link(ins)
                    else:
                        s_sum.on(ins)

            def norm(n, out, summed=False):
                for i in range(KD - 1 if summed else 0, KD):
                    sum_square(n, i)

                def low_part(i):
                    dve.wait_ge(s_hh.sem, KD * SPLIT_NORMS.index(n) + i + 1)
                    s_hl.on(dve.tensor_tensor(h_low[:, i, :], hT[:, i, :], h_high[:, i, :], ALU.subtract))
                G.moved(dve, f"ms_{n}")
                link(dve.reciprocal(rstd[:], rstd[:]))
                for i in range(KD):
                    s_h.on(dve.scalar_tensor_tensor(out[:, i, :], xT[:, i, :], vec(n, i), rstd[:], ALU.mult, ALU.mult))
                    if n in SPLIT_NORMS and i >= 1:
                        low_part(i - 1)
                if n in SPLIT_NORMS:
                    low_part(KD - 1)
                settle(dve, s_h)

            def memory_norm():
                def low_part(i):
                    dve.wait_ge(s_memh.sem, i + 1)
                    s_meml.on(dve.tensor_tensor(mem_low[:, i, :], memT[:, i, :], mem_high[:, i, :], ALU.subtract))
                G.moved(dve, "ms_mem")
                link(dve.reciprocal(rstd[:, 0:MEM], rstd[:, 0:MEM]))
                for i in range(KD):
                    s_mh.on(dve.scalar_tensor_tensor(memT[:, i, :], memT[:, i, :], vec("mem", i), rstd[:, 0:MEM], ALU.mult, ALU.mult))
                    if i >= 1:
                        low_part(i - 1)
                low_part(KD - 1)
                settle(dve, s_mh)

            S = lambda i: st[:, i, :]
            tt = lambda o, a, b, op: link(dve.tensor_tensor(S(o), S(a) if isinstance(a, int) else a, S(b) if isinstance(b, int) else b, op))
            are, aim = vec("are", 0, NT), vec("aim", 0, NT)

            def state_scalars():
                dve.wait_ge(s_dt.sem, 1)
                link(dve.tensor_tensor(S(1), are, S(0), ALU.mult))
                s_r.on(dve.tensor_tensor(S(2), aim, S(0), ALU.mult))
                settle(dve, s_r)
                link(dve.tensor_scalar(S(9), S(2), float(1 / (2 * np.pi)), MAGIC, ALU.mult, ALU.add))
                link(dve.tensor_scalar(S(9), S(9), MAGIC, None, ALU.subtract))
                link(dve.scalar_tensor_tensor(S(8), S(9), -PI_A, S(2), ALU.mult, ALU.add))
                link(dve.scalar_tensor_tensor(S(8), S(9), -PI_B, S(8), ALU.mult, ALU.add))
                link(dve.scalar_tensor_tensor(S(8), S(9), -float(PI_C), S(8), ALU.mult, ALU.add))
                s_r.on(dve.tensor_scalar(S(8), S(8), 3.1415925, -3.1415925, ALU.min, ALU.max))
                settle(dve, s_r)
                link(dve.tensor_scalar(S(10), S(8), float(1 / (2 * np.pi)), None, ALU.mult))
                link(dve.tensor_scalar(S(11), S(10), MAGIC / 16384, None, ALU.add))
                link(dve.tensor_scalar(S(11), S(11), MAGIC / 16384, None, ALU.subtract))
                link(dve.tensor_tensor(S(12), S(10), S(11), ALU.subtract))
                dve.wait_ge(s_trig.sem, 5)
                link(dve.scalar_tensor_tensor(S(13), S(3), 1.0, S(4), ALU.add, ALU.mult))
                tt(13, 13, 5, ALU.mult)
                tt(14, 7, 7, ALU.mult)
                link(dve.scalar_tensor_tensor(S(13), S(14), -2.0, S(13), ALU.mult, ALU.add))
                tt(14, 3, 6, ALU.mult)
                tt(15, are, are, ALU.mult)
                tt(16, aim, aim, ALU.mult)
                tt(15, 15, 16, ALU.add)
                link(dve.reciprocal(S(15), S(15)))
                tt(16, 13, are, ALU.mult)
                tt(17, 14, aim, ALU.mult)
                tt(16, 16, 17, ALU.add)
                tt(16, 16, 15, ALU.mult)
                tt(17, 14, are, ALU.mult)
                tt(18, 13, aim, ALU.mult)
                tt(17, 17, 18, ALU.subtract)
                tt(17, 17, 15, ALU.mult)

            def ffn(n):
                def low_part(i):
                    dve.wait_ge(s_gh.sem, (0 if n == "f1" else KF) + i + 1)
                    s_gl.on(dve.tensor_tensor(act_low[:, i, :], big[:, i, :], act_high[:, i, :], ALU.subtract))
                for i in range(KF):
                    bank = G.whole(dve, f"{n}b{i}")
                    G.moved(dve, f"{n}a{i}")
                    G.empty(dve.tensor_tensor(big[:, i, :], bank[:, :], big[:, i, :], ALU.mult), f"{n}b{i}")
                    if i >= 2:
                        low_part(i - 2)
                low_part(KF - 2)
                low_part(KF - 1)
                if n == "f1":
                    memory_norm()
                    state_scalars()
                for d in range(KD):
                    bank = G.whole(dve, f"{n}d{d}")
                    G.empty(dve.scalar_tensor_tensor(xT[:, d, :], bank[:, :], 0.5, xT[:, d, :], ALU.mult, ALU.add), f"{n}d{d}")
                    if d >= 1:
                        sum_square("mix" if n == "f1" else "fin2", d - 1)

            s_set.on(dve.memset(halfpi, HALF_PI))
            s_set.on(dve.memset(epsc, EPS))
            dve.wait_ge(s_const.sem, 32)
            norm("fin1", xT)
            norm("ffn1", hT)
            ffn("f1")

            norm("mix", hT, True)
            dve.wait_ge(s_ssm.sem, 64)
            wide = lambda i: st[:, i, :].unsqueeze(2).to_broadcast([P, NT, 32])
            t1 = work[0][2].rearrange("p (a b) -> p a b", a=NT)
            link(dve.tensor_tensor(t1, c_raw[1], wide(17), ALU.mult))
            link(dve.tensor_tensor(c_out[0], c_raw[0], wide(16), ALU.mult))
            link(dve.tensor_tensor(c_out[0], c_out[0], t1, ALU.subtract))
            link(dve.tensor_tensor(t1, c_raw[1], wide(16), ALU.mult))
            link(dve.tensor_tensor(c_out[1], c_raw[0], wide(17), ALU.mult))
            s_cw.on(dve.scalar_tensor_tensor(c_out[1], c_out[1], -1.0, t1, ALU.mult, ALU.subtract))
            settle(dve, s_cw)


            def phase(j):
                c, s, t1, t2, t3, t4 = work[j % 2]
                if j >= 2:
                    dve.wait_ge(s_y.sem, j - 1)
                link(dve.tensor_scalar(t1, iota, st[:, 10, j:j + 1], MAGIC, ALU.mult, ALU.add))
                link(dve.tensor_scalar(t1, t1, MAGIC, None, ALU.subtract))
                link(dve.scalar_tensor_tensor(t2, iota, st[:, 11, j:j + 1], t1, ALU.mult, ALU.subtract))
                link(dve.scalar_tensor_tensor(t2, iota, st[:, 12, j:j + 1], t2, ALU.mult, ALU.add))
                s_ph.on(dve.tensor_scalar(t2, t2, 0.5, -0.5, ALU.min, ALU.max))

            phase(0)
            phase(1)
            for j in range(NT):
                c, s, t1, t2, t3, t4 = work[j % 2]
                re, im = att[2 * (j % 2)], att[2 * (j % 2) + 1]
                dve.wait_ge(s_tab.sem, 2 * (j + 1))
                dve.wait_ge(s_bu.sem, j + 1)
                s_rot.on(dve.tensor_tensor(t1, re[:, :], c, ALU.mult))
                s_rot.on(dve.tensor_tensor(t2, im[:, :], s, ALU.mult))
                s_rot.on(dve.tensor_tensor(t3, im[:, :], c, ALU.mult))
                s_rot.on(dve.tensor_tensor(t4, re[:, :], s, ALU.mult))
                mag = st[:, 3, j:j + 1].to_broadcast([P, T])
                settle(dve, s_rot)
                s_w.on(dve.tensor_tensor(t1, t1, t2, ALU.add))
                s_w.on(dve.tensor_tensor(t3, t3, t4, ALU.subtract))
                dve.wait_ge(s_w.sem, 2 * j + 1)
                s_z.on(dve.tensor_tensor_scan(t1, mag, t1, 0.0, ALU.mult, ALU.add))
                dve.wait_ge(s_w.sem, 2 * j + 2)
                s_z.on(dve.tensor_tensor_scan(t3, mag, t3, 0.0, ALU.mult, ALU.add))
                if j >= 4 and j % 4 == 0:
                    i = j // 4 - 1
                    dve.wait_ge(s_y.sem, j)
                    s_yv.on(dve.scalar_tensor_tensor(uT[:, i, :], uT[:, i, :], vec("skip", i), att[4 + i % 2][:, :], ALU.mult, ALU.add))
                if j >= 1 and j + 1 < NT:
                    phase(j + 1)
            dve.wait_ge(s_y.sem, NT)
            s_yv.on(dve.scalar_tensor_tensor(uT[:, 3, :], uT[:, 3, :], vec("skip", 3), att[5][:, :], ALU.mult, ALU.add))

            def glu_gated(d):
                bank = G.whole(dve, f"gla{d}")
                G.moved(dve, f"glb{d}")
                G.empty(dve.tensor_tensor(merged[:, d, :], bank[:, :], ssm_gates[:, 1, :], ALU.mult), f"gla{d}")
                settle(dve, s_v)
                s_glu.on(dve.tensor_tensor(merged[:, d, :], merged[:, d, :], ssm_gates[:, 0, :], ALU.mult))

            def branch_low(a, b):
                outputs = [(u_low, uT, u_high, i) for i in range(4)] + [(yatt_low, yatt, yatt_high, i) for i in range(2)]
                outputs += [(x_low, xq, x_high, i) for i in range(XH)]
                for n in range(a, b):
                    lo, x, hi, i = outputs[n]
                    dve.wait_ge(s_bh.sem, n + 1)
                    s_bl.on(dve.tensor_tensor(lo[:, i, :], x[:, i, :], hi[:, i, :], ALU.subtract))

            branch_low(0, 4)

            def dil_logits(h):
                for g in range(PATTERNS):
                    n = PATTERNS * h + g
                    dve.wait_ge(s_S.sem, n + 1)
                    dve.wait_ge(s_bias[g].sem, 16 * (h + 1))
                    if h >= 1:
                        dve.wait_ge(s_T.sem, PATTERNS * (h - 1) + g + 1)
                    for b in range(TB):
                        bank, col = KPLACE[TB - 1 - b]
                        w = DIL[g][b][1]
                        end = 2 * P if g == 0 else T
                        s_lg.on(dve.tensor_tensor_reduce(
                            out=logits[:, DOFF[g][b]:DOFF[g][b] + w], in0=att[bank][:, col:col + w],
                            in1=biases[g][:, end - w:end], scale=1.0, scalar=TAKEN, op0=ALU.add, op1=ALU.max,
                            accum_out=am[:, 4 * g + b:4 * g + b + 1]))
                settle(dve, s_lg)
                link(dve.tensor_tensor(am[:, 0:4], am[:, 0:4], am[:, 4:8], ALU.max))
                link(dve.tensor_tensor(am[:, 0:4], am[:, 0:4], am[:, 8:12], ALU.max))
                s_neg.on(dve.tensor_scalar(am[:, 12:16], am[:, 0:4], -1.0, None, ALU.mult))
                glu_gated(2 * h)
                dve.wait_ge(s_exp.sem, TB * PATTERNS * (h + 1))
                link(dve.tensor_tensor(am[:, 16:20], am[:, 16:20], am[:, 20:24], ALU.add))
                link(dve.tensor_tensor(am[:, 16:20], am[:, 16:20], am[:, 24:28], ALU.add))
                s_rinv.on(dve.reciprocal(am[:, 28:32], am[:, 16:20]))

            for h in range(SLOTS_H):
                dil_logits(h)
                for g in range(PATTERNS):
                    n = PATTERNS * h + g
                    dve.wait_ge(s_T.sem, n + 1)
                    if g:
                        s_TV.on(dve.tensor_copy(turned[:, n % 2, 512:1024], att[4][:, :]))
                        s_TV.on(dve.tensor_copy(turned[:, n % 2, 1024:1280], att[5][:, 0:256]))
                    else:
                        s_TV.on(dve.tensor_copy(turned[:, n % 2, 512:768], att[4][:, 0:256]))
                        s_am2.on(dve.tensor_copy(turned[:, n % 2, 896:1024], att[4][:, 384:512]))
                        settle(dve, s_am2)
                        s_TV.on(dve.tensor_copy(turned[:, n % 2, 1024:1280], att[5][:, 0:256]))
                    if g == 0:
                        glu_gated(2 * h + 1)
                r = slice(64 * (h % 2), 64 * (h % 2) + 64)
                dve.wait_ge(s_att.sem, h + 1)
                s_att_moved.on(dve.tensor_copy(yatt[r, h // 2, :], att_out[r, :]))

            def cross_max(h):
                dve.wait_ge(s_xS.sem, h + 1)
                mx = am[:, 52:56]
                for i in range(2):
                    ins = dve.tensor_reduce(mx[:, 2 * i:2 * i + 2], att[i][:, :].rearrange("p (a b) -> p a b", a=2), AX.X, ALU.max)
                    link(ins)
                s_xneg.on(dve.tensor_scalar(am[:, 36 + 4 * (h % 2):40 + 4 * (h % 2)], mx, -(XD ** -0.5), None, ALU.mult))

            def cross_rinv(h):
                dve.wait_ge(s_xexp.sem, TB * (h + 1))
                o = 60 - 4 * (h % 2)
                s_xrinv.on(dve.reciprocal(am[:, o:o + 4], am[:, 44 + 4 * (h % 2):48 + 4 * (h % 2)]))

            cross_max(0)
            cross_rinv(0)
            for h in range(XH):
                if h + 1 < XH:
                    cross_max(h + 1)
                dve.wait_ge(s_xT.sem, h + 1)
                if h >= 2:
                    G.whole(dve, f"xo{h - 2}")
                s_xTV.on(dve.tensor_copy(turned[:, h % 2, T:2 * T], att[4][:, :]))
                if h + 1 < XH:
                    cross_rinv(h + 1)
                bank = G.whole(dve, f"xo{h}")
                G.empty(dve.tensor_copy(xq[:, h, :], bank[:, :]), f"xo{h}")
            def merged_low_part(d):
                dve.wait_ge(s_mgh.sem, d + 1)
                s_mgl.on(dve.tensor_tensor(merged_low[:, d, :], merged[:, d, :], merged_high[:, d, :], ALU.subtract))

            branch_low(4, 10)
            for d in range(KD):
                for i, n in enumerate(("up", "xup")):
                    bank = G.whole(dve, f"{n}{d}")
                    G.moved(dve, f"g{i + 1}{d}")
                    G.empty(dve.tensor_tensor(parts[:, i, :], bank[:, :], gates[:, i, :], ALU.mult), f"{n}{d}")
                    settle(dve, s_v)
                    ins = dve.tensor_tensor(merged[:, d, :], merged[:, d, :], parts[:, i, :], ALU.add)
                    if i == 0:
                        link(ins)
                    else:
                        s_merged.on(ins)
                if d >= 1:
                    merged_low_part(d - 1)
            merged_low_part(KD - 1)
            for d in range(KD):
                bank = G.whole(dve, f"o{d}")
                G.empty(dve.tensor_tensor(xT[:, d, :], bank[:, :], xT[:, d, :], ALU.add), f"o{d}")
                if d >= 1:
                    sum_square("ffn2", d - 1)
            settle(dve, s_v)
            norm("ffn2", hT, True)
            ffn("f2")
            settle(dve, s_v)
            norm("fin2", hT, True)


def tile_k(w):
    k, c = w.shape
    return w.reshape(k // P, P, c).transpose(1, 0, 2).reshape(P, -1)


def pack(order, tiles):
    place, n = place_tiles(order)
    flat = np.zeros((P, n * UNIT), np.float32)
    for name, k, width in order:
        pos = place[name][0]
        flat[:, pos:pos + k * width] = tile_k(tiles[name])
    return np.ascontiguousarray(flat.reshape(P, n, UNIT).transpose(1, 0, 2))


def columns():
    widths = [("q", 512), ("ckv", 128), ("kr", 16), ("iq", 256), ("ik", 64), ("iw", 4), ("za", 512), ("sbq", 512),
              ("sbk", 512), ("sbv", 512), ("zb", 512), ("mlq", 512), ("mlk", 512), ("mlv", 512), ("mi", 4), ("mf", 4),
              ("mlo", 512), ("zc", 512), ("merge", 3072)]
    out, at = {}, 0
    for n, w in widths:
        out[n] = (at, at + w)
        at += w
    return out


def lay_out_first(I):
    C = columns()
    A = {k: [] for k in ("weights", "vec", "wuk", "wuv")}
    for l in range(DEPTH):
        def c(n):
            return I["w_in"][l][:, C[n][0]:C[n][1]]
        index = np.concatenate([c("iq"), c("ik"), c("ik"), c("ckv")], 1)
        m = np.zeros((D, P), np.float32)
        m[:, 0:16], m[:, 32:36], m[:, 64:68], m[:, 96:100] = c("kr"), c("mi"), c("mf"), c("iw")
        tiles = {f"idx{i}": index[:, i * P:(i + 1) * P] for i in range(4)}
        tiles["misc"] = m
        for n in ("q", "za", "zb", "sbq", "sbk", "mlq", "mlk", "mlo", "zc"):
            for i in range(4):
                tiles[f"{n}{i}"] = c(n)[:, i * P:(i + 1) * P]
        for n in ("sbv", "mlv"):
            for i in range(2):
                tiles[f"{n}_half{i}"] = c(n)[:, i * HALF:(i + 1) * HALF]
        for d in range(KD):
            for k in range(3):
                tiles[f"gate{d}{k}"] = c("merge")[:, k * D + d * P:k * D + (d + 1) * P]
                tiles[f"proj{d}{k}"] = I["w_branch"][l][k][:, d * P:(d + 1) * P]
            tiles[f"out{d}"] = I["w_out"][l][:, d * P:(d + 1) * P]
        A["weights"].append(pack(layer_tiles(), tiles))
        v = np.zeros((P, N_VEC), np.float32)
        v[:, 0:8] = I["norm_w"][l].reshape(KD, P).T
        v[:, 8] = I["dsa_kv_norm_w"][l]
        v[:, 9:41] = I["ml_conv_w"][l].reshape(4, 8, P).transpose(2, 0, 1).reshape(P, 32)
        v[:, 41:45] = I["ml_norm_w"][l].reshape(4, P).T
        v[32:36, 45] = I["ml_i_bias"][l]
        v[64:68, 46] = I["ml_f_bias"][l]
        A["vec"].append(v)
        uk = np.zeros((P, HEADS, HD), np.float32)
        uk[:, :, ROPE:] = I["w_dsa_uk"][l]
        A["wuk"].append(uk.reshape(P, -1))
        A["wuv"].append(I["w_dsa_uv"][l].reshape(P, -1))
    return {k: np.ascontiguousarray(np.stack(v)) for k, v in A.items()}


def constants():
    out = np.zeros((P, N_CONST), np.float32)

    def put(n, v):
        a, b = CONST[n]
        out[:v.shape[0], a:b] = v
    put("ident", np.eye(P))
    R = np.zeros((P, P))
    for h in (0, 64):
        for i in range(8):
            R[h + i, h + i + 8] = -1
            R[h + i + 8, h + i] = 1
    put("rot", R.T)
    E = np.zeros((ROPE, P))
    for h in (0, 64):
        E[np.arange(16), h + np.arange(16)] = 1
    put("dup", E)
    i = np.arange(P)
    put("tri", -(i[:, None] >= i[None, :]).astype(float))
    put("negones", -np.ones((P, P)))
    put("ones", np.ones((P, P)))
    put("cmask", np.where(i[None, :] <= i[:, None], 0, NEG))
    f = np.float32
    inv = f(500000.0) ** (-np.arange(0, ROPE, 2, dtype=f) / f(ROPE))
    ang = np.arange(T, dtype=f)[:, None] * inv[None]
    cos, sin = np.ones((P, T), f), np.zeros((P, T), f)
    for h in (0, 8, 64, 72):
        cos[h:h + 8] = np.cos(ang).T
        sin[h:h + 8] = np.sin(ang).T
    put("cos", cos)
    put("sin", sin)
    s = np.zeros((ML_H, ML_H, P))
    s[np.arange(ML_H), np.arange(ML_H)] = 1
    put("sel", s.reshape(ML_H, -1))
    return out


def t5_buckets(dist):
    dist = np.asarray(dist, np.int32)
    exact = 16
    safe = np.maximum(dist, 1).astype(np.float32)
    large = exact + (np.log(safe / exact) / np.log(2048 / exact) * (32 - exact)).astype(np.int32)
    return np.where(dist < exact, dist, np.minimum(large, 31)).astype(np.int32)


def onehot_rows():
    out = np.zeros((33, PATTERNS, TOEP), np.float32)
    i = np.arange(TOEP)
    for g, (top, step, win) in enumerate([(255, 1, 128), (511, 4, 512), (511, 16, 2048)]):
        d = top - i
        ok = (d >= 0) & (d % step == 0) & (d <= win)
        out[t5_buckets(np.where(ok, d, 0))[ok], g, i[ok]] = 1
        out[32, g, ~ok] = NEG
    return out.reshape(33, -1)


def lay_out_second(I):
    A = {}
    c = np.zeros((P, N_CONST2), np.float32)
    c[:, 0:P], c[:, P:2 * P], c[:, 2 * P:] = np.eye(P), 1, np.arange(T)
    A["const2"] = c
    A["onehot"] = onehot_rows()
    A["table"] = np.concatenate([I["rel_table_2"], np.ones((1, PATTERNS * SLOTS_H), np.float32)])
    v = np.zeros((P, N_VEC2), np.float32)

    def put(n, x):
        a, b = VEC2[n]
        v[:, a:b] = x
    for n, k in (("fin1", "final_norm_w"), ("ffn1", "ffn1_norm_2"), ("mix", "mix_norm_2"), ("ffn2", "ffn2_norm_2"),
                 ("fin2", "final_norm_2"), ("mem", "mem_norm_2")):
        put(n, I[k].reshape(KD, P).T)
    put("skip", I["ssm_d_2"].reshape(4, P).T)
    put("are", I["ssm_a_re_2"].reshape(NT, P).T)
    put("aim", I["ssm_a_im_2"].reshape(NT, P).T)
    put("ldt", np.repeat(I["ssm_log_dt_2"].reshape(SG), SS).reshape(NT, P).T)
    A["vec2"] = v
    A["mem"] = np.ascontiguousarray(I["mem_2"][0].T.reshape(KD, P, MEM).transpose(1, 0, 2))
    for n in ("re", "im"):
        b, cc = I[f"ssm_b_{n}_2"][0], I[f"ssm_c_{n}_2"][0]
        B, C = np.zeros((P, 4, P), np.float32), np.zeros((P, NT, 32), np.float32)
        for j in range(NT):
            for g in range(2):
                r = 32 * (j % 4) + 16 * g
                B[r:r + 16, j // 4, 64 * g:64 * g + 64] = b[2 * j + g].T
                C[64 * g:64 * g + 64, j, 16 * g:16 * g + 16] = cc[2 * j + g].T
        A["b" + n], A["c" + n] = B.reshape(P, -1), C
    tiles = {}

    def w(n, x):
        tiles[n] = x
    for n, a, b in (("f1", "ffn1_w_in_2", "ffn1_w_down_2"), ("f2", "ffn2_w_in_2", "ffn2_w_down_2")):
        for i in range(KF):
            w(f"{n}a{i}", I[a][0][:, i * P:(i + 1) * P])
            w(f"{n}b{i}", I[a][0][:, FF + i * P:FF + (i + 1) * P])
        for d in range(KD):
            w(f"{n}d{d}", I[b][0][:, d * P:(d + 1) * P])
    kv, win = I["xattn_w_kv_2"][0], I["w_in_2"][0]
    kv_w = XH * XD
    q0, xq0 = T, T + 3 * AW
    for i in range(4):
        w(f"mk{i}", kv[:, i * P:(i + 1) * P])
        w(f"u{i}", win[:, i * P:(i + 1) * P])
        w(f"xq{i}", win[:, xq0 + i * P:xq0 + (i + 1) * P])
    for i in range(6):
        w(f"q{i}", win[:, q0 + i * P:q0 + (i + 1) * P])
        w(f"k{i}", win[:, q0 + AW + i * P:q0 + AW + (i + 1) * P])
    for i in range(2):
        w(f"mv_part{i}", kv[:, kv_w + i * HALF:kv_w + (i + 1) * HALF])
    for i in range(3):
        w(f"v_part{i}", win[:, q0 + 2 * AW + i * HALF:q0 + 2 * AW + (i + 1) * HALF])
    g0 = xq0 + kv_w
    glu = I["ssm_w_glu_2"][0]
    for d in range(KD):
        cols = slice(d * P, (d + 1) * P)
        for k in range(3):
            w(f"g{k}{d}", win[:, g0 + k * D + d * P:g0 + k * D + (d + 1) * P])
        w(f"gla{d}", glu[:, cols])
        w(f"glb{d}", glu[:, D + d * P:D + (d + 1) * P])
        w(f"up{d}", I["attn_w_up_2"][0][:, cols])
        w(f"xup{d}", I["xattn_w_up_2"][0][:, cols])
        w(f"o{d}", I["w_out_2"][0][:, cols])
    A["stream"] = pack(block_tiles(), tiles)
    return A


def both_blocks(nc, A, scratch, out_dram):
    with ExitStack() as stack:
        xT = stack.enter_context(nc.sbuf_tensor("xT", [P, KD, T], F32))
        s_load = Signal(stack.enter_context(nc.semaphore("load")))
        s_eps = Signal(stack.enter_context(nc.semaphore("eps_set")))
        with ExitStack() as first:
            consts = first.enter_context(nc.sbuf_tensor("consts", [P, N_CONST], F32))
            eps = first.enter_context(nc.sbuf_tensor("eps", [P, 1], F32))
            with nc.Block() as block:

                @block.sync
                def _(sp):
                    s_load.on(sp.dma_start(xT[:], A["x"]), 16)
                    s_load.on(sp.dma_start(consts[:], A["const"]), 16)
                    sp.wait_ge(s_load.sem, 32)

                @block.vector
                def _(dve):
                    s_eps.on(dve.memset(eps[:], EPS))
                    settle(dve, s_eps)

            hybrid_layers(nc, first, xT, A, consts, {"eps": eps[:, 0:1]})
        second_block(nc, stack, xT, A, scratch, out_dram)


def kernel(**inputs):
    from concourse import bacc
    from concourse.bass_utils import run_bass_kernel_spmd

    I = {n: np.asarray(a) for n, a in inputs.items()}
    A = lay_out_first(I)
    A.update(lay_out_second(I))
    A["const"] = constants()
    A["x"] = np.ascontiguousarray(I["x"][0].T.reshape(KD, P, T).transpose(1, 0, 2))

    nc = bacc.Bacc("TRN2", target_bir_lowering=False, num_devices=1)
    aps = {n: nc.dram_tensor("in_" + n, a.shape, F32, kind="ExternalInput").ap() for n, a in A.items()}
    out = nc.dram_tensor("out", (P, KD, T), F32, kind="ExternalOutput").ap()
    scratch = nc.dram_tensor("bias_rows", (PATTERNS * SLOTS_H, P, TOEP), F32, kind="Internal").ap()
    both_blocks(nc, aps, scratch, out)
    r = run_bass_kernel_spmd(nc, [{"in_" + n: a for n, a in A.items()}], core_ids=[0])
    y = r.results[0]["out"]
    return np.ascontiguousarray(y.transpose(1, 0, 2).reshape(D, T).T).reshape(1, T, D)
```
